# Optimizing a Trainium2 kernel written in Bass

```python
import jax, jax.numpy as jnp
from jax import lax
import numpy as np

D_MODEL = 1024
BATCH = 1
SEQ = 512
DEPTH = 1
DEC_BATCH = 8
DEC_SEQ = 4
PAST_LEN = 2048
PAGE_SIZE = 128

HEAD_DIM = 64
ROT_DIM = HEAD_DIM // 4
ROPE_THETA = 500000.0
EPS = 1e-6
QB = 128
NEG = -1e30
A_HEADS = 8
A_PATTERNS = ((128, 1), (512, 4), (2048, 16))
A_BUF = 2048
B_HEADS = 8
B_KV = 2
B_REP = B_HEADS // B_KV
CMP_LEN = 32
CMP_STRIDE = 16
CMP_HIDDEN = 128
SEL_BLOCK = 64
SEL_TOPK = 16
WIN_B = 512
SEL_QB = 32
MEM_TOKENS = 256
MEM_HEADS = 4
MEM_HEAD_DIM = 128
D_FF = 2816
CONV_W = 3

A_WIDTH = A_HEADS * HEAD_DIM
B_WIDTH = B_HEADS * HEAD_DIM
IN_SIZES = (A_WIDTH, A_WIDTH, A_WIDTH, B_WIDTH, 6 * B_KV * HEAD_DIM, 3 * B_HEADS, 2 * D_MODEL)
IN_TOTAL = sum(IN_SIZES)

kernel_name = 'hybrid_dilated_nsa_memxattn_convffn_step'

def rmsnorm(x, g):
    xf = x.astype(jnp.float32)
    y = xf * lax.rsqrt(jnp.mean(xf * xf, -1, keepdims=True) + EPS)
    return (y * g.astype(jnp.float32)).astype(x.dtype)

def rope(x, pos):
    half = ROT_DIM // 2
    inv = ROPE_THETA ** (-jnp.arange(half, dtype=jnp.float32) / half)
    ang = pos.astype(jnp.float32)[:, None] * inv[None, :]
    shape = (pos.shape[0],) + (1,) * (x.ndim - 3) + (half,)
    cos = jnp.cos(ang).reshape(shape)
    sin = jnp.sin(ang).reshape(shape)
    xf = x.astype(jnp.float32)
    x1, x2, rest = xf[..., :half], xf[..., half:ROT_DIM], xf[..., ROT_DIM:]
    return jnp.concatenate([x1 * cos - x2 * sin, x2 * cos + x1 * sin, rest], -1).astype(x.dtype)

def softmax_stats(s, mask):
    s = jnp.where(mask, s, NEG)
    m = jnp.max(s, -1, keepdims=True)
    e = jnp.where(mask, jnp.exp(s - m), 0.0)
    den = jnp.maximum(jnp.sum(e, -1, keepdims=True), 1e-30)
    return e / den, (m + jnp.log(den))[..., 0]

def banded_attention(q, k, v, max_dist):
    n, L, hk, r, hd = q.shape
    qb = min(QB, L)
    nb = -(-L // qb)
    lp = nb * qb
    nprev = -(-max_dist // qb)
    span = (nprev + 1) * qb
    qp = jnp.pad(q, ((0, 0), (0, lp - L), (0, 0), (0, 0), (0, 0)))
    kp = jnp.pad(k, ((0, 0), (nprev * qb, lp - L), (0, 0), (0, 0)))
    vp = jnp.pad(v, ((0, 0), (nprev * qb, lp - L), (0, 0), (0, 0)))
    qblocks = jnp.moveaxis(qp.reshape(n, nb, qb, hk, r, hd), 1, 0)
    scale = hd ** -0.5

    def block(args):
        b, qblk = args
        start = b * qb
        kb = lax.dynamic_slice_in_dim(kp, start, span, axis=1)
        vb = lax.dynamic_slice_in_dim(vp, start, span, axis=1)
        qpos = start + jnp.arange(qb)
        kpos = start - nprev * qb + jnp.arange(span)
        dist = qpos[:, None] - kpos[None, :]
        mask = (dist >= 0) & (dist <= max_dist) & (kpos[None, :] >= 0)
        s = jnp.einsum('nqhrd,nkhd->nhrqk', qblk, kb).astype(jnp.float32) * scale
        p, lse = softmax_stats(s, mask)
        o = jnp.einsum('nhrqk,nkhd->nqhrd', p.astype(vb.dtype), vb)
        return o, jnp.moveaxis(lse, 3, 1)

    o, lse = lax.map(block, (jnp.arange(nb), qblocks))
    o = jnp.moveaxis(o, 0, 1).reshape(n, lp, hk, r, hd)[:, :L]
    lse = jnp.moveaxis(lse, 0, 1).reshape(n, lp, hk, r)[:, :L]
    return o, lse

def combine_by_denominator(outs, lses, dtype):
    wts = jax.nn.softmax(jnp.stack(lses, 0), axis=0)
    o = jnp.einsum('pnth,pnthd->nthd', wts, jnp.stack(outs, 0).astype(jnp.float32))
    return o.astype(dtype)

def dilated_prompt(q, k, v):
    B, T, H, hd = q.shape
    outs, lses = [], []
    for w, d in A_PATTERNS:
        L = T // d
        strided = lambda t: jnp.swapaxes(t.reshape(B, L, d, H, hd), 1, 2).reshape(B * d, L, H, hd)
        o, lse = banded_attention(strided(q)[:, :, :, None], strided(k), strided(v), w // d)
        outs.append(jnp.swapaxes(o[:, :, :, 0].reshape(B, d, L, H, hd), 1, 2).reshape(B, T, H, hd))
        lses.append(jnp.swapaxes(lse[..., 0].reshape(B, d, L, H), 1, 2).reshape(B, T, H))
    return combine_by_denominator(outs, lses, q.dtype)

def dilated_sample(q, k_all, v_all):
    N, S, H, hd = q.shape
    lc = k_all.shape[1]
    qidx = lc - S + jnp.arange(S)
    outs, lses = [], []
    for w, d in A_PATTERNS:
        idx = qidx[:, None] - d * jnp.arange(w // d + 1)[None, :]
        valid = idx >= 0
        idc = jnp.clip(idx, 0)
        kg = k_all[:, idc]
        vg = v_all[:, idc]
        s = jnp.einsum('nshd,nskhd->nhsk', q, kg).astype(jnp.float32) * (hd ** -0.5)
        p, lse = softmax_stats(s, valid[None, None])
        outs.append(jnp.einsum('nhsk,nskhd->nshd', p.astype(vg.dtype), vg))
        lses.append(jnp.swapaxes(lse, 1, 2))
    return combine_by_denominator(outs, lses, q.dtype)

def compress(x, pe, w1, w2):
    N, L, G, hd = x.shape
    m = CMP_LEN // CMP_STRIDE
    nch = L // CMP_STRIDE
    n_cmp = nch - m + 1
    ch = x[:, :nch * CMP_STRIDE].reshape(N, nch, CMP_STRIDE, G, hd)
    pe = pe.reshape(m, CMP_STRIDE, hd)
    w1 = w1.reshape(m, CMP_STRIDE, hd, CMP_HIDDEN)
    hsum = 0
    for r in range(m):
        proj = jnp.einsum('ncsgd,sdh->ncgh', ch + pe[r][:, None, :], w1[r])
        hsum = hsum + proj[:, r:r + n_cmp]
    return jnp.einsum('ncgh,hd->ncgd', jax.nn.gelu(hsum), w2)

def compressed_attention(q, qpos, kc, vc, n_sel):
    C = kc.shape[1]
    start = CMP_STRIDE * jnp.arange(C)
    end = start + CMP_LEN - 1
    mask = end[None, :] <= qpos[:, None]
    s = jnp.einsum('nqgrd,ncgd->ngrqc', q, kc).astype(jnp.float32) * (HEAD_DIM ** -0.5)
    p, _ = softmax_stats(s, mask)
    o = jnp.einsum('ngrqc,ncgd->nqgrd', p.astype(vc.dtype), vc)
    sel_start = SEL_BLOCK * jnp.arange(n_sel)
    overlap = ((start[:, None] <= sel_start[None, :] + SEL_BLOCK - 1) & (end[:, None] >= sel_start[None, :])).astype(jnp.float32)
    imp = jnp.einsum('ngrqc,cj->nqgj', p, overlap)
    return o, imp

def select_blocks(imp, qpos, n_sel):
    cur = qpos // SEL_BLOCK
    j = jnp.arange(n_sel)[None, :]
    valid = (j <= cur[:, None])[None, :, None, :]
    forced = ((j == 0) | (j == cur[:, None]) | (j == cur[:, None] - 1))[None, :, None, :]
    score = jnp.where(forced, jnp.inf, jnp.where(valid, imp, -jnp.inf))
    _, idx = lax.top_k(score, min(SEL_TOPK, n_sel))
    ok = idx <= cur[None, :, None, None]
    return idx, ok

def to_blocks(x, n_sel):
    N, L, G, hd = x.shape
    x = jnp.pad(x, ((0, 0), (0, n_sel * SEL_BLOCK - L), (0, 0), (0, 0)))
    return x.reshape(N, n_sel, SEL_BLOCK, G, hd).transpose(0, 3, 1, 2, 4)

def selected_attention(q, qpos, kblk, vblk, idx, ok):
    N, Q, G, R, hd = q.shape
    kk = idx.shape[-1]
    ni = jnp.arange(N)[:, None, None, None]
    gi = jnp.arange(G)[None, None, :, None]
    kg = kblk[ni, gi, idx].reshape(N, Q, G, kk * SEL_BLOCK, hd)
    vg = vblk[ni, gi, idx].reshape(N, Q, G, kk * SEL_BLOCK, hd)
    kpos = idx[..., None] * SEL_BLOCK + jnp.arange(SEL_BLOCK)
    mask = (ok[..., None] & (kpos <= qpos[None, :, None, None, None])).reshape(N, Q, G, 1, kk * SEL_BLOCK)
    s = jnp.einsum('nqgrd,nqgkd->nqgrk', q, kg).astype(jnp.float32) * (hd ** -0.5)
    p, _ = softmax_stats(s, mask)
    return jnp.einsum('nqgrk,nqgkd->nqgrd', p.astype(vg.dtype), vg)

def window_sample(q, qpos, k, v, kpos):
    s = jnp.einsum('nqgrd,nkgd->ngrqk', q, k).astype(jnp.float32) * (HEAD_DIM ** -0.5)
    dist = qpos[:, None] - kpos[None, :]
    p, _ = softmax_stats(s, (dist >= 0) & (dist < WIN_B))
    return jnp.einsum('ngrqk,nkgd->nqgrd', p.astype(v.dtype), v)

def gate_branches(gb, o_cmp, o_slc, o_win):
    g = jax.nn.sigmoid(gb)[..., None]
    return g[:, :, 0] * o_cmp + g[:, :, 1] * o_slc + g[:, :, 2] * o_win

def nsa_prompt(qb, kvb, gb, W):
    N, T = qb.shape[:2]
    pos = jnp.arange(T)
    kc = compress(kvb[:, :, 0], W['pe_cmp'][0], W['w_cmp1'][0], W['w_cmp2'][0])
    vc = compress(kvb[:, :, 1], W['pe_cmp'][1], W['w_cmp1'][1], W['w_cmp2'][1])
    n_sel = -(-T // SEL_BLOCK)
    o_cmp, imp = compressed_attention(qb, pos, kc, vc, n_sel)
    idx, ok = select_blocks(imp, pos, n_sel)
    kblk = to_blocks(kvb[:, :, 2], n_sel)
    vblk = to_blocks(kvb[:, :, 3], n_sel)
    nc = T // SEL_QB
    chunk = lambda a: jnp.moveaxis(a.reshape((N, nc, SEL_QB) + a.shape[2:]), 1, 0)

    def one(args):
        qc, ic, okc, pc = args
        return selected_attention(qc, pc, kblk, vblk, ic, okc)

    o_slc = lax.map(one, (chunk(qb), chunk(idx), chunk(ok), pos.reshape(nc, SEL_QB)))
    o_slc = jnp.moveaxis(o_slc, 0, 1).reshape(qb.shape)
    o_win, _ = banded_attention(qb, kvb[:, :, 4], kvb[:, :, 5], WIN_B - 1)
    return gate_branches(gb, o_cmp, o_slc, o_win)

def nsa_sample(qb, qpos, kvb, gb, b_pages, page_table, b_win, W):
    N, S = qb.shape[:2]
    past = page_table.shape[1] * PAGE_SIZE
    rows = b_pages[page_table].reshape((N, past) + b_pages.shape[2:])
    full = jnp.concatenate([rows, kvb[:, :, :4]], 1)
    L = past + S
    kc = compress(full[:, :, 0], W['pe_cmp'][0], W['w_cmp1'][0], W['w_cmp2'][0])
    vc = compress(full[:, :, 1], W['pe_cmp'][1], W['w_cmp1'][1], W['w_cmp2'][1])
    n_sel = -(-L // SEL_BLOCK)
    o_cmp, imp = compressed_attention(qb, qpos, kc, vc, n_sel)
    idx, ok = select_blocks(imp, qpos, n_sel)
    o_slc = selected_attention(qb, qpos, to_blocks(full[:, :, 2], n_sel), to_blocks(full[:, :, 3], n_sel), idx, ok)
    lw = b_win.shape[1]
    win = jnp.concatenate([b_win, kvb[:, :, 4:]], 1)
    kpos = past - lw + jnp.arange(lw + S)
    o_win = window_sample(qb, qpos, win[:, :, 0], win[:, :, 1], kpos)
    return gate_branches(gb, o_cmp, o_slc, o_win)

def project(h, pos, W):
    N, L, _ = h.shape
    z = h @ W['w_in']
    offs, acc = [], 0
    for size in IN_SIZES[:-1]:
        acc += size
        offs.append(acc)
    qa, ka, va, qb, kvb, gb, gm = jnp.split(z, offs, axis=-1)
    heads = lambda t, *s: t.reshape((N, L) + s)
    qa = rope(rmsnorm(heads(qa, A_HEADS, HEAD_DIM), W['g_qa']), pos)
    ka = rope(rmsnorm(heads(ka, A_HEADS, HEAD_DIM), W['g_ka']), pos)
    va = heads(va, A_HEADS, HEAD_DIM)
    qb = rope(rmsnorm(heads(qb, B_KV, B_REP, HEAD_DIM), W['g_qb']), pos)
    kvb = heads(kvb, 3, 2, B_KV, HEAD_DIM)
    keys = rope(rmsnorm(kvb[:, :, :, 0], W['g_kb'][:, None, :]), pos)
    kvb = jnp.stack([keys, kvb[:, :, :, 1]], 3).reshape(N, L, 6, B_KV, HEAD_DIM)
    return qa, ka, va, qb, kvb, heads(gb, 3, B_KV, B_REP), heads(gm, 2, D_MODEL)

def merge(oa, ob, gm, W):
    N, L = oa.shape[:2]
    pa = oa.reshape(N, L, A_WIDTH) @ W['w_br_a']
    pb = ob.reshape(N, L, B_WIDTH) @ W['w_br_b']
    g = jax.nn.sigmoid(gm)
    return (g[:, :, 0] * pa + g[:, :, 1] * pb) @ W['w_o']

def mem_kv(mem, W):
    N, M, _ = mem.shape
    kv = (rmsnorm(mem, W['g_mem']) @ W['w_mkv']).reshape(N, M, 2, MEM_HEADS, MEM_HEAD_DIM)
    return jnp.stack([rmsnorm(kv[:, :, 0], W['g_mk']), kv[:, :, 1]], 2)

def mem_attend(x, kv, W):
    N, L, _ = x.shape
    q = rmsnorm((rmsnorm(x, W['g_xattn']) @ W['w_mq']).reshape(N, L, MEM_HEADS, MEM_HEAD_DIM), W['g_mq'])
    s = jnp.einsum('nlhd,nmhd->nhlm', q, kv[:, :, 0]).astype(jnp.float32) * (MEM_HEAD_DIM ** -0.5)
    p = jax.nn.softmax(s, axis=-1)
    o = jnp.einsum('nhlm,nmhd->nlhd', p.astype(kv.dtype), kv[:, :, 1]).reshape(N, L, MEM_HEADS * MEM_HEAD_DIM)
    return o @ W['w_mo']

def conv_ffn(x, buf, W):
    L = x.shape[1]
    u = rmsnorm(x, W['g_ffn']) @ W['w_ffn_up']
    ext = jnp.concatenate([buf, u], 1)
    c = W['b_conv'] + sum(ext[:, j:j + L] * W['w_conv'][j] for j in range(CONV_W))
    a = jax.nn.silu(c[..., :D_FF]) * c[..., D_FF:]
    return a @ W['w_ffn_down'], ext[:, -(CONV_W - 1):]

def layer_prompt(x, mem, W):
    N, T, _ = x.shape
    pos = jnp.arange(T)
    qa, ka, va, qb, kvb, gb, gm = project(rmsnorm(x, W['g_mix']), pos, W)
    oa = dilated_prompt(qa, ka, va)
    ob = nsa_prompt(qb, kvb, gb, W)
    x = x + merge(oa, ob, gm, W)
    mkv = mem_kv(mem, W)
    x = x + mem_attend(x, mkv, W)
    f, conv_state = conv_ffn(x, jnp.zeros((N, CONV_W - 1, 2 * D_FF), x.dtype), W)
    x = x + f
    a_rows = jnp.stack([ka, va], 2)[:, -min(A_BUF, T):]
    w_rows = kvb[:, :, 4:][:, -min(WIN_B, T):]
    return x, a_rows, kvb[:, :, :4], w_rows, mkv, conv_state

def layer_sample(x, a_buf, b_pages, page_table, b_win, mkv, conv_buf, W):
    N, S, _ = x.shape
    pos = page_table.shape[1] * PAGE_SIZE + jnp.arange(S)
    qa, ka, va, qb, kvb, gb, gm = project(rmsnorm(x, W['g_mix']), pos, W)
    oa = dilated_sample(qa, jnp.concatenate([a_buf[:, :, 0], ka], 1), jnp.concatenate([a_buf[:, :, 1], va], 1))
    ob = nsa_sample(qb, pos, kvb, gb, b_pages, page_table, b_win, W)
    x = x + merge(oa, ob, gm, W)
    x = x + mem_attend(x, mkv, W)
    f, conv_state = conv_ffn(x, conv_buf, W)
    x = x + f
    return x, jnp.stack([ka, va], 2), kvb[:, :, :4], kvb[:, :, 4:], conv_state

def setup_inputs(seed: int = 0) -> dict:
    key = jax.random.key(seed)
    ks = iter(jax.random.split(key, 48))
    nrm = lambda shape, scale: scale * jax.random.normal(next(ks), shape, jnp.float32)
    gain = lambda shape: 1.0 + 0.02 * jax.random.normal(next(ks), shape, jnp.float32)
    n_pages = PAST_LEN // PAGE_SIZE
    n_used = DEC_BATCH * n_pages
    n_phys = n_used + n_used // 4
    x_prompt = nrm((BATCH, SEQ, D_MODEL), 1.0)
    x_sample = nrm((DEC_BATCH, DEC_SEQ, D_MODEL), 1.0)
    cache_a_kv = nrm((DEPTH, DEC_BATCH, min(A_BUF, PAST_LEN), 2, A_HEADS, HEAD_DIM), 1.0)
    cache_b_kv = nrm((DEPTH, n_phys, PAGE_SIZE, 4, B_KV, HEAD_DIM), 1.0)
    cache_b_win = nrm((DEPTH, DEC_BATCH, min(WIN_B, PAST_LEN), 2, B_KV, HEAD_DIM), 1.0)
    cache_mem_kv = nrm((DEPTH, DEC_BATCH, MEM_TOKENS, 2, MEM_HEADS, MEM_HEAD_DIM), 1.0)
    cache_ffn_conv = nrm((DEPTH, DEC_BATCH, CONV_W - 1, 2 * D_FF), 1.0)
    page_table = jax.random.permutation(next(ks), n_phys)[:n_used].reshape(DEC_BATCH, n_pages).astype(jnp.int32)
    mem_prompt = nrm((BATCH, MEM_TOKENS, D_MODEL), 1.0)
    mw = MEM_HEADS * MEM_HEAD_DIM
    return {
        'x_prompt': x_prompt, 'x_sample': x_sample,
        'cache_a_kv': cache_a_kv, 'cache_b_kv': cache_b_kv, 'cache_b_win': cache_b_win,
        'cache_mem_kv': cache_mem_kv, 'cache_ffn_conv': cache_ffn_conv,
        'page_table': page_table, 'mem_prompt': mem_prompt,
        'g_mix': gain((DEPTH, D_MODEL)),
        'w_in': nrm((DEPTH, D_MODEL, IN_TOTAL), D_MODEL ** -0.5),
        'g_qa': gain((DEPTH, HEAD_DIM)), 'g_ka': gain((DEPTH, HEAD_DIM)),
        'g_qb': gain((DEPTH, HEAD_DIM)), 'g_kb': gain((DEPTH, 3, HEAD_DIM)),
        'pe_cmp': nrm((DEPTH, 2, CMP_LEN, HEAD_DIM), 0.1),
        'w_cmp1': nrm((DEPTH, 2, CMP_LEN * HEAD_DIM, CMP_HIDDEN), (CMP_LEN * HEAD_DIM) ** -0.5),
        'w_cmp2': nrm((DEPTH, 2, CMP_HIDDEN, HEAD_DIM), CMP_HIDDEN ** -0.5),
        'w_br_a': nrm((DEPTH, A_WIDTH, D_MODEL), A_WIDTH ** -0.5),
        'w_br_b': nrm((DEPTH, B_WIDTH, D_MODEL), B_WIDTH ** -0.5),
        'w_o': nrm((DEPTH, D_MODEL, D_MODEL), D_MODEL ** -0.5),
        'g_xattn': gain((DEPTH, D_MODEL)), 'g_mem': gain((DEPTH, D_MODEL)),
        'w_mq': nrm((DEPTH, D_MODEL, mw), D_MODEL ** -0.5),
        'w_mkv': nrm((DEPTH, D_MODEL, 2 * mw), D_MODEL ** -0.5),
        'g_mq': gain((DEPTH, MEM_HEAD_DIM)), 'g_mk': gain((DEPTH, MEM_HEAD_DIM)),
        'w_mo': nrm((DEPTH, mw, D_MODEL), mw ** -0.5),
        'g_ffn': gain((DEPTH, D_MODEL)),
        'w_ffn_up': nrm((DEPTH, D_MODEL, 2 * D_FF), D_MODEL ** -0.5),
        'w_conv': nrm((DEPTH, CONV_W, 2 * D_FF), CONV_W ** -0.5),
        'b_conv': nrm((DEPTH, 2 * D_FF), 0.01),
        'w_ffn_down': nrm((DEPTH, D_FF, D_MODEL), D_FF ** -0.5),
    }

def reference(x_prompt, x_sample, cache_a_kv, cache_b_kv, cache_b_win, cache_mem_kv, cache_ffn_conv,
              page_table, mem_prompt, g_mix, w_in, g_qa, g_ka, g_qb, g_kb, pe_cmp, w_cmp1, w_cmp2,
              w_br_a, w_br_b, w_o, g_xattn, g_mem, w_mq, w_mkv, g_mq, g_mk, w_mo, g_ffn, w_ffn_up,
              w_conv, b_conv, w_ffn_down):
    yp, ys = x_prompt, x_sample
    pa, pb, pw, pm, pc = [], [], [], [], []
    sa, sb, sw, sc = [], [], [], []
    for l in range(DEPTH):
        W = dict(g_mix=g_mix[l], w_in=w_in[l], g_qa=g_qa[l], g_ka=g_ka[l], g_qb=g_qb[l], g_kb=g_kb[l],
                 pe_cmp=pe_cmp[l], w_cmp1=w_cmp1[l], w_cmp2=w_cmp2[l], w_br_a=w_br_a[l], w_br_b=w_br_b[l],
                 w_o=w_o[l], g_xattn=g_xattn[l], g_mem=g_mem[l], w_mq=w_mq[l], w_mkv=w_mkv[l], g_mq=g_mq[l],
                 g_mk=g_mk[l], w_mo=w_mo[l], g_ffn=g_ffn[l], w_ffn_up=w_ffn_up[l], w_conv=w_conv[l],
                 b_conv=b_conv[l], w_ffn_down=w_ffn_down[l])
        yp, a_r, b_r, w_r, m_r, c_r = layer_prompt(yp, mem_prompt, W)
        pa.append(a_r); pb.append(b_r); pw.append(w_r); pm.append(m_r); pc.append(c_r)
        ys, a_s, b_s, w_s, c_s = layer_sample(ys, cache_a_kv[l], cache_b_kv[l], page_table, cache_b_win[l],
                                              cache_mem_kv[l], cache_ffn_conv[l], W)
        sa.append(a_s); sb.append(b_s); sw.append(w_s); sc.append(c_s)
    return (yp, ys, jnp.stack(pa), jnp.stack(pb), jnp.stack(pw), jnp.stack(pm), jnp.stack(pc),
            jnp.stack(sa), jnp.stack(sb), jnp.stack(sw), jnp.stack(sc))


_drawn_inputs = setup_inputs


def setup_inputs(seed=0):
    import zlib

    import numpy as np

    out = dict(_drawn_inputs(seed))
    spreads = {}
    factors = {'g_mix': 2.837,
     'g_qa': 8.0,
     'g_ka': 4.452,
     'g_qb': 8.0,
     'g_kb': 4.173,
     'pe_cmp': 3.577,
     'g_xattn': 8.0,
     'g_mem': 2.803,
     'g_mq': 8.0,
     'g_mk': 4.336,
     'g_ffn': 2.719,
     'b_conv': 7.923}
    for name, (base, spread) in spreads.items():
        noise = np.random.default_rng([zlib.crc32(name.encode()), seed]).standard_normal(out[name].shape)
        drawn = base * np.exp(spread * noise) if base else spread * noise
        out[name] = __import__('jax').numpy.asarray(drawn.astype(out[name].dtype))
    for name, factor in factors.items():
        out[name] = (out[name] * factor).astype(out[name].dtype)
    return out
```

```python
from contextlib import ExitStack

import numpy as np

import concourse.bass as bass
from concourse import mybir

F32 = mybir.dt.float32
I32 = mybir.dt.int32
ALU = mybir.AluOpType
ACT = mybir.ActivationFunctionType
AX_X = mybir.AxisListType.X
ds = bass.ds

P = 128
D = 1024
KD = D // P
T = 512
QT = T // P
NSEQ, S = 8, 4
SN = NSEQ * S
NT = T + SN
HALF = NT // 2
PAST, PAGE = 2048, 128
NPAGE = PAST // PAGE
HD = 64
EPS = 1e-6
NEG = -1e30
SCALE = HD ** -0.5
MTOK, MH, MHD = 256, 4, 128
MSCALE = MHD ** -0.5
FF = 2816
KF = FF // P
NTILE = 16
QA, KA, QB, KC, KS, KW, VC = 0, 4, 8, 12, 13, 14, 15
VCOL = 512 + 128 + 128 + 24
NKEY_A = 896
NCMP_P, NCMP_S = 31, 127
NBLK, TOPK = 33, 16
RING = 4

KEYS_A = np.array([t for t in range(PAST) if t % 16 < S or t >= PAST - 512])
assert len(KEYS_A) == NKEY_A


def rope_tables():
    pos = np.concatenate([np.arange(T), np.tile(PAST + np.arange(S), NSEQ)]).astype(np.float32)
    inv = (np.float32(500000.0) ** (-np.arange(8, dtype=np.float32) / np.float32(8))).astype(np.float32)
    ang = pos[:, None] * inv[None, :]
    cos, sin = np.ones((P, NT), np.float32), np.zeros((P, NT), np.float32)
    for p in range(P):
        if p % HD < 16:
            cos[p], sin[p] = np.cos(ang[:, p % 8]), np.sin(ang[:, p % 8])
    return cos, sin


def rotation():
    r = np.zeros((P, P), np.float32)
    for m in range(P):
        if m % HD < 8:
            r[m + 8, m] = -1.0
        elif m % HD < 16:
            r[m - 8, m] = 1.0
    return r


def multiplicity(dist):
    n = ((dist >= 0) & (dist <= 128)).astype(int) + ((dist >= 0) & (dist % 4 == 0) & (dist <= 512)) \
        + ((dist >= 0) & (dist % 16 == 0) & (dist <= 2048))
    return np.where(n > 0, np.log(np.maximum(n, 1).astype(np.float64)) / SCALE, NEG).astype(np.float32)


def constants():
    q, k = np.arange(P)[:, None], np.arange(P)[None, :]
    c = {}
    c["ident"] = np.eye(P, dtype=np.float32)
    c["ones"] = np.ones((P, P), np.float32)
    c["head_ones"] = (q // HD == k // HD).astype(np.float32)
    c["rot"] = rotation()
    c["cos"], c["sin"] = rope_tables()
    dist = np.concatenate([P * b + q - k for b in (3, 2, 1, 0)], 1)
    c["mask_dil"] = multiplicity(dist)
    c["mask_causal"] = np.where(dist >= 0, 0.0, NEG).astype(np.float32)
    end = 16 * np.arange(NCMP_P) + 31
    tok = np.arange(T)
    seen = (end[None, :] <= tok[:, None])
    seen[:31, 0] = True
    c["mask_cmp"] = np.where(seen, 0.0, NEG).astype(np.float32).reshape(QT, P, NCMP_P).transpose(1, 0, 2).reshape(P, -1)
    c["cmp_live"] = np.ascontiguousarray((tok >= 31).astype(np.float32).reshape(QT, P).T)
    rows = np.arange(P)
    seq, qs = rows // 32, rows % 4
    new_seq, new_q = np.arange(SN) // S, np.arange(SN) % S
    a, w, b = [], [], []
    for g in range(2):
        own = (new_seq[None, :] == 4 * g + seq[:, None]) & (new_q[None, :] <= qs[:, None])
        dn = np.where(own, qs[:, None] - new_q[None, :], -1)
        a.append(np.concatenate([multiplicity(PAST + qs[:, None] - KEYS_A[None, :]), multiplicity(dn)], 1))
        dw = PAST + qs[:, None] - (PAST - 512 + np.arange(512))[None, :]
        w.append(np.concatenate([np.where(dw < 512, 0.0, NEG), np.where(own, 0.0, NEG)], 1))
        b.append(np.where(own, 0.0, NEG))
    c["mask_sdil"] = np.stack(a).astype(np.float32)
    c["mask_swin"] = np.stack(w).astype(np.float32)
    c["mask_snew"] = np.stack(b).astype(np.float32)
    j = np.arange(NBLK)
    cs = 16 * np.arange(NCMP_S)
    c["overlap"] = ((cs[:, None] <= 64 * j + 63) & (cs[:, None] + 31 >= 64 * j)).astype(np.float32)
    same = (seq[:, None] == seq[None, :]) & (qs[:, None] == qs[None, :]) & ((rows // 16)[:, None] == (rows // 16)[None, :])
    c["same_query"] = same.astype(np.float32)
    c["forced"] = np.broadcast_to(np.where((j == 0) | (j >= NBLK - 2), 1e30, 0.0), (P, NBLK)).astype(np.float32)
    c["earlier"] = np.broadcast_to((j[None, :] < j[:, None]).astype(np.float32).reshape(-1), (P, NBLK * NBLK)).astype(np.float32)
    pick = np.zeros((2, SN, P), np.float32)
    for g in range(2):
        pick[g, 4 * (4 * g + seq) + qs, rows] = 1.0
    c["token_of_row"] = pick.transpose(1, 0, 2).reshape(SN, 2 * P)
    je = (rows % 16 // 4) * 2 + rows % 32 // 16
    c["gate_of_row"] = np.tile((np.arange(8)[None, :] == je[:, None]).astype(np.float32), (1, 3))
    return {k: np.ascontiguousarray(v) for k, v in c.items()}


def tiles(w):
    k, n = w.shape
    return w.reshape(k // P, P, n // P, P).transpose(2, 1, 0, 3)


def by_partition(v):
    return v.reshape(-1, P).T


def lay_out(x_prompt, x_sample, cache_a_kv, cache_b_kv, cache_b_win, cache_mem_kv, cache_ffn_conv, page_table,
            mem_prompt, g_mix, w_in, g_qa, g_ka, g_qb, g_kb, pe_cmp, w_cmp1, w_cmp2, w_br_a, w_br_b, w_o, g_xattn,
            g_mem, w_mq, w_mkv, g_mq, g_mk, w_mo, g_ffn, w_ffn_up, w_conv, b_conv, w_ffn_down):
    a = dict(constants())
    feature = lambda x: x.reshape(-1, D).T.reshape(KD, P, -1).transpose(1, 0, 2)
    a["x"] = np.concatenate([feature(x_prompt), feature(x_sample)], 2)
    a["mem"] = feature(mem_prompt)
    w = w_in[0]
    at = np.cumsum([0, 512, 512, 512, 512, 768, 24, 2048])
    qa, ka, va, qb, kvb, gb, gm = (w[:, at[i]:at[i + 1]] for i in range(7))
    qb = qb.reshape(D, 2, 4, HD).transpose(0, 2, 1, 3).reshape(D, 512)
    gb = gb.reshape(D, 3, 2, 4).transpose(0, 1, 3, 2).reshape(D, 24)
    kv = [kvb[:, i * P:(i + 1) * P] for i in range(6)]
    a["w_proj"] = tiles(np.concatenate([qa, ka, qb, kv[0], kv[2], kv[4], kv[1]], 1))
    a["w_val"] = np.concatenate([va, kv[3], kv[5], gb], 1).reshape(KD, P, VCOL).transpose(1, 0, 2)
    a["w_memk"] = tiles(w_mkv[0][:, :512])
    a["w_memv"] = w_mkv[0][:, 512:].reshape(KD, P, 512).transpose(1, 0, 2)
    two = lambda g: np.tile(g, 2)
    a["g_heads"] = np.stack([two(g_qa[0])] * 4 + [two(g_ka[0])] * 4 + [two(g_qb[0])] * 4
                            + [two(g_kb[0, i]) for i in range(3)], 1)
    a["g_model"] = np.concatenate([by_partition(g[0]) for g in (g_mix, g_mem, g_xattn, g_ffn)], 1)
    a["g_memh"] = np.stack([g_mk[0], g_mq[0]], 1)
    a["w_cmp1"] = w_cmp1[0].reshape(2, 2, 8, 2 * HD, P).transpose(3, 0, 1, 2, 4)
    a["pe_cmp"] = pe_cmp[0].reshape(2, 2, 8, 2 * HD).transpose(3, 0, 1, 2)
    k2 = np.zeros((P, 2, P), np.float32)
    k2[:, 0, :HD] = k2[:, 1, HD:] = w_cmp2[0, 0]
    a["w_cmp2"] = np.concatenate([k2.reshape(P, 2 * P), w_cmp2[0, 1]], 1)
    gates = tiles(gm)
    br_a = tiles(w_br_a[0])
    br_b = tiles(w_br_b[0].reshape(2, 4, HD, D).transpose(1, 0, 2, 3).reshape(512, D))
    chunks = []
    for n in range(KD):
        chunks += [gates[n], gates[KD + n], np.concatenate([br_a[n], br_b[n]], 1)]
    chunks += list(tiles(w_o[0])) + list(tiles(w_mq[0]))
    mo = tiles(w_mo[0])
    chunks += [np.concatenate([mo[n], mo[n + 1]], 1) for n in range(0, KD, 2)]
    up = tiles(w_ffn_up[0])
    for n in range(KF):
        chunks += [up[n], up[KF + n]]
    down = tiles(w_ffn_down[0])
    for n in range(KD):
        padded = np.zeros((P, 24, P), np.float32)
        padded[:, :KF] = down[n]
        chunks += [padded[:, i:i + 8] for i in (0, 8, 16)]
    a["w_close"] = np.stack(chunks)
    cw = w_conv[0].reshape(3, 2 * KF, P).transpose(2, 1, 0)
    a["w_conv"] = np.concatenate([cw, b_conv[0].reshape(2 * KF, P).T[:, :, None]], 2)
    a["ffn_past"] = cache_ffn_conv[0].reshape(NSEQ, 2, 2 * KF, P).transpose(3, 2, 0, 1)
    ka_, va_ = cache_a_kv[0, :, :, 0], cache_a_kv[0, :, :, 1]
    a["past_ka"] = ka_[:, KEYS_A].reshape(NSEQ, NKEY_A, 4, P).transpose(0, 3, 2, 1)
    a["past_va"] = va_[:, KEYS_A].reshape(NSEQ, 7, P, 512).transpose(0, 2, 1, 3)
    pg = cache_b_kv[0]
    n_phys = pg.shape[0]
    cmp_ = pg[:, :, 0:2].reshape(n_phys, 8, 8, 2, 2, 2, HD).transpose(0, 3, 6, 4, 5, 2, 1).reshape(n_phys, P, 256)
    ks_ = pg[:, :, 2].reshape(n_phys, PAGE, P).transpose(0, 2, 1)
    a["pages_k"] = np.concatenate([cmp_, ks_], 2)
    a["pages_v"] = pg[:, :, 3].reshape(n_phys, PAGE, P)
    a["past_kw"] = cache_b_win[0, :, :, 0].reshape(NSEQ, 512, P).transpose(0, 2, 1)
    a["past_vw"] = cache_b_win[0, :, :, 1].reshape(NSEQ, 4, P, P).transpose(0, 2, 1, 3)
    a["past_km"] = cache_mem_kv[0, :, :, 0].transpose(0, 3, 2, 1)
    a["past_vm"] = cache_mem_kv[0, :, :, 1].reshape(NSEQ, 2, P, 512).transpose(0, 2, 1, 3)
    a["page_table"] = page_table.reshape(1, -1).astype(np.int32)
    return {k: np.ascontiguousarray(v) for k, v in a.items()}


OUTS = {
    "o_y": (P, KD, NT), "o_z": (P, NTILE, NT), "o_va": (P, QT, 512), "o_vas": (SN, 512),
    "o_vb": (P, QT, 256), "o_vbs": (SN, 256), "o_mk": (P, MH, MTOK), "o_mv": (P, 2, 512),
    "o_conv": (P, 2 * KF, 18),
}


def lay_back(o):
    y = o["o_y"].transpose(2, 1, 0).reshape(NT, D)
    z = o["o_z"].transpose(2, 1, 0)
    va = np.concatenate([o["o_va"].transpose(1, 0, 2).reshape(T, 512), o["o_vas"]])
    vb = np.concatenate([o["o_vb"].transpose(1, 0, 2).reshape(T, 256), o["o_vbs"]])
    ka = z[:, KA:KA + 4].reshape(NT, 8, HD)
    new_a = np.stack([ka, va.reshape(NT, 8, HD)], 1)
    head = lambda v: v.reshape(NT, 2, HD)
    new_b = np.stack([head(z[:, KC]), head(z[:, VC]), head(z[:, KS]), head(vb[:, :P])], 1)
    new_w = np.stack([head(z[:, KW]), head(vb[:, P:])], 1)
    mk = o["o_mk"].transpose(2, 1, 0)
    mv = o["o_mv"].transpose(1, 0, 2).reshape(MTOK, MH, MHD)
    conv = o["o_conv"].transpose(2, 1, 0).reshape(18, 2 * FF)
    smp = lambda v: v[T:].reshape((1, NSEQ, S) + v.shape[1:])
    pro = lambda v: v[:T].reshape((1, 1, T) + v.shape[1:])
    out = (y[:T].reshape(1, T, D), y[T:].reshape(NSEQ, S, D), pro(new_a), pro(new_b), pro(new_w),
           np.stack([mk, mv], 1)[None, None], conv[:2].reshape(1, 1, 2, 2 * FF),
           smp(new_a), smp(new_b), smp(new_w), conv[2:].reshape(1, NSEQ, 2, 2 * FF))
    return tuple(np.ascontiguousarray(v) for v in out)


class Steps:

    def __init__(self, engine, sem):
        self.engine, self.sem, self.n, self.offset = engine, sem, 0, None

    def done(self, instruction):
        instruction.then_inc(self.sem, 1)
        self.n += 1
        return self.n

    def wait(self, n=None):
        n = self.n if n is None else n
        self.engine.wait_ge(self.sem, n if self.offset is None else self.offset + n)


def halves(ap):
    return ap.rearrange("p (a b) -> p a b", a=2)


def reciprocal_root(dve, act, who, v, y, t, v_ready, y_ready, n, steps=None):
    if who == "act":
        act.wait_ge(v_ready, n + 1)
        act.activation(y, v, ACT.Ln).then_inc(y_ready, 1)
        act.wait_ge(y_ready, 2 * n + 1)
        act.activation(y, y, ACT.Exp, scale=-0.5).then_inc(y_ready, 1)
    else:
        dve.wait_ge(y_ready, 2 * n + 2)
        steps.done(dve.scalar_tensor_tensor(out=t, in0=v, scalar=-0.5, in1=y, op0=ALU.mult, op1=ALU.mult))
        steps.wait()
        steps.done(dve.tensor_tensor(t, t, y, ALU.mult))
        steps.wait()
        steps.done(dve.scalar_tensor_tensor(out=y, in0=t, scalar=1.5, in1=y, op0=ALU.add, op1=ALU.mult))
        steps.wait()


def project(nc, d, m, sem):
    with ExitStack() as mine:
        def sb(name, shape, dt=F32):
            return mine.enter_context(nc.sbuf_tensor(name, shape, dt))

        ps = m.ps
        x, h = sb("x", [P, KD, NT]), sb("h", [P, KD, NT])
        ring = sb("proj_ring", [P, RING, KD, P])
        w_val = sb("w_val_sb", [P, KD, VCOL])
        w_memv = sb("w_memv_sb", [P, KD, 512])
        mem = sb("mem_sb", [P, KD, MTOK])
        head_ones = sb("head_ones_sb", [P, P])
        rot = sb("rot_sb", [P, P])
        cos, sin = sb("cos_sb", [P, NT]), sb("sin_sb", [P, NT])
        g_heads = sb("g_heads_sb", [P, 15])
        mean, root, scratch = sb("mean", [P, NT]), sb("root", [P, NT]), sb("scratch", [P, NT])
        raw, square, normed = sb("raw", [P, 2, NT]), sb("square", [P, 2, NT]), sb("normed", [P, 2, NT])
        hm = m.oa

        def z_pair(j):
            return ps[:, 2 * (j % 2):2 * (j % 2) + 2, 0:HALF]

        sum_pair, rot_pair = ps[:, 4:6, 0:HALF], ps[:, 6:8, 0:HALF]
        order = [VC] + list(range(VC))
        NJOB = NTILE + MH
        NVAL = QT + 1 + 2

        const_in, x_in, mem_in = sem("const_in"), sem("x_in"), sem("mem_in")
        val_in, memv_in = sem("val_in"), sem("memv_in")
        chunk_in = [sem(f"proj_chunk{i}") for i in range(RING)]
        squared, sum_full = sem("squared"), sem("sum_full")
        v_ready, y_ready = sem("mean_ready"), sem("root_ready")
        h_ready = sem("h_ready")
        z_full, z_out = sem("z_full"), sem("z_out")
        n_ready, rot_full, tile_done = sem("normed_ready"), sem("rot_full"), sem("tile_done")
        val_full, val_out, gate_ready = sem("val_full"), sem("val_out"), sem("gate_ready")
        dve_step = sem("proj_dve_step")
        stored = sem("proj_stored")

        with nc.Block() as block:
            @block.sync
            def _(sp):
                for dst, name in ((m.ones, "ones"), (m.g_model, "g_model"), (head_ones, "head_ones"), (rot, "rot"),
                                  (cos, "cos"), (sin, "sin"), (g_heads, "g_heads"), (m.g_memh, "g_memh"),
                                  (m.ident, "ident")):
                    sp.dma_start(dst[:, :], d[name]).then_inc(const_in, 16)
                for j in range(NJOB):
                    if j >= RING:
                        sp.wait_ge(z_full, j - RING + 1)
                    src = d["w_proj"][order[j]] if j < NTILE else d["w_memk"][j - NTILE]
                    sp.dma_start(ring[:, j % RING], src).then_inc(chunk_in[j % RING], 16)
                sp.wait_ge(z_out, 1)
                sp.wait_ge(tile_done, NJOB - 1)
                sp.dma_start(d["o_z"], m.z[:, :, :]).then_inc(stored, 16)
                sp.dma_start(d["o_mk"], m.mk[:, :, :]).then_inc(stored, 16)
                sp.wait_ge(val_out, NVAL)
                sp.dma_start(d["o_va"], m.va[:, 0:QT, :]).then_inc(stored, 16)
                sp.dma_start(d["o_vas"], m.va[0:SN, QT, :]).then_inc(stored, 16)
                sp.dma_start(d["o_vb"], m.vb[:, 0:QT, :]).then_inc(stored, 16)
                sp.dma_start(d["o_vbs"], m.vb[0:SN, QT, :]).then_inc(stored, 16)
                sp.dma_start(d["o_mv"], m.mv[:, :, :]).then_inc(stored, 16)
                sp.wait_ge(stored, 16 * 7)

            @block.scalar
            def _(act):
                act.dma_start(x[:, :, :], d["x"]).then_inc(x_in, 16)
                act.dma_start(mem[:, :, :], d["mem"]).then_inc(mem_in, 16)
                act.dma_start(w_val[:, :, :], d["w_val"]).then_inc(val_in, 16)
                act.dma_start(w_memv[:, :, :], d["w_memv"]).then_inc(memv_in, 16)
                act.wait_ge(x_in, 16)
                for k in range(KD):
                    act.activation(h[:, k, :], x[:, k, :], ACT.Square).then_inc(squared, 1)
                act.wait_ge(mem_in, 16)
                for k in range(KD):
                    act.activation(hm[:, k, 0:MTOK], mem[:, k, :], ACT.Square).then_inc(squared, 1)
                reciprocal_root(None, act, "act", mean[:, :], root[:, :], None, v_ready, y_ready, 0)
                reciprocal_root(None, act, "act", mean[:, 0:MTOK], root[:, 0:MTOK], None, v_ready, y_ready, 1)

                def roots(j):
                    c = slice(0, NT if j < NTILE else MTOK)
                    reciprocal_root(None, act, "act", mean[:, c], root[:, c], None, v_ready, y_ready, j + 1)

                for j in range(NJOB):
                    act.wait_ge(z_full, j + 1)
                    if j == 0:
                        act.copy(halves(m.z[:, VC, :]), z_pair(0)).then_inc(z_out, 1)
                        continue
                    if j >= 3:
                        act.wait_ge(tile_done, j - 2)
                        act.wait_ge(sum_full, j)
                    if j < NTILE:
                        act.copy(halves(raw[:, j % 2, :]), z_pair(j))
                        act.activation(halves(square[:, j % 2, :]), z_pair(j), ACT.Square).then_inc(z_out, 1)
                    else:
                        act.copy(raw[:, j % 2, 0:MTOK], z_pair(j)[:, 0, 0:MTOK])
                        act.activation(square[:, j % 2, 0:MTOK], z_pair(j)[:, 0, 0:MTOK], ACT.Square)\
                            .then_inc(z_out, 1)
                    if j >= 2:
                        roots(j - 1)
                roots(NJOB - 1)
                for u in range(NVAL):
                    act.wait_ge(val_full, u + 1)
                    wide, narrow = ps[:, 2 * (u % 2), :], ps[:, 2 * (u % 2) + 1, :]
                    if u > QT:
                        act.copy(m.mv[:, u - QT - 1, :], wide).then_inc(val_out, 1)
                        continue
                    n = P if u < QT else SN
                    act.copy(m.va[0:n, u, :], wide[0:n])
                    act.copy(m.vb[0:n, u, :], narrow[0:n, 0:256])
                    act.activation(m.gate[0:n, u, :], narrow[0:n, 256:280], ACT.Exp, scale=-1.0).then_inc(val_out, 1)

            @block.tensor
            def _(pe):
                def sums(j, lhs, src, width, k_tiles):
                    for k in range(k_tiles):
                        if width == NT:
                            for a in range(2):
                                last = pe.matmul(ps[:, 4 + a, 0:HALF], lhs, src(k)[:, a * HALF:(a + 1) * HALF],
                                                 start=(k == 0), stop=(k == k_tiles - 1))
                        else:
                            last = pe.matmul(ps[:, 4, 0:width], lhs, src(k)[:, 0:width],
                                             start=(k == 0), stop=(k == k_tiles - 1))
                    last.then_inc(sum_full, 1)

                pe.wait_ge(const_in, 16 * 9)
                pe.wait_ge(squared, KD)
                sums(0, m.ones[:, :], lambda k: h[:, k, :], NT, KD)
                pe.wait_ge(squared, 2 * KD)
                pe.wait_ge(v_ready, 1)
                sums(0, m.ones[:, :], lambda k: hm[:, k, :], MTOK, KD)
                pe.wait_ge(h_ready, 1)

                def product(j):
                    pe.wait_ge(chunk_in[j % RING], 16 * (j // RING + 1))
                    if j >= 2:
                        pe.wait_ge(z_out, j - 1)
                    if j == NTILE:
                        pe.wait_ge(h_ready, 2)
                    for k in range(KD):
                        w = ring[:, j % RING, k, :]
                        if j < NTILE:
                            for a in range(2):
                                last = pe.matmul(ps[:, 2 * (j % 2) + a, 0:HALF], w, h[:, k, a * HALF:(a + 1) * HALF],
                                                 start=(k == 0), stop=(k == KD - 1))
                        else:
                            last = pe.matmul(ps[:, 2 * (j % 2), 0:MTOK], w, hm[:, k, 0:MTOK],
                                             start=(k == 0), stop=(k == KD - 1))
                    last.then_inc(z_full, 1)

                def job_sum(j):
                    pe.wait_ge(z_out, j + 1)
                    pe.wait_ge(v_ready, j + 1)
                    lhs = head_ones if j < NTILE else m.ones
                    sums(j, lhs[:, :], lambda k: square[:, j % 2, :], NT if j < NTILE else MTOK, 1)

                def job_rot(j):
                    pe.wait_ge(n_ready, j)
                    if j >= 2:
                        pe.wait_ge(tile_done, j - 1)
                    for a in range(2):
                        last = pe.matmul(ps[:, 6 + a, 0:HALF], rot[:, :], normed[:, j % 2, a * HALF:(a + 1) * HALF],
                                         start=True, stop=True)
                    last.then_inc(rot_full, 1)

                for j in range(NJOB + 2):
                    if j < NJOB:
                        product(j)
                    if 1 <= j - 1 < NJOB:
                        job_sum(j - 1)
                    if 1 <= j - 2 < NTILE:
                        job_rot(j - 2)
                pe.wait_ge(val_in, 16)
                pe.wait_ge(memv_in, 16)
                for u in range(NVAL):
                    pe.wait_ge(z_out, NJOB)
                    if u >= 2:
                        pe.wait_ge(val_out, u - 1)
                    wide, narrow = ps[:, 2 * (u % 2), :], ps[:, 2 * (u % 2) + 1, :]
                    if u > QT:
                        for k in range(KD):
                            last = pe.matmul(wide, hm[:, k, (u - QT - 1) * P:(u - QT) * P], w_memv[:, k, :],
                                             start=(k == 0), stop=(k == KD - 1))
                    else:
                        n = P if u < QT else SN
                        for cols, out in ((slice(0, 512), wide[0:n]), (slice(512, VCOL), narrow[0:n, 0:VCOL - 512])):
                            for k in range(KD):
                                last = pe.matmul(out, h[:, k, u * P:u * P + n], w_val[:, k, cols],
                                                 start=(k == 0), stop=(k == KD - 1))
                    last.then_inc(val_full, 1)

            @block.vector
            def _(dve):
                step = Steps(dve, dve_step)

                def root_of(j, full, cols, divisor):
                    dve.wait_ge(sum_full, j + 1)
                    pair, mean_ = full
                    dve.tensor_scalar(mean_, pair, 1.0 / divisor, EPS, ALU.mult, ALU.add).then_inc(v_ready, 1)
                    dve.wait_ge(v_ready, j + 1)
                    reciprocal_root(dve, None, "dve", mean[:, 0:cols], root[:, 0:cols], scratch[:, 0:cols],
                                    v_ready, y_ready, j, step)

                dve.wait_ge(const_in, 16 * 9)
                root_of(0, (sum_pair, halves(mean[:, :])), NT, D)
                for k in range(KD):
                    last = dve.scalar_tensor_tensor(out=h[:, k, :], in0=x[:, k, :], scalar=m.g_model[:, k:k + 1],
                                                    in1=root[:, :], op0=ALU.mult, op1=ALU.mult)
                last.then_inc(h_ready, 1)
                dve.wait_ge(h_ready, 1)
                root_of(1, (ps[:, 4, 0:MTOK], mean[:, 0:MTOK]), MTOK, D)
                for k in range(KD):
                    last = dve.scalar_tensor_tensor(out=hm[:, k, 0:MTOK], in0=mem[:, k, :],
                                                    scalar=m.g_model[:, KD + k:KD + k + 1],
                                                    in1=root[:, 0:MTOK], op0=ALU.mult, op1=ALU.mult)
                last.then_inc(h_ready, 1)
                for j in range(1, NJOB):
                    if j < NTILE:
                        root_of(j + 1, (sum_pair, halves(mean[:, :])), NT, HD)
                        t = order[j]
                        if j >= 3:
                            dve.wait_ge(rot_full, j - 2)
                        dve.scalar_tensor_tensor(out=normed[:, j % 2, :], in0=raw[:, j % 2, :],
                                                 scalar=g_heads[:, t:t + 1], in1=root[:, :],
                                                 op0=ALU.mult, op1=ALU.mult).then_inc(n_ready, 1)
                        dve.wait_ge(rot_full, j)
                        step.done(dve.tensor_tensor(halves(scratch[:, :]), rot_pair, halves(sin[:, :]), ALU.mult))
                        dve.wait_ge(n_ready, j)
                        step.done(dve.tensor_tensor(m.z[:, t, :], normed[:, j % 2, :], cos[:, :], ALU.mult))
                        step.wait()
                        dve.tensor_tensor(m.z[:, t, :], m.z[:, t, :], scratch[:, :], ALU.add).then_inc(tile_done, 1)
                        dve.wait_ge(tile_done, j)
                    else:
                        root_of(j + 1, (ps[:, 4, 0:MTOK], mean[:, 0:MTOK]), MTOK, MHD)
                        dve.scalar_tensor_tensor(out=m.mk[:, j - NTILE, :], in0=raw[:, j % 2, 0:MTOK],
                                                 scalar=m.g_memh[:, 0:1], in1=root[:, 0:MTOK],
                                                 op0=ALU.mult, op1=ALU.mult).then_inc(tile_done, 1)
                        dve.wait_ge(tile_done, j)
                dve.wait_ge(val_out, QT + 1)
                for part in (m.gate[:, 0:QT, :], m.gate[0:SN, QT, :]):
                    step.done(dve.tensor_scalar(part, part, 1.0, None, ALU.add))
                    step.wait()
                    dve.reciprocal(part, part).then_inc(gate_ready, 1)


def one(t, index, cols):
    return t[:, ds(index, 1), cols].rearrange("p a n -> p (a n)")


class Compress:

    GELU, CUBE = -2.0 * (2.0 / np.pi) ** 0.5, 0.044715

    def __init__(self, sb, sem, ps, w1, w2, bias, n, banks):
        self.ps, self.w1, self.w2, self.bias, self.n = ps, w1, w2, bias, n
        self.proj, self.small = banks
        self.second = sb(f"cmp_second{n}", [P, 2, n])
        self.hid = sb(f"cmp_hid{n}", [P, 2, n])
        self.cube = sb(f"cmp_cube{n}", [P, 2, n])
        self.proj_full, self.second_ready = sem(f"cmp_proj_full{n}"), sem(f"cmp_second_ready{n}")
        self.inner_ready, self.exp_ready = sem(f"cmp_inner_ready{n}"), sem(f"cmp_exp_ready{n}")
        self.hid_ready, self.small_full, self.small_out = (sem(f"cmp_hid_ready{n}"), sem(f"cmp_small_full{n}"),
                                                          sem(f"cmp_small_out{n}"))

    def parts(self):
        v = self.ps[:, self.proj, 0:4 * self.n].rearrange("p (r g c) -> p r g c", r=2, g=2)
        return v[:, 0], v[:, 1]

    def pe_project(self, pe, kv, x):
        for r in range(2):
            for s1 in range(8):
                last = pe.matmul(self.parts()[r], self.w1[:, kv, r, s1, :], x(s1), start=(s1 == 0), stop=(s1 == 7))
        last.then_inc(self.proj_full, 1)

    def act_second(self, act, turn, kv):
        act.wait_ge(self.proj_full, turn + 1)
        act.activation(self.second[:, :, :], self.parts()[1], ACT.Identity, bias=self.bias[:, kv:kv + 1])\
            .then_inc(self.second_ready, 1)

    def dve_inner(self, dve, step, turn):
        n = self.n
        a, b = self.hid[:, :, 0:n - 1], self.cube[:, :, 0:n - 1]
        dve.wait_ge(self.second_ready, turn + 1)
        step.done(dve.tensor_tensor(a, self.second[:, :, 1:n], self.parts()[0][:, :, 0:n - 1], ALU.add))
        step.wait()
        step.done(dve.tensor_tensor(b, a, a, ALU.mult))
        step.wait()
        step.done(dve.scalar_tensor_tensor(out=b, in0=b, scalar=self.CUBE, in1=a, op0=ALU.mult, op1=ALU.mult))
        step.wait()
        step.done(dve.tensor_tensor(b, b, a, ALU.add))
        step.wait()
        dve.tensor_scalar(b, b, -50.0, None, ALU.max).then_inc(self.inner_ready, 1)

    def act_exp(self, act, turn):
        b = self.cube[:, :, 0:self.n - 1]
        act.wait_ge(self.inner_ready, turn + 1)
        act.activation(b, b, ACT.Exp, scale=self.GELU).then_inc(self.exp_ready, 1)

    def dve_hidden(self, dve, step, turn):
        a, b = self.hid[:, :, 0:self.n - 1], self.cube[:, :, 0:self.n - 1]
        dve.wait_ge(self.exp_ready, turn + 1)
        step.done(dve.tensor_scalar(b, b, 1.0, None, ALU.add))
        step.wait()
        step.done(dve.reciprocal(b, b))
        step.wait()
        dve.tensor_tensor(a, a, b, ALU.mult).then_inc(self.hid_ready, 1)

    def pe_small(self, pe, turn, kv):
        n = self.n
        pe.wait_ge(self.hid_ready, turn + 1)
        for g in range(2):
            if kv == 0:
                last = pe.matmul(self.ps[:, self.small, 0:n - 1], self.w2[:, g * P:(g + 1) * P],
                                 self.hid[:, g, 0:n - 1], start=(g == 0), stop=(g == 1))
            else:
                last = pe.matmul(self.ps[0:n - 1, self.small, P + g * HD:P + (g + 1) * HD],
                                 self.hid[:, g, 0:n - 1], self.w2[:, 2 * P:2 * P + HD], start=True, stop=True)
        last.then_inc(self.small_full, 1)

    def act_small(self, act, turn, kv, dst):
        act.wait_ge(self.small_full, turn + 1)
        n = self.n
        src = self.ps[:, self.small, 0:n - 1] if kv == 0 else self.ps[0:n - 1, self.small, P:2 * P]
        act.copy(dst, src).then_inc(self.small_out, 1)


def attend_prompt(nc, d, m, sem):
    with ExitStack() as mine:
        def sb(name, shape, dt=F32):
            return mine.enter_context(nc.sbuf_tensor(name, shape, dt))

        ps = m.ps
        mask_dil, mask_causal = sb("mask_dil_sb", [P, T]), sb("mask_causal_sb", [P, T])
        mask_cmp, live = sb("mask_cmp_sb", [P, QT * NCMP_P]), sb("cmp_live_sb", [P, QT])
        w1, w2, pe_col = sb("pw1", [P, 2, 2, 8, P]), sb("pw2", [P, 320]), sb("pe_col", [P, 2, 2, 8])
        chunked = sb("chunked", [P, 2, 2, 8, 32])
        q_pad = [sb(f"q_pad{i}", [P, T]) for i in range(4)]
        kc, vc = sb("kc", [P, NCMP_P]), sb("vc", [NCMP_P, P])
        score, prob_t = sb("score", [P, 3, T]), sb("prob_t", [P, 2, T])
        low, total, factor = sb("low", [P, 8]), sb("total", [P, 8]), sb("factor", [P, 2])
        o_dil, o_nsa = sb("o_dil", [P, QT, P]), sb("o_nsa", [P, QT, P])

        const_in = sem("prompt_const_in")
        chunked_ready, bias_full, bias_out = sem("chunked_ready"), sem("bias_full"), sem("bias_out")
        zeroed, pads_ready = sem("pads_zeroed"), sem("pads_ready")
        s_full, s_done, e_done = sem("s_full"), sem("s_done"), sem("e_done")
        pt_full, pt_out = sem("pt_full"), sem("pt_out")
        o_full, o_out = sem("o_full"), sem("o_out")
        ot_full, ot_out = sem("ot_full"), sem("ot_out")
        dve_step, begun = sem("prompt_dve_step"), sem("prompt_begun")
        cmp = Compress(sb, sem, ps, w1, w2, m.cmp_bias, 32, (4, 5))
        DIL, SLC, WIN, CMP = range(4)
        units = [(e, kind, qt) for e in range(2) for kind in (DIL, SLC, WIN, CMP) for qt in range(QT)]
        U = len(units)

        def width(u):
            return NCMP_P if units[u][1] == CMP else (units[u][2] + 1) * P

        with nc.Block() as block:
            @block.sync
            def _(sp):
                for dst, name in ((w1, "w_cmp1"), (pe_col, "pe_cmp"), (w2, "w_cmp2"), (mask_dil, "mask_dil"),
                                  (mask_causal, "mask_causal"), (mask_cmp, "mask_cmp"), (live, "cmp_live")):
                    full = (slice(None),) * len(dst.shape)
                    sp.dma_start(dst[full], d[name]).then_inc(const_in, 16)

            @block.gpsimd
            def _(pool):
                for dst, src in ((m.zs[:, :, :], m.z[:, :, T:NT]), (m.vas[:, :], m.va[0:SN, QT, :]),
                                 (m.vbs[:, :], m.vb[0:SN, QT, :]), (m.gates[:, :], m.gate[0:SN, QT, :])):
                    pool.tensor_copy(dst, src)
                for i in range(4):
                    pool.memset(q_pad[i][:, :], 0.0).then_inc(zeroed, 1)
                pool.wait_ge(zeroed, 4)
                with pool.Fori(0, 4) as j:
                    for i in range(4):
                        e = i % 2
                        src = one(m.z, j + (QA if i < 2 else QB), slice(0, T))
                        pool.tensor_copy(q_pad[i][e * HD:(e + 1) * HD, :], src[e * HD:(e + 1) * HD, :])\
                            .then_inc(pads_ready, 1)
                    pool.wait_ge(s_full, j * U + U)

            @block.scalar
            def _(act):
                act.wait_ge(bias_full, 1)
                act.copy(m.cmp_bias[:, :], ps[:, 6, 0:2]).then_inc(bias_out, 1)
                act.wait_ge(bias_out, 1)
                for kv in range(2):
                    cmp.act_second(act, kv, kv)
                    cmp.act_exp(act, kv)
                    cmp.act_small(act, kv, kv, (kc, vc)[kv][:, :])
                with act.Fori(0, 4) as j:
                    for u in range(U + 1):
                        if u < U:
                            n = width(u)
                            act.wait_ge(s_done, j * U + (u + 1))
                            act.activation(score[:, u % 3, 0:n], score[:, u % 3, 0:n], ACT.Exp,
                                           bias=low[:, u % 8:u % 8 + 1], scale=-1.0,
                                           accum_out=total[:, u % 8:u % 8 + 1]).then_inc(e_done, 1)
                        if u >= 1:
                            v = u - 1
                            act.wait_ge(pt_full, j * U + (v + 1))
                            if v >= 2:
                                act.wait_ge(o_full, j * U + (v - 1))
                            if units[v][1] == CMP:
                                act.copy(prob_t[0:NCMP_P, v % 2, 0:P], ps[0:NCMP_P, 4 + v % 2, 0:P])\
                                    .then_inc(pt_out, 1)
                            else:
                                act.copy(prob_t[:, v % 2, 0:width(v)], ps[:, 4 + v % 2, 0:width(v)])\
                                    .then_inc(pt_out, 1)
                    for i in range(2):
                        act.wait_ge(ot_full, j * 2 + (i + 1))
                        act.copy(one(m.oa, j + 4 * i, slice(0, T)), ps[:, 4 + i, :]).then_inc(ot_out, 1)

            @block.tensor
            def _(pe):
                pe.wait_ge(const_in, 16 * 7)
                for kv in range(2):
                    for r in range(2):
                        for s1 in range(8):
                            last = pe.matmul(ps[:, 6, kv:kv + 1], w1[:, kv, r, s1, :], pe_col[:, kv, r, s1:s1 + 1],
                                             start=(r + s1 == 0), stop=(r + s1 == 8))
                last.then_inc(bias_full, 1)
                pe.wait_ge(chunked_ready, 8)
                for kv in range(2):
                    if kv == 1:
                        pe.wait_ge(cmp.hid_ready, 1)
                    cmp.pe_project(pe, kv, lambda s1: chunked[:, kv, :, s1, :])
                    cmp.pe_small(pe, kv, kv)
                pe.wait_ge(cmp.small_out, 2)
                with pe.Fori(0, 4) as j:
                    def scores(u):
                        e, kind, qt = units[u]
                        if u >= 4:
                            pe.wait_ge(s_done, j * U + (u - 3))
                        key = {DIL: lambda n: one(m.z, j + KA, slice(0, n)), SLC: lambda n: m.z[:, KS, 0:n],
                               WIN: lambda n: m.z[:, KW, 0:n], CMP: lambda n: kc[:, 0:n]}[kind]
                        q = q_pad[e if kind == DIL else 2 + e]
                        pe.matmul(ps[:, u % 4, 0:width(u)], q[:, qt * P:(qt + 1) * P], key(width(u)),
                                  start=True, stop=True).then_inc(s_full, 1)

                    def turn(u):
                        e, kind, qt = units[u]
                        pe.wait_ge(e_done, j * U + (u + 1))
                        if u >= 2:
                            pe.wait_ge(pt_out, j * U + (u - 1))
                        if kind == CMP:
                            last = pe.transpose(ps[0:NCMP_P, 4 + u % 2, 0:P], score[:, u % 3, 0:NCMP_P], m.ident[:, :])
                        else:
                            for k in range(qt + 1):
                                last = pe.transpose(ps[:, 4 + u % 2, k * P:(k + 1) * P],
                                                    score[:, u % 3, k * P:(k + 1) * P], m.ident[:, :])
                        last.then_inc(pt_full, 1)

                    def values(u):
                        e, kind, qt = units[u]
                        pe.wait_ge(pt_out, j * U + (u + 1))
                        if u >= 2:
                            pe.wait_ge(o_out, j * U + (u - 1))
                        out = ps[:, 6 + u % 2, 0:HD]
                        if kind == CMP:
                            last = pe.matmul(out, prob_t[0:NCMP_P, u % 2, 0:P], vc[:, e * HD:(e + 1) * HD],
                                             start=True, stop=True)
                        else:
                            for k in range(qt + 1):
                                v = m.va[:, k, ds(j * P + e * HD, HD)] if kind == DIL else \
                                    m.vb[:, k, (kind == WIN) * P + e * HD:(kind == WIN) * P + (e + 1) * HD]
                                last = pe.matmul(out, prob_t[:, u % 2, k * P:(k + 1) * P], v,
                                                 start=(k == 0), stop=(k == qt))
                        last.then_inc(o_full, 1)

                    pe.wait_ge(pads_ready, j * 4 + 4)
                    for u in range(U + 3):
                        if u < U:
                            scores(u)
                        if 0 <= u - 2 < U:
                            turn(u - 2)
                        if 0 <= u - 3 < U:
                            values(u - 3)
                    pe.wait_ge(o_out, j * U + U)
                    for i, o in enumerate((o_dil, o_nsa)):
                        for qt in range(QT):
                            last = pe.transpose(ps[:, 4 + i, qt * P:(qt + 1) * P], o[:, qt, :], m.ident[:, :])
                        last.then_inc(ot_full, 1)
                    pe.wait_ge(ot_out, j * 2 + 2)

            @block.vector
            def _(dve):
                step = Steps(dve, dve_step)
                for kv, tile in enumerate((KC, VC)):
                    v = m.z[:, tile, 0:T].rearrange("p (c s t) -> p t s c", s=8, t=2)
                    for g in range(2):
                        for s2 in range(2):
                            dve.tensor_copy(chunked[s2 * HD:(s2 + 1) * HD, kv, g], v[g * HD:(g + 1) * HD, s2])\
                                .then_inc(chunked_ready, 1)
                for kv in range(2):
                    cmp.dve_inner(dve, step, kv)
                    cmp.dve_hidden(dve, step, kv)
                dve.wait_ge(const_in, 16 * 7)
                with dve.Fori(0, 4) as j:
                    PER = 64
                    first, step.offset = step.n, j * PER

                    def finish_unit(u):
                        e, kind, qt = units[u]
                        r, f = total[:, u % 8:u % 8 + 1], factor[:, u % 2:u % 2 + 1]
                        step.done(dve.reciprocal(f, r))
                        step.wait()
                        if kind != DIL:
                            branch = (CMP, SLC, WIN).index(kind)
                            gate = m.gate[:, qt, ds(j * 2 + branch * 8 + e, 1)]
                            if kind == CMP:
                                step.done(dve.tensor_tensor(f, f, live[:, qt:qt + 1], ALU.mult))
                                step.wait()
                            step.done(dve.tensor_tensor(f, f, gate, ALU.mult))
                            step.wait()
                        o = (o_dil if kind == DIL else o_nsa)[:, qt, e * HD:(e + 1) * HD]
                        src = ps[:, 6 + u % 2, 0:HD]
                        dve.wait_ge(o_full, j * U + (u + 1))
                        if kind in (DIL, SLC):
                            dve.tensor_scalar(o, src, f, None, ALU.mult).then_inc(o_out, 1)
                        else:
                            dve.wait_ge(o_out, j * U + (u - 3))
                            dve.scalar_tensor_tensor(out=o, in0=src, scalar=f, in1=o, op0=ALU.mult, op1=ALU.add)\
                                .then_inc(o_out, 1)

                    for u in range(U + 4):
                        if u < U:
                            e, kind, qt = units[u]
                            n = width(u)
                            table = {DIL: mask_dil, SLC: mask_causal, WIN: mask_causal}.get(kind)
                            mask = mask_cmp[:, qt * NCMP_P:(qt + 1) * NCMP_P] if kind == CMP else table[:, T - n:T]
                            dve.wait_ge(s_full, j * U + (u + 1))
                            if u >= 3:
                                dve.wait_ge(pt_full, j * U + (u - 2))
                            dve.sem_inc(begun, 1)
                            dve.tensor_tensor_reduce(score[:, u % 3, 0:n], ps[:, u % 4, 0:n], mask, -SCALE, 3e38,
                                                     ALU.add, ALU.min, low[:, u % 8:u % 8 + 1]).then_inc(s_done, 1)
                        if u >= 4:
                            dve.wait_ge(e_done, j * U + (u - 3))
                            finish_unit(u - 4)
                    dve.wait_ge(ot_full, j * 2 + 2)
                    assert step.n - first == PER
                step.offset = None




def attend_sample(nc, d, m, sem):
    with ExitStack() as mine:
        def sb(name, shape, dt=F32):
            return mine.enter_context(nc.sbuf_tensor(name, shape, dt))

        ps = m.ps
        NB = NPAGE
        pages = sb("pages", [P, 2, NB * 384])
        dil = sb("dil", [P, 2, 7 * 512])
        win = sb("win", [P, 2, 512])
        w1, w2 = sb("sw1", [P, 2, 2, 8, P]), sb("sw2", [P, 320])
        q_dil, q_nsa = sb("q_dil", [P, 4, P]), sb("q_nsa", [P, P])
        s_dil, s_slc = sb("s_dil", [P, NKEY_A + SN]), sb("s_slc", [P, PAST + SN])
        s_win, s_cmp = sb("s_win", [P, 512 + SN]), sb("s_cmp", [P, NCMP_S])
        mask_dil, mask_win = sb("mask_sdil_sb", [P, NKEY_A + SN]), sb("mask_swin_sb", [P, 512 + SN])
        mask_new, pick = sb("mask_snew_sb", [P, SN]), sb("pick_sb", [SN, P])
        t_dil, t_slc = sb("t_dil", [P, 8, P]), sb("t_slc", [P, 18, P])
        t_win, t_cmp, t_cmpg = sb("t_win", [P, 5, P]), sb("t_cmp", [P, P]), sb("t_cmpg", [P, P])
        kc, vc = sb("skc", [P, NCMP_S]), sb("svc", [NCMP_S, 4, P])
        overlap, same = sb("overlap_sb", [NCMP_S, NBLK]), sb("same_sb", [P, P])
        forced, earlier = sb("forced_sb", [P, NBLK]), sb("earlier_sb", [P, NBLK * NBLK])
        gate_pick, gates = sb("gate_pick_sb", [P, 24]), sb("gates", [P, 24])
        gate3, importance = sb("gate3", [P, 3]), sb("importance", [P, NBLK])
        points, drop = sb("points", [P, NBLK]), sb("drop", [P, NBLK])
        small = sb("small_s", [P, 16])
        low, total, factor = (lambda i: small[:, i:i + 1]), (lambda i: small[:, 4 + i:5 + i]), \
            (lambda i: small[:, 8 + i:9 + i])
        table = sb("page_table_sb", [1, NSEQ * NPAGE], I32)
        rank = t_slc[:, :, :].rearrange("p a b -> p (a b)")
        beats, ties = (rank[:, i * NBLK * NBLK:(i + 1) * NBLK * NBLK].rearrange("p (j i) -> p j i", i=NBLK)
                       for i in range(2))

        table_in, const_in = sem("table_in"), sem("sample_const_in")
        pages_in = [sem(f"pages_in{i}") for i in range(2)]
        dil_in = [sem(f"dil_in{i}") for i in range(2)]
        win_in = [sem(f"win_in{i}") for i in range(2)]
        slot_used = sem("slot_used")
        group_in, group_used = sem("group_in"), sem("group_used")
        q_zero, q_ready, k_pass = sem("q_zero"), sem("q_ready"), sem("k_pass")
        tile_full, tile_act, tile_dve = sem("tile_full"), sem("tile_act"), sem("tile_dve")
        new_full, new_out = sem("new_full"), sem("new_out")
        low_ready, exp_ready, prob_ready = sem("low_ready"), sem("sexp_ready"), sem("prob_ready")
        turn_full, turn_out = sem("turn_full"), sem("turn_out")
        imp_full, imp_out, points_full = sem("imp_full"), sem("imp_out"), sem("points_full")
        so_full, so_out = sem("so_full"), sem("so_out")
        dve_step, begun = sem("sample_dve_step"), sem("sample_begun")
        cmp = Compress(sb, sem, ps, w1, w2, m.cmp_bias, 128, (0, 1))
        C, A, W, S_ = range(4)
        turns = [(1, s_cmp, [0], t_cmp), (2, s_cmp, [0], t_cmpg), (3, s_dil, [0, 1, 2, 3], t_dil),
                 (3, s_dil, [4, 5, 6, 7], t_dil), (4, s_win, [0, 1, 2, 3], t_win), (4, s_win, [4], t_win)] \
            + [(5, s_slc, list(range(a, min(a + 4, NB + 1))), t_slc) for a in range(0, NB + 1, 4)]
        NTURN = len(turns)

        with nc.Block() as block:
            @block.sync
            def _(sp):
                sp.dma_start(table[:, :], d["page_table"]).then_inc(table_in, 16)
                for dst, name in ((w1, "w_cmp1"), (w2, "w_cmp2"), (overlap, "overlap"), (same, "same_query"),
                                  (forced, "forced"), (earlier, "earlier"), (gate_pick, "gate_of_row")):
                    sp.dma_start(dst[(slice(None),) * len(dst.shape)], d[name]).then_inc(const_in, 16)
                sp.wait_ge(table_in, 16)
                sp.sem_inc(slot_used, 2)
                sp.sem_inc(group_used, 1)
                with sp.Fori(0, 2) as g:
                    for load in range(8):
                        i, slot = load % 4, load % 2
                        seq = g * 4 + i
                        sp.wait_ge(slot_used, g * 8 + (load + 1))
                        if load < 4:
                            sp.dma_start(dil[:, slot, :], d["past_ka"][ds(seq, 1)].rearrange("a p h n -> p (a h n)"))\
                                .then_inc(dil_in[slot], 16)
                            sp.dma_start(win[:, slot, :], d["past_kw"][ds(seq, 1)].rearrange("a p n -> p (a n)"))\
                                .then_inc(win_in[slot], 16)
                        else:
                            sp.dma_start(dil[:, slot, :], d["past_va"][ds(seq, 1)].rearrange("a p h n -> p (a h n)"))\
                                .then_inc(dil_in[slot], 16)
                            sp.dma_start(win[:, slot, :], d["past_vw"][ds(seq, 1)].rearrange("a p h n -> p (a h n)"))\
                                .then_inc(win_in[slot], 16)
                        if load == 0:
                            sp.wait_ge(group_used, g + 1)
                            for dst, name in ((mask_dil, "mask_sdil"), (mask_win, "mask_swin"), (mask_new, "mask_snew")):
                                sp.dma_start(dst[:, :], d[name][ds(g, 1)].rearrange("a p n -> p (a n)"))\
                                    .then_inc(group_in, 16)
                            sp.dma_start(pick[:, :], d["token_of_row"][:, ds(g * P, P)]).then_inc(group_in, 16)
                        with sp.Fori(0, NB) as p:
                            page = sp.value_load(table[0:1, ds(seq * NPAGE + p, 1)], min_val=0,
                                                 max_val=d["pages_k"].shape[0] - 1)
                            if load < 4:
                                dst, src = pages[:, slot, ds(p * 384, 384)], d["pages_k"]
                            else:
                                dst, src = pages[:, slot, ds(p * P, P)], d["pages_v"]
                            sp.dma_start(dst, src[ds(page, 1)].rearrange("a p n -> p (a n)"))\
                                .then_inc(pages_in[slot], 16)

            @block.gpsimd
            def _(pool):
                pool.memset(q_dil[:, :, :], 0.0).then_inc(q_zero, 1)
                pool.memset(q_nsa[:, :], 0.0).then_inc(q_zero, 1)
                pool.wait_ge(q_zero, 2)
                with pool.Fori(0, 2) as g:
                    for e in range(2):
                        half = slice(e * HD, (e + 1) * HD)
                        for hp in range(4):
                            dst = q_dil[half, hp, :].rearrange("p (i h q) -> p i h q", i=4, q=S)[:, :, 2 * hp + e, :]
                            src = m.zs[half, QA + hp, ds(g * 16, 16)].rearrange("p (i q) -> p i q", q=S)
                            pool.tensor_copy(dst, src).then_inc(q_ready, 1)
                        for r in range(4):
                            dst = q_nsa[half, :].rearrange("p (i e r q) -> p i e r q", i=4, e=2, q=S)[:, :, e, r, :]
                            src = m.zs[half, QB + r, ds(g * 16, 16)].rearrange("p (i q) -> p i q", q=S)
                            pool.tensor_copy(dst, src).then_inc(q_ready, 1)
                    pool.wait_ge(new_full, g + 1)

            @block.scalar
            def _(act):
                with act.Fori(0, 2) as g:
                    for i in range(4):
                        rows = slice(32 * i, 32 * i + 32)

                        def take(k):
                            act.wait_ge(tile_full, g * 32 + (8 * i + k + 1))
                            dst = {0: s_dil[rows, 0:448], 2: s_slc[rows, 0:512], 4: s_slc[rows, 1024:1536],
                                   6: s_win[rows, 0:512]}[k]
                            act.copy(dst, ps[rows, 2 + k % 4, 0:dst.shape[-1]]).then_inc(tile_act, 1)

                        for kv in range(2):
                            turn = g * 8 + (2 * i + kv)
                            cmp.act_second(act, turn, kv)
                            if kv == 0:
                                take(0)
                            cmp.act_exp(act, turn)
                            if kv == 0:
                                if i > 0:
                                    act.wait_ge(tile_full, g * 32 + 8 * i)
                                cmp.act_small(act, turn, kv, kc[:, :])
                            else:
                                for k in (2, 4, 6):
                                    take(k)
                                cmp.act_small(act, turn, kv, vc[:, i, :])
                    act.wait_ge(new_full, g * 1 + 1)
                    act.copy(s_dil[:, NKEY_A:], ps[:, 2, 0:SN])
                    act.copy(s_slc[:, PAST:], ps[:, 2, SN:2 * SN])
                    act.copy(s_win[:, 512:], ps[:, 2, 2 * SN:3 * SN])
                    act.copy(gates[:, :], ps[:, 3, 0:24]).then_inc(new_out, 1)

                    def exp(n, which, scores, scale):
                        act.wait_ge(low_ready, g * 4 + (n + 1))
                        act.activation(scores[:, :], scores[:, :], ACT.Exp, bias=low(which), scale=scale,
                                       accum_out=total(which)).then_inc(exp_ready, 1)

                    def take_turn(b):
                        _, scores, blocks, dst = turns[b]
                        act.wait_ge(turn_full, g * NTURN + (b + 1))
                        if b == 6:
                            act.wait_ge(low_ready, g * 4 + 4)
                        part = P if blocks[-1] * P + P <= scores.shape[1] else scores.shape[1] - blocks[-1] * P
                        bank = ps[:, 6 + b % 2, :]
                        if scores is s_cmp:
                            act.copy(dst[0:NCMP_S, :], bank[0:NCMP_S, 0:P]).then_inc(turn_out, 1)
                            return
                        whole = len(blocks) - (part < P)
                        if whole:
                            c = act.copy(dst[:, blocks[0]:blocks[0] + whole, :],
                                         bank[:, 0:whole * P].rearrange("p (a b) -> p a b", b=P))
                        if part < P:
                            c = act.copy(dst[0:part, blocks[-1], :], bank[0:part, whole * P:(whole + 1) * P])
                        c.then_inc(turn_out, 1)

                    exp(0, C, s_cmp, SCALE)
                    exp(1, A, s_dil, -1.0)
                    take_turn(0)
                    act.wait_ge(imp_full, g * 1 + 1)
                    act.copy(importance[:, :], ps[:, 4, 0:NBLK]).then_inc(imp_out, 1)
                    take_turn(1)
                    exp(2, W, s_win, -1.0)
                    for b in range(2, 6):
                        take_turn(b)
                    exp(3, S_, s_slc, SCALE)
                    for b in range(6, NTURN):
                        take_turn(b)
                    act.wait_ge(so_full, g * 4 + 4)

            @block.tensor
            def _(pe):
                pe.wait_ge(const_in, 16 * 7)
                with pe.Fori(0, 2) as g:
                    pe.wait_ge(q_ready, g * 16 + 16)
                    for i in range(4):
                        slot, rows, cols = i % 2, slice(32 * i, 32 * i + 32), slice(32 * i, 32 * i + 32)
                        page = pages[:, slot, :].rearrange("p (n w) -> p n w", w=384)
                        rounds = g * 4 + (i // 2 + 1)

                        def chunks(kv):
                            v = page[:, :, kv * P:(kv + 1) * P].rearrange("p n (e s c) -> p e s n c", e=2, c=8)
                            return lambda s1: v[:, :, s1]

                        def room(k):
                            if k >= 4:
                                pe.wait_ge((tile_act, tile_dve)[k % 2], g * 16 + (4 * i + k // 2 - 1))
                            elif i > 0:
                                pe.wait_ge((tile_act, tile_dve)[k % 2], g * 16 + (4 * i + k // 2 - 1))

                        def dilated(k):
                            room(k)
                            for hp in range(4):
                                last = pe.matmul(ps[rows, 2 + k, 0:448], q_dil[:, hp, cols],
                                                 dil[:, slot, hp * NKEY_A + k * 448:hp * NKEY_A + k * 448 + 448],
                                                 start=(hp == 0), stop=(hp == 3))
                            last.then_inc(tile_full, 1)

                        pe.wait_ge(pages_in[slot], rounds * (16 * NB))
                        turn = g * 8 + 2 * i
                        cmp.pe_project(pe, 0, chunks(0))
                        pe.wait_ge(dil_in[slot], rounds * 16)
                        dilated(0)
                        dilated(1)
                        pe.wait_ge(cmp.hid_ready, turn + 1)
                        cmp.pe_project(pe, 1, chunks(1))
                        cmp.pe_small(pe, turn, 0)
                        for k in range(2, 6):
                            room(k)
                            pe.matmul(ps[rows, 2 + k % 4, :], q_nsa[:, cols], page[:, 4 * (k - 2):4 * (k - 1), 256:384],
                                      start=True, stop=True).then_inc(tile_full, 1)
                        room(6)
                        pe.wait_ge(win_in[slot], rounds * 16)
                        pe.matmul(ps[rows, 4, :], q_nsa[:, cols], win[:, slot, :], start=True, stop=True)\
                            .then_inc(tile_full, 1)
                        cmp.pe_small(pe, turn + 1, 1)
                        room(7)
                        pe.wait_ge(cmp.small_out, turn + 1)
                        pe.matmul(ps[rows, 5, 0:NCMP_S], q_nsa[:, cols], kc[:, :], start=True, stop=True)\
                            .then_inc(tile_full, 1)
                        pe.wait_ge(cmp.small_out, turn + 2)
                        pe.wait_ge(tile_act, g * 16 + 4 * (i + 1))
                        pe.wait_ge(tile_dve, g * 16 + 4 * (i + 1))
                        pe.sem_inc(slot_used, 1)
                    for hp in range(4):
                        pe.matmul(ps[:, 2, 0:SN], q_dil[:, hp, :], m.zs[:, KA + hp, :], start=(hp == 0), stop=(hp == 3))
                    pe.matmul(ps[:, 2, SN:2 * SN], q_nsa[:, :], m.zs[:, KS, :], start=True, stop=True)
                    pe.matmul(ps[:, 2, 2 * SN:3 * SN], q_nsa[:, :], m.zs[:, KW, :], start=True, stop=True)
                    pe.wait_ge(group_in, g * 64 + 64)
                    pe.matmul(ps[:, 3, 0:24], pick[:, :], m.gates[:, :], start=True, stop=True).then_inc(new_full, 1)

                    def turn_bank(b):
                        need, scores, blocks, _ = turns[b]
                        pe.wait_ge(prob_ready, g * 5 + need)
                        if b >= 2:
                            pe.wait_ge(turn_out, g * NTURN + (b - 1))
                        for c, k in enumerate(blocks):
                            n = min(P, scores.shape[1] - k * P)
                            last = pe.transpose(ps[0:n, 6 + b % 2, c * P:(c + 1) * P], scores[:, k * P:k * P + n],
                                                m.ident[:, :])
                        last.then_inc(turn_full, 1)

                    turn_bank(0)
                    pe.wait_ge(turn_out, g * NTURN + 1)
                    pe.matmul(ps[:, 4, 0:NBLK], t_cmp[0:NCMP_S, :], overlap[:, :], start=True, stop=True)\
                        .then_inc(imp_full, 1)
                    pe.wait_ge(imp_out, g * 1 + 1)
                    pe.matmul(ps[:, 5, 0:NBLK], same[:, :], importance[:, :], start=True, stop=True)\
                        .then_inc(points_full, 1)
                    for b in range(1, NTURN):
                        turn_bank(b)
                    pe.wait_ge(turn_out, g * NTURN + NTURN)
                    for i in range(4):
                        slot, c0 = i % 2, 32 * i
                        rounds = g * 4 + (i // 2 + 3)
                        out = ps[:, 2 + i % 2, :]
                        if i >= 2:
                            pe.wait_ge(so_out, g * 16 + 4 * (i - 1))
                        pe.wait_ge(dil_in[slot], rounds * 16)
                        for hp in range(4):
                            cols = slice(c0 + 8 * hp, c0 + 8 * hp + 8)
                            for k in range(7):
                                pe.matmul(out[:, 8 * hp:8 * hp + 8], dil[:, slot, k * 512 + hp * P:k * 512 + (hp + 1) * P],
                                          t_dil[:, k, cols], start=(k == 0), stop=False)
                            pe.matmul(out[:, 8 * hp:8 * hp + 8], m.vas[:, hp * P:(hp + 1) * P], t_dil[0:SN, 7, cols],
                                      start=False, stop=True)
                        pe.wait_ge(pages_in[slot], rounds * (16 * NB))
                        pe.wait_ge(win_in[slot], rounds * 16)
                        cols = slice(c0, c0 + 32)
                        out = out[:, 64:96]
                        pe.matmul(out, vc[:, i, :], t_cmpg[0:NCMP_S, cols], start=True, stop=False)
                        for k in range(NB):
                            pe.matmul(out, pages[:, slot, k * P:(k + 1) * P], t_slc[:, k, cols], start=False, stop=False)
                        pe.matmul(out, m.vbs[:, 0:P], t_slc[0:SN, NB, cols], start=False, stop=False)
                        for k in range(4):
                            pe.matmul(out, win[:, slot, k * P:(k + 1) * P], t_win[:, k, cols], start=False, stop=False)
                        pe.matmul(out, m.vbs[:, P:2 * P], t_win[0:SN, 4, cols], start=False, stop=True)\
                            .then_inc(so_full, 1)
                        pe.wait_ge(so_out, g * 16 + 4 * (i + 1))
                        pe.sem_inc(slot_used, 1)

            @block.vector
            def _(dve):
                step = Steps(dve, dve_step)
                dve.wait_ge(const_in, 16 * 7)
                with dve.Fori(0, 2) as g:
                    PER = 67
                    first, step.offset = step.n, g * PER
                    for i in range(4):
                        rows = slice(32 * i, 32 * i + 32)

                        def take(k):
                            dve.wait_ge(tile_full, g * 32 + (8 * i + k + 1))
                            dst = {1: s_dil[rows, 448:896], 3: s_slc[rows, 512:1024], 5: s_slc[rows, 1536:2048],
                                   7: s_cmp[rows, :]}[k]
                            dve.tensor_copy(dst, ps[rows, 2 + k % 4, 0:dst.shape[-1]]).then_inc(tile_dve, 1)

                        cmp.dve_inner(dve, step, g * 8 + 2 * i)
                        take(1)
                        cmp.dve_hidden(dve, step, g * 8 + 2 * i)
                        cmp.dve_inner(dve, step, g * 8 + 2 * i + 1)
                        take(3)
                        cmp.dve_hidden(dve, step, g * 8 + 2 * i + 1)
                        take(5)
                        take(7)
                    dve.wait_ge(tile_dve, g * 16 + 16)
                    step.done(dve.tensor_reduce(low(C), s_cmp[:, :], AX_X, ALU.max))
                    step.wait()
                    dve.tensor_scalar(low(C), low(C), -SCALE, None, ALU.mult).then_inc(low_ready, 1)
                    dve.wait_ge(group_in, g * 64 + 64)
                    dve.wait_ge(new_out, g * 1 + 1)
                    dve.wait_ge(tile_act, g * 16 + 16)
                    dve.sem_inc(begun, 1)
                    dve.tensor_tensor_reduce(s_dil[:, :], s_dil[:, :], mask_dil[:, :], -SCALE, 3e38, ALU.add,
                                             ALU.min, low(A)).then_inc(low_ready, 1)
                    step.done(dve.tensor_tensor(gates[:, :], gates[:, :], gate_pick[:, :], ALU.mult))
                    step.wait()
                    step.done(dve.tensor_reduce(gate3[:, :], gates[:, :].rearrange("p (b h) -> p b h", b=3),
                                                AX_X, ALU.add))
                    dve.wait_ge(exp_ready, g * 4 + 1)
                    step.done(dve.reciprocal(factor(C), total(C)))
                    step.wait()
                    dve.tensor_scalar(s_cmp[:, :], s_cmp[:, :], factor(C), None, ALU.mult).then_inc(prob_ready, 1)
                    dve.wait_ge(turn_full, g * NTURN + 1)
                    dve.tensor_scalar(s_cmp[:, :], s_cmp[:, :], gate3[:, 0:1], None, ALU.mult).then_inc(prob_ready, 1)
                    dve.wait_ge(exp_ready, g * 4 + 2)
                    step.done(dve.reciprocal(factor(A), total(A)))
                    step.wait()
                    dve.tensor_scalar(s_dil[:, :], s_dil[:, :], factor(A), None, ALU.mult).then_inc(prob_ready, 1)
                    dve.wait_ge(points_full, g * 1 + 1)
                    step.done(dve.tensor_tensor(points[:, :], ps[:, 5, 0:NBLK], forced[:, :], ALU.add))
                    step.wait()
                    other = points[:, :].unsqueeze(1).broadcast_to([P, NBLK, NBLK])
                    this = points[:, :].unsqueeze(2).broadcast_to([P, NBLK, NBLK])
                    step.done(dve.tensor_tensor(beats, other, this, ALU.is_gt))
                    step.done(dve.tensor_tensor(ties, other, this, ALU.is_equal))
                    step.wait()
                    step.done(dve.tensor_tensor(ties, ties, earlier[:, :].rearrange("p (j i) -> p j i", i=NBLK), ALU.mult))
                    step.wait()
                    step.done(dve.tensor_tensor(beats, beats, ties, ALU.add))
                    step.wait()
                    step.done(dve.tensor_reduce(drop[:, :], beats, AX_X, ALU.add))
                    step.wait()
                    step.done(dve.tensor_scalar(drop[:, :], drop[:, :], TOPK - 0.5, NEG, ALU.is_gt, ALU.mult))
                    dve.sem_inc(begun, 1)
                    dve.tensor_tensor_reduce(s_win[:, :], s_win[:, :], mask_win[:, :], -SCALE, 3e38, ALU.add,
                                             ALU.min, low(W)).then_inc(low_ready, 1)
                    step.done(dve.tensor_tensor(s_slc[:, PAST:], s_slc[:, PAST:], mask_new[:, :], ALU.add))
                    step.wait()
                    dve.sem_inc(group_used, 1)
                    past = s_slc[:, 0:PAST].rearrange("p (b t) -> p b t", t=64)
                    step.done(dve.tensor_tensor(past, past, drop[:, 0:32].unsqueeze(2).broadcast_to([P, 32, 64]),
                                                ALU.add))
                    step.wait()
                    step.done(dve.tensor_reduce(low(S_), s_slc[:, :], AX_X, ALU.max))
                    step.wait()
                    dve.wait_ge(exp_ready, g * 4 + 3)
                    step.done(dve.reciprocal(factor(W), total(W)))
                    step.wait()
                    step.done(dve.tensor_tensor(factor(W), factor(W), gate3[:, 2:3], ALU.mult))
                    step.wait()
                    dve.tensor_scalar(low(S_), low(S_), -SCALE, None, ALU.mult).then_inc(low_ready, 1)
                    dve.tensor_scalar(s_win[:, :], s_win[:, :], factor(W), None, ALU.mult).then_inc(prob_ready, 1)
                    dve.wait_ge(exp_ready, g * 4 + 4)
                    step.done(dve.reciprocal(factor(S_), total(S_)))
                    step.wait()
                    step.done(dve.tensor_tensor(factor(S_), factor(S_), gate3[:, 1:2], ALU.mult))
                    step.wait()
                    dve.tensor_scalar(s_slc[:, :], s_slc[:, :], factor(S_), None, ALU.mult).then_inc(prob_ready, 1)
                    for i in range(4):
                        dve.wait_ge(so_full, g * 4 + (i + 1))
                        bank = ps[:, 2 + i % 2, :]
                        col = g * 16 + (T + 4 * i)
                        for e in range(2):
                            half = slice(e * HD, (e + 1) * HD)
                            a = bank[half, 0:32].rearrange("p (h e q) -> p h e q", e=2, q=S)[:, :, e, :]
                            b = bank[half, 64 + 16 * e:80 + 16 * e].rearrange("p (r q) -> p r q", q=S)
                            dve.tensor_copy(m.oa[half, 0:4, ds(col, S)], a).then_inc(so_out, 1)
                            dve.tensor_copy(m.oa[half, 4:8, ds(col, S)], b).then_inc(so_out, 1)
                    assert step.n - first == PER
                step.offset = None




def finish(nc, d, m, sem):
    with ExitStack() as mine:
        def sb(name, shape, dt=F32):
            return mine.enter_context(nc.sbuf_tensor(name, shape, dt))

        ps = m.ps
        x, h = sb("fx", [P, KD, NT]), sb("fh", [P, KD, NT])
        ring = sb("ring", [P, RING, KD * P])
        mean, root, scratch = sb("fmean", [P, NT]), sb("froot", [P, NT]), sb("fscratch", [P, NT])
        merged = sb("merged", [P, KD, NT])
        q_mem, o_mem = merged[:, 0:MH, :], merged[:, MH:2 * MH, :]
        wide = sb("wide", [P, 2 * NSEQ * 1024])
        km = wide[:, 0:NSEQ * 1024].rearrange("p (n h t) -> p n h t", n=NSEQ, h=MH)
        vm = wide[:, NSEQ * 1024:].rearrange("p (n k f) -> p n k f", n=NSEQ, k=2)
        act_a = wide[:, 0:KF * NT].rearrange("p (f t) -> p f t", f=KF)
        prob = sb("m_prob", [P, QT, MTOK])
        prob_t = sb("m_prob_t", [P, 2, T])
        low, total = sb("m_low", [P, QT]), sb("m_total", [P, QT])
        CW = 2 + T + NSEQ * 6
        u, c = sb("u", [P, 2, CW]), sb("c", [P, 2, CW])
        e_a, e_b = sb("e_a", [P, CW]), sb("e_b", [P, NT])
        w_conv, past = sb("w_conv_sb", [P, 2 * KF, 4]), sb("ffn_past_sb", [P, 2 * KF, 16])
        last_u = sb("last_u", [P, 2 * KF, 18])
        C0 = CW - 2

        T_O, T_Q, T_M, T_UP, T_DOWN = 32, 40, 44, 52, 96
        N_O, N_Q, N_M, N_UP, N_DOWN, N_ALL = 24, 32, 36, 40, 84, 108

        x_in, past_in, kv_in = sem("fx_in"), sem("past_in"), sem("kv_in")
        chunk_in = [sem(f"chunk_in{i}") for i in range(RING)]
        acc_full, acc_out = sem("acc_full"), [sem("acc_out0"), sem("acc_out1")]
        down_part = sem("down_part")
        x_ready, squared, sum_full = sem("x_ready"), sem("fsquared"), sem("fsum_full")
        v_ready, y_ready, h_ready = sem("fmean_ready"), sem("froot_ready"), sem("fh_ready")
        gate_ready, merged_ready = sem("fgate_ready"), sem("merged_ready")
        q_ready, q_square = sem("q_mem_ready"), sem("q_square")
        ms_full, ms_low, ms_exp, ms_prob = sem("ms_full"), sem("ms_low"), sem("ms_exp"), sem("ms_prob")
        mt_full, mt_out, mo_full, mo_out = sem("mt_full"), sem("mt_out"), sem("mo_full"), sem("mo_out")
        past_put, rows_kept, conv_done = sem("past_put"), sem("rows_kept"), sem("conv_done")
        silu_exp, a_ready, y_done = sem("silu_exp"), sem("a_ready"), sem("y_done")
        edge_zero = sem("edge_zero")
        dve_step = sem("finish_dve_step")
        stored = sem("finish_stored")

        def pair(t):
            return ps[:, 2 * (t % 2):2 * (t % 2) + 2, 0:HALF]

        with nc.Block() as block:
            @block.sync
            def _(sp):
                def load(chunk, slot):
                    src = d["w_close"][ds(chunk, 1)].rearrange("a p k n -> p (a k n)")
                    sp.dma_start(ring[:, slot, :], src).then_inc(chunk_in[slot], 16)

                sp.dma_start(x[:, :, :], d["x"]).then_inc(x_in, 16)
                for i in range(RING):
                    load(i, i)
                sp.dma_start(w_conv[:, :, :], d["w_conv"]).then_inc(past_in, 16)
                sp.dma_start(past[:, :, :], d["ffn_past"].rearrange("p f n r -> p f (n r)")).then_inc(past_in, 16)
                with sp.Fori(0, 2) as i:
                    for n in range(12):
                        sp.wait_ge(acc_full, i * 16 + (4 * (n // 3) + (1, 2, 4)[n % 3]))
                        load(i * 12 + (n + RING), n % 4)
                with sp.Fori(0, 2) as i:
                    for n in range(4):
                        sp.wait_ge(acc_full, i * 4 + (T_O + n + 1))
                        load(i * 4 + (N_O + n + RING), n)
                for n in range(4):
                    sp.wait_ge(acc_full, T_Q + n + 1)
                    load(N_Q + n + RING, n)
                for n in range(4):
                    sp.wait_ge(acc_full, T_M + 2 * n + 2)
                    load(N_M + n + RING, n)
                with sp.Fori(0, KF // 2) as i:
                    for n in range(4):
                        sp.wait_ge(acc_full, i * 4 + (T_UP + n + 1))
                        load(i * 4 + (N_UP + n + RING), n)
                for n in range(N_ALL - N_DOWN - RING):
                    if n % 3 == 2:
                        sp.wait_ge(acc_full, T_DOWN + n // 3 + 1)
                    else:
                        sp.wait_ge(down_part, n // 3 * 2 + n % 3 + 1)
                    load(N_DOWN + n + RING, n % 4)
                sp.wait_ge(rows_kept, 2 * KF)
                sp.dma_start(d["o_conv"], last_u[:, :, :]).then_inc(stored, 16)
                sp.wait_ge(y_done, KD)
                sp.dma_start(d["o_y"], x[:, :, :]).then_inc(stored, 16)
                sp.wait_ge(stored, 32)

            @block.gpsimd
            def _(pool):
                for p in range(2):
                    pool.memset(u[:, p, 0:2], 0.0).then_inc(edge_zero, 1)
                pool.wait_ge(past_in, 32)
                with pool.Fori(0, KF) as f:
                    for p in range(2):
                        heads = u[:, p, 2 + T:].rearrange("p (n s) -> p n s", s=6)
                        src = one(past, f + p * KF, slice(0, 16)).rearrange("p (n r) -> p n r", r=2)
                        pool.tensor_copy(heads[:, :, 0:2], src).then_inc(past_put, 1)
                    for p in range(2):
                        pool.wait_ge(acc_out[p], f * 1 + (T_UP // 2 + 1))
                        dst = one(last_u, f + p * KF, slice(0, 18))
                        heads = u[:, p, 2 + T:].rearrange("p (n s) -> p n s", s=6)
                        pool.tensor_copy(dst[:, 0:2], u[:, p, T:T + 2])
                        pool.tensor_copy(dst[:, 2:18].rearrange("p (n r) -> p n r", r=2), heads[:, :, 4:6])\
                            .then_inc(rows_kept, 1)
                    pool.wait_ge(conv_done, f * 2 + 2)

            @block.scalar
            def _(act):
                act.dma_start(km.rearrange("p n h t -> p n (h t)"), d["past_km"].rearrange("n p h t -> p n (h t)"))\
                    .then_inc(kv_in, 16)
                act.dma_start(vm.rearrange("p n k f -> p n (k f)"), d["past_vm"].rearrange("n p k f -> p n (k f)"))\
                    .then_inc(kv_in, 16)

                def norm(n, ready, first):
                    for k in range(KD):
                        if ready is not None:
                            act.wait_ge(ready, first + k + 1)
                        act.activation(h[:, k, :], x[:, k, :], ACT.Square).then_inc(squared, 1)
                    reciprocal_root(None, act, "act", mean[:, :], root[:, :], None, v_ready, y_ready, n)

                act.wait_ge(x_in, 16)
                norm(0, None, 0)
                with act.Fori(0, 2) as i:
                    for n in range(4):
                        for b, e in ((0, e_a), (1, e_b)):
                            act.wait_ge(acc_full, i * 16 + (4 * n + b + 1))
                            if n > 0:
                                act.wait_ge(merged_ready, i * 4 + n)
                            act.activation(halves(e[:, 0:NT]), pair(b), ACT.Exp, scale=-1.0).then_inc(acc_out[b], 1)
                    act.wait_ge(merged_ready, i * 4 + 4)
                act.wait_ge(acc_full, T_Q)
                norm(1, x_ready, 0)
                for j in range(MH):
                    act.wait_ge(acc_full, T_Q + j + 1)
                    act.copy(halves(q_mem[:, j, :]), pair(j))
                    act.activation(halves(o_mem[:, j, :]), pair(j), ACT.Square).then_inc(acc_out[j % 2], 1)
                for j in range(MH):
                    reciprocal_root(None, act, "act", mean[:, :], root[:, :], None, v_ready, y_ready, 2 + j)

                def exps(first, n):
                    act.wait_ge(ms_low, first // 4 + 1)
                    for i in range(n):
                        last = act.activation(prob[:, i, :], prob[:, i, :] if n == 1 else ps[:, 4 + i // 2,
                                              (i % 2) * MTOK:(i % 2 + 1) * MTOK], ACT.Exp, bias=low[:, i:i + 1],
                                              scale=MSCALE, accum_out=total[:, i:i + 1])
                    last.then_inc(ms_exp, 1)

                for j in range(MH):
                    if j >= 1:
                        act.wait_ge(mt_full, j)
                    exps(4 * j, 4)
                    act.wait_ge(mt_full, j + 1)
                    if j >= 1:
                        act.wait_ge(mo_full, j)
                    act.copy(prob_t[:, 0, :], ps[:, 6, :])
                    act.copy(prob_t[:, 1, :], ps[:, 7, :]).then_inc(mt_out, 1)
                    act.wait_ge(mo_full, j + 1)
                    act.copy(o_mem[:, j, 0:T], ps[:, j % 2, :]).then_inc(mo_out, 1)
                act.wait_ge(ms_full, MH + 1)
                act.copy(prob_t[:, :, 0:P], ps[:, 4, 0:2 * P].rearrange("p (a b) -> p a b", b=P)).then_inc(mt_out, 1)
                act.wait_ge(mt_full, MH + 1)
                act.copy(prob[:, 0, :], ps[:, 6, 0:MTOK]).then_inc(mt_out, 1)
                exps(16, 1)
                act.wait_ge(mt_full, MH + 2)
                act.copy(prob_t[:, :, 0:P], ps[:, 7, 0:MTOK].rearrange("p (a b) -> p a b", b=P)).then_inc(mt_out, 1)
                act.wait_ge(mo_full, MH + 1)
                out = ps[:, 4, 0:P].rearrange("p (n h q) -> p n h q", n=NSEQ, h=MH)
                for j in range(MH):
                    last = act.copy(o_mem[:, j, T:NT].rearrange("p (n q) -> p n q", q=S), out[:, :, j, :])
                last.then_inc(mo_out, 1)
                norm(6, x_ready, KD)
                act.wait_ge(edge_zero, 2)
                with act.Fori(0, KF) as f:
                    for p in range(2):
                        act.wait_ge(acc_full, f * 2 + (T_UP + p + 1))
                        act.wait_ge(past_put, f * 2 + (p + 1))
                        act.copy(u[:, p, 2:2 + HALF], ps[:, 2 * p, 0:HALF])
                        act.copy(u[:, p, 2 + HALF:2 + T], ps[:, 2 * p + 1, 0:T - HALF])
                        act.copy(u[:, p, 2 + T:].rearrange("p (n s) -> p n s", s=6)[:, :, 2:6],
                                 ps[:, 2 * p + 1, T - HALF:HALF].rearrange("p (n s) -> p n s", s=S))\
                            .then_inc(acc_out[p], 1)
                    act.wait_ge(conv_done, f * 2 + 1)
                    act.wait_ge(a_ready, f + 1)
                    act.activation(e_a[:, 0:C0], c[:, 0, 0:C0], ACT.Exp, scale=-1.0).then_inc(silu_exp, 1)
                    act.wait_ge(conv_done, f * 2 + 2)
                    act.wait_ge(rows_kept, f * 2 + 2)

            @block.tensor
            def _(pe):
                def sums(rhs, first_bank=4, k_tiles=KD, step=None):
                    for k in range(k_tiles):
                        if step is not None:
                            pe.wait_ge(squared, step + k + 1)
                        for a in range(2):
                            last = pe.matmul(ps[:, first_bank + a, 0:HALF], m.ones[:, :],
                                             rhs(k)[:, a * HALF:(a + 1) * HALF], start=(k == 0), stop=(k == k_tiles - 1))
                    last.then_inc(sum_full, 1)

                def tile(p, parts, rhs):
                    k, total_k = 0, sum(n for _, _, n in parts)
                    for slot, w0, n in parts:
                        for w in range(n):
                            for a in range(2):
                                last = pe.matmul(ps[:, 2 * p + a, 0:HALF], ring[:, slot, (w0 + w) * P:(w0 + w + 1) * P],
                                                 rhs(k)[:, a * HALF:(a + 1) * HALF],
                                                 start=(k == 0), stop=(k == total_k - 1))
                            k += 1
                        if k < total_k:
                            last.then_inc(down_part, 1)
                    last.then_inc(acc_full, 1)

                sums(lambda k: h[:, k, :], step=0)
                pe.wait_ge(h_ready, KD)
                with pe.Fori(0, 2) as i:
                    for n in range(4):
                        for b in range(4):
                            chunk, p = 3 * n + min(b, 2), b % 2
                            if b < 3:
                                pe.wait_ge(chunk_in[chunk % 4], (i * 3 + (chunk // 4 + 1)) * 16)
                            if n + b // 2 > 0:
                                pe.wait_ge(acc_out[p], i * 8 + (2 * n + b // 2))
                            if b < 2:
                                tile(p, [(chunk % 4, 0, 8)], lambda k: h[:, k, :])
                            else:
                                tile(p, [(chunk % 4, 4 * (b - 2), 4)], lambda k: m.oa[:, 4 * (b - 2) + k, :])
                    for p in range(2):
                        pe.wait_ge(acc_out[p], i * 8 + 8)
                pe.wait_ge(merged_ready, KD)
                with pe.Fori(0, 2) as i:
                    for n in range(4):
                        pe.wait_ge(chunk_in[n], (i + (N_O // 4 + 1)) * 16)
                        pe.wait_ge(acc_out[n % 2], i * 2 + (T_O // 2 + n // 2))
                        tile(n % 2, [(n, 0, 8)], lambda k: merged[:, k, :])
                sums(lambda k: h[:, k, :], step=KD)
                for n in range(MH):
                    pe.wait_ge(h_ready, 2 * KD)
                    pe.wait_ge(chunk_in[n], (N_Q // 4 + 1) * 16)
                    pe.wait_ge(acc_out[n % 2], (T_Q + n) // 2)
                    tile(n % 2, [(n, 0, 8)], lambda k: h[:, k, :])
                for j in range(MH):
                    pe.wait_ge(acc_out[j % 2], (T_Q + j) // 2 + 1)
                    pe.wait_ge(v_ready, 2 + j)
                    sums(lambda k: o_mem[:, j, :], k_tiles=1)
                for j in range(MH):
                    pe.wait_ge(q_ready, MH)
                    if j >= 1:
                        pe.wait_ge(ms_exp, j)
                    for qt in range(QT):
                        last = pe.matmul(ps[:, 4 + qt // 2, (qt % 2) * MTOK:(qt % 2 + 1) * MTOK],
                                         q_mem[:, j, qt * P:(qt + 1) * P], m.mk[:, j, :], start=True, stop=True)
                    last.then_inc(ms_full, 1)
                    pe.wait_ge(ms_prob, j + 1)
                    if j >= 1:
                        pe.wait_ge(mt_out, j)
                    for k in range(2):
                        for qt in range(QT):
                            last = pe.transpose(ps[:, 6 + k, qt * P:(qt + 1) * P], prob[:, qt, k * P:(k + 1) * P],
                                                m.ident[:, :])
                    last.then_inc(mt_full, 1)
                    pe.wait_ge(mt_out, j + 1)
                    if j >= 2:
                        pe.wait_ge(mo_out, j - 1)
                    for k in range(2):
                        last = pe.matmul(ps[:, j % 2, :], m.mv[:, k, j * P:(j + 1) * P], prob_t[:, k, :],
                                         start=(k == 0), stop=(k == 1))
                    last.then_inc(mo_full, 1)
                pe.wait_ge(kv_in, 32)
                pe.wait_ge(ms_exp, MH)
                for k in range(2):
                    for n in range(NSEQ):
                        for j in range(MH):
                            at = k * P + n * 16 + j * 4
                            last = pe.matmul(ps[:, 4, at:at + 4], km[:, n, j, k * P:(k + 1) * P],
                                             q_mem[:, j, T + 4 * n:T + 4 * n + 4], start=True, stop=True)
                last.then_inc(ms_full, 1)
                pe.wait_ge(mt_out, MH + 1)
                for k in range(2):
                    last = pe.transpose(ps[:, 6, k * P:(k + 1) * P], prob_t[:, k, 0:P], m.ident[:, :])
                last.then_inc(mt_full, 1)
                pe.wait_ge(ms_prob, MH + 1)
                for k in range(2):
                    last = pe.transpose(ps[:, 7, k * P:(k + 1) * P], prob[:, 0, k * P:(k + 1) * P], m.ident[:, :])
                last.then_inc(mt_full, 1)
                pe.wait_ge(mt_out, MH + 3)
                for n in range(NSEQ):
                    for j in range(MH):
                        at = n * 16 + j * 4
                        for k in range(2):
                            last = pe.matmul(ps[:, 4, at:at + 4], vm[:, n, k, j * P:(j + 1) * P],
                                             prob_t[:, k, at:at + 4], start=(k == 0), stop=(k == 1))
                last.then_inc(mo_full, 1)
                pe.wait_ge(mo_out, MH + 1)
                for n in range(KD):
                    pe.wait_ge(chunk_in[n // 2], (N_M // 4 + 1) * 16)
                    pe.wait_ge(acc_out[n % 2], (T_M + n) // 2)
                    tile(n % 2, [(n // 2, 4 * (n % 2), 4)], lambda k: o_mem[:, k, :])
                sums(lambda k: h[:, k, :], step=2 * KD)
                pe.wait_ge(h_ready, 3 * KD)
                with pe.Fori(0, KF // 2) as i:
                    for n in range(4):
                        pe.wait_ge(chunk_in[n], (i + (N_UP // 4 + 1)) * 16)
                        pe.wait_ge(acc_out[n % 2], i * 2 + (T_UP // 2 + n // 2))
                        tile(n % 2, [(n, 0, 8)], lambda k: h[:, k, :])
                pe.wait_ge(a_ready, KF + 1)
                with pe.Fori(0, 2) as i:
                    for n in range(4):
                        for b in range(3):
                            chunk = 3 * n + b
                            pe.wait_ge(chunk_in[chunk % 4], (i * 3 + (N_DOWN // 4 + chunk // 4 + 1)) * 16)
                        pe.wait_ge(acc_out[n % 2], i * 2 + (T_DOWN // 2 + n // 2))
                        tile(n % 2, [((3 * n + b) % 4, 0, 8 if b < 2 else KF - 16) for b in range(3)],
                             lambda k: act_a[:, k, :])

            @block.vector
            def _(dve):
                step = Steps(dve, dve_step)

                def root_of(n, divisor):
                    dve.wait_ge(sum_full, n + 1)
                    dve.tensor_scalar(halves(mean[:, :]), ps[:, 4:6, 0:HALF], 1.0 / divisor, EPS, ALU.mult, ALU.add)\
                        .then_inc(v_ready, 1)
                    dve.wait_ge(v_ready, n + 1)
                    reciprocal_root(dve, None, "dve", mean[:, :], root[:, :], scratch[:, :], v_ready, y_ready, n, step)

                def norm(n, which, model):
                    root_of(n, D)
                    for k in range(KD):
                        dve.scalar_tensor_tensor(out=h[:, k, :], in0=x[:, k, :],
                                                 scalar=m.g_model[:, model * KD + k:model * KD + k + 1],
                                                 in1=root[:, :], op0=ALU.mult, op1=ALU.mult).then_inc(h_ready, 1)
                    dve.wait_ge(h_ready, (which + 1) * KD)

                def add_to_x(k, full, t):
                    dve.wait_ge(acc_full, full)
                    return dve.tensor_tensor(halves(k), halves(k), pair(t), ALU.add)

                dve.wait_ge(x_in, 16)
                norm(0, 0, 0)
                with dve.Fori(0, 2) as i:
                    PER = 4 * 5
                    first, step.offset = step.n, i * PER
                    for n in range(4):
                        for b, e in ((0, e_a), (1, e_b)):
                            dve.wait_ge(acc_out[b], i * 8 + (2 * n + 1))
                            step.done(dve.tensor_scalar(e[:, 0:NT], e[:, 0:NT], 1.0, None, ALU.add))
                            step.wait()
                            step.done(dve.reciprocal(e[:, 0:NT], e[:, 0:NT]))
                            step.wait()
                        dst = one(merged, i * 4 + n, slice(0, NT))
                        for b, e, to in ((0, e_a[:, 0:NT], dst), (1, e_b[:, :], e_b[:, :])):
                            dve.wait_ge(acc_full, i * 16 + (4 * n + b + 3))
                            dve.tensor_tensor(halves(to), pair(b), halves(e), ALU.mult).then_inc(acc_out[b], 1)
                        dve.wait_ge(acc_out[0], i * 8 + (2 * n + 2))
                        dve.wait_ge(acc_out[1], i * 8 + (2 * n + 2))
                        step.done(dve.tensor_tensor(dst, dst, e_b[:, :], ALU.add))
                        step.wait()
                        dve.sem_inc(merged_ready, 1)
                    assert step.n - first == PER
                    step.n = first + 2 * PER
                step.offset = None
                with dve.Fori(0, 2) as i:
                    for n in range(4):
                        add_to_x(one(x, i * 4 + n, slice(0, NT)), i * 4 + (T_O + n + 1), n).then_inc(acc_out[n % 2], 1)
                        dve.wait_ge(acc_out[n % 2], i * 2 + (T_O // 2 + n // 2 + 1))
                        dve.sem_inc(x_ready, 1)
                norm(1, 1, 2)
                for j in range(MH):
                    root_of(2 + j, MHD)
                    dve.wait_ge(acc_out[j % 2], (T_Q + j) // 2 + 1)
                    dve.scalar_tensor_tensor(out=q_mem[:, j, :], in0=q_mem[:, j, :], scalar=m.g_memh[:, 1:2],
                                             in1=root[:, :], op0=ALU.mult, op1=ALU.mult).then_inc(q_ready, 1)
                    dve.wait_ge(q_ready, j + 1)

                def softmax(j, n):
                    if j >= 1:
                        dve.wait_ge(ms_prob, j)
                    src = ps[:, 4:6, :].rearrange("p a (b k) -> p a b k", b=2) if n == 4 else prob[:, 0, :]
                    dst = low[:, 0:n].rearrange("p (a b) -> p a b", b=2) if n == 4 else low[:, 0:1]
                    step.done(dve.tensor_reduce(dst, src, AX_X, ALU.max))
                    step.wait()
                    dve.tensor_scalar(low[:, 0:n], low[:, 0:n], -MSCALE, None, ALU.mult).then_inc(ms_low, 1)
                    dve.wait_ge(ms_exp, j + 1)
                    step.done(dve.reciprocal(total[:, 0:n], total[:, 0:n]))
                    step.wait()
                    for i in range(n):
                        last = dve.tensor_scalar(prob[:, i, :], prob[:, i, :], total[:, i:i + 1], None, ALU.mult)
                    last.then_inc(ms_prob, 1)

                for j in range(MH):
                    dve.wait_ge(ms_full, j + 1)
                    softmax(j, 4)
                dve.wait_ge(mt_out, MH + 2)
                softmax(MH, 1)
                for n in range(KD):
                    add_to_x(x[:, n, :], T_M + n + 1, n).then_inc(acc_out[n % 2], 1)
                    dve.wait_ge(acc_out[n % 2], (T_M + n) // 2 + 1)
                    dve.sem_inc(x_ready, 1)
                norm(6, 2, 3)
                dve.wait_ge(past_in, 32)
                dve.sem_inc(a_ready, 1)
                with dve.Fori(0, KF) as f:
                    PER = 8
                    first, step.offset = step.n, f * PER
                    for p in range(2):
                        w = one(w_conv, f + p * KF, slice(0, 4))
                        cc = c[:, p, 0:C0]
                        dve.wait_ge(acc_out[p], f + (T_UP // 2 + 1))
                        dve.wait_ge(past_put, f * 2 + (p + 1))
                        step.done(dve.tensor_scalar(cc, u[:, p, 0:C0], w[:, 0:1], w[:, 3:4], ALU.mult, ALU.add))
                        step.wait()
                        step.done(dve.scalar_tensor_tensor(out=cc, in0=u[:, p, 1:1 + C0], scalar=w[:, 1:2], in1=cc,
                                                           op0=ALU.mult, op1=ALU.add))
                        step.wait()
                        dve.scalar_tensor_tensor(out=cc, in0=u[:, p, 2:2 + C0], scalar=w[:, 2:3], in1=cc,
                                                 op0=ALU.mult, op1=ALU.add).then_inc(conv_done, 1)
                    dve.wait_ge(conv_done, f * 2 + 2)
                    dve.wait_ge(silu_exp, f + 1)
                    e = e_a[:, 0:C0]
                    step.done(dve.tensor_scalar(e, e, 1.0, None, ALU.add))
                    step.wait()
                    step.done(dve.reciprocal(e, e))
                    step.wait()
                    step.done(dve.tensor_tensor(e, e, c[:, 0, 0:C0], ALU.mult))
                    step.wait()
                    a = one(act_a, f, slice(0, NT))
                    step.done(dve.tensor_tensor(a[:, 0:T], e[:, 0:T], c[:, 1, 0:T], ALU.mult))
                    of_seq = lambda v: v[:, 2 + T:2 + T + 48].rearrange("p (n s) -> p n s", s=6)[:, :, 0:S]
                    dve.tensor_tensor(a[:, T:NT].rearrange("p (n q) -> p n q", q=S), of_seq(e_a[:, :]),
                                      of_seq(c[:, 1, :]), ALU.mult).then_inc(a_ready, 1)
                    dve.wait_ge(a_ready, f + 2)
                    assert step.n - first == PER
                step.offset = None
                for n in range(KD):
                    add_to_x(x[:, n, :], T_DOWN + n + 1, n).then_inc(acc_out[n % 2], 1)
                    dve.wait_ge(acc_out[n % 2], (T_DOWN + n) // 2 + 1)
                    dve.sem_inc(y_done, 1)




def program(nc, d):
    with ExitStack() as ctx:
        def sem(name):
            return ctx.enter_context(nc.semaphore(name))

        def sb(name, shape, dt=F32):
            return ctx.enter_context(nc.sbuf_tensor(name, shape, dt))

        class Shared:
            pass

        m = Shared()
        m.ps = ctx.enter_context(nc.psum_tensor("ps", [P, 8, 512], F32))
        m.oa, m.ob = (lambda o: (o, o))(sb("attended", [P, 8, NT]))
        m.mk, m.mv = sb("mk", [P, MH, MTOK]), sb("mv", [P, 2, 512])
        m.ones, m.ident = sb("ones_sb", [P, P]), sb("ident_sb", [P, P])
        m.cmp_bias = sb("cmp_bias", [P, 2])
        m.g_model, m.g_memh = sb("g_model_sb", [P, 4 * KD]), sb("g_memh_sb", [P, 2])
        m.zs, m.vas, m.vbs, m.gates = sb("zs", [P, NTILE, SN]), sb("vas", [SN, 512]), sb("vbs", [SN, 256]), \
            sb("gates_s", [SN, 24])
        with ExitStack() as tokens:
            m.z = tokens.enter_context(nc.sbuf_tensor("z", [P, NTILE, NT], F32))
            m.va = tokens.enter_context(nc.sbuf_tensor("va", [P, QT + 1, 512], F32))
            m.vb = tokens.enter_context(nc.sbuf_tensor("vb", [P, QT + 1, 256], F32))
            m.gate = tokens.enter_context(nc.sbuf_tensor("gate", [P, QT + 1, 24], F32))
            project(nc, d, m, sem)
            attend_prompt(nc, d, m, sem)
        attend_sample(nc, d, m, sem)
        finish(nc, d, m, sem)


def kernel(**inputs):
    import concourse.bacc as bacc
    from concourse.bass_utils import run_bass_kernel_spmd

    nc = bacc.Bacc("TRN2", target_bir_lowering=False, num_devices=1)
    laid = lay_out(**{k: np.asarray(v) for k, v in inputs.items()})
    arrays = {"in_" + k: v for k, v in laid.items()}
    d = {k: nc.dram_tensor("in_" + k, v.shape, mybir.dt.from_np(v.dtype), kind="ExternalInput").ap()
         for k, v in laid.items()}
    d |= {k: nc.dram_tensor(k, s, F32, kind="ExternalOutput").ap() for k, s in OUTS.items()}
    program(nc, d)
    r = run_bass_kernel_spmd(nc, [arrays], core_ids=[0])
    return lay_back({k: np.asarray(r.results[0][k]) for k in OUTS})
```

```python
from contextlib import ExitStack

import numpy as np

import concourse.bass as bass
from concourse import mybir

F32 = mybir.dt.float32
I32 = mybir.dt.int32
ALU = mybir.AluOpType
ACT = mybir.ActivationFunctionType
AX_X = mybir.AxisListType.X
ds = bass.ds

P = 128
D = 1024
KD = D // P
T = 512
QT = T // P
NSEQ, S = 8, 4
SN = NSEQ * S
NT = T + SN
HALF = NT // 2
PAST, PAGE = 2048, 128
NPAGE = PAST // PAGE
HD = 64
EPS = 1e-6
NEG = -1e30
SCALE = HD ** -0.5
MTOK, MH, MHD = 256, 4, 128
MSCALE = MHD ** -0.5
FF = 2816
KF = FF // P
NTILE = 16
QA, KA, QB, KC, KS, KW, VC = 0, 4, 8, 12, 13, 14, 15
VCOL = 512 + 128 + 128 + 24
NKEY_A = 896
NCMP_P, NCMP_S = 31, 127
NBLK, TOPK = 33, 16
RING = 4

KEYS_A = np.array([t for t in range(PAST) if t % 16 < S or t >= PAST - 512])
assert len(KEYS_A) == NKEY_A


def rope_tables():
    pos = np.concatenate([np.arange(T), np.tile(PAST + np.arange(S), NSEQ)]).astype(np.float32)
    inv = (np.float32(500000.0) ** (-np.arange(8, dtype=np.float32) / np.float32(8))).astype(np.float32)
    ang = pos[:, None] * inv[None, :]
    cos, sin = np.ones((P, NT), np.float32), np.zeros((P, NT), np.float32)
    for p in range(P):
        if p % HD < 16:
            cos[p], sin[p] = np.cos(ang[:, p % 8]), np.sin(ang[:, p % 8])
    return cos, sin


def rotation():
    r = np.zeros((P, P), np.float32)
    for m in range(P):
        if m % HD < 8:
            r[m + 8, m] = -1.0
        elif m % HD < 16:
            r[m - 8, m] = 1.0
    return r


def multiplicity(dist):
    n = ((dist >= 0) & (dist <= 128)).astype(int) + ((dist >= 0) & (dist % 4 == 0) & (dist <= 512)) \
        + ((dist >= 0) & (dist % 16 == 0) & (dist <= 2048))
    return np.where(n > 0, np.log(np.maximum(n, 1).astype(np.float64)) / SCALE, NEG).astype(np.float32)


def constants():
    q, k = np.arange(P)[:, None], np.arange(P)[None, :]
    c = {}
    c["ident"] = np.eye(P, dtype=np.float32)
    c["ones"] = np.ones((P, P), np.float32)
    c["head_ones"] = (q // HD == k // HD).astype(np.float32)
    c["rot"] = rotation()
    c["cos"], c["sin"] = rope_tables()
    dist = np.concatenate([P * b + q - k for b in (3, 2, 1, 0)], 1)
    c["mask_dil"] = multiplicity(dist)
    c["mask_causal"] = np.where(dist >= 0, 0.0, NEG).astype(np.float32)
    end = 16 * np.arange(NCMP_P) + 31
    tok = np.arange(T)
    seen = (end[None, :] <= tok[:, None])
    seen[:31, 0] = True
    c["mask_cmp"] = np.where(seen, 0.0, NEG).astype(np.float32).reshape(QT, P, NCMP_P).transpose(1, 0, 2).reshape(P, -1)
    c["cmp_live"] = np.ascontiguousarray((tok >= 31).astype(np.float32).reshape(QT, P).T)
    rows = np.arange(P)
    seq, qs = rows // 32, rows % 4
    new_seq, new_q = np.arange(SN) // S, np.arange(SN) % S
    a, w, b = [], [], []
    for g in range(2):
        own = (new_seq[None, :] == 4 * g + seq[:, None]) & (new_q[None, :] <= qs[:, None])
        dn = np.where(own, qs[:, None] - new_q[None, :], -1)
        a.append(np.concatenate([multiplicity(PAST + qs[:, None] - KEYS_A[None, :]), multiplicity(dn)], 1))
        dw = PAST + qs[:, None] - (PAST - 512 + np.arange(512))[None, :]
        w.append(np.concatenate([np.where(dw < 512, 0.0, NEG), np.where(own, 0.0, NEG)], 1))
        b.append(np.where(own, 0.0, NEG))
    c["mask_sdil"] = np.stack(a).astype(np.float32)
    c["mask_swin"] = np.stack(w).astype(np.float32)
    c["mask_snew"] = np.stack(b).astype(np.float32)
    j = np.arange(NBLK)
    cs = 16 * np.arange(NCMP_S)
    c["overlap"] = ((cs[:, None] <= 64 * j + 63) & (cs[:, None] + 31 >= 64 * j)).astype(np.float32)
    same = (seq[:, None] == seq[None, :]) & (qs[:, None] == qs[None, :]) & ((rows // 16)[:, None] == (rows // 16)[None, :])
    c["same_query"] = same.astype(np.float32)
    c["forced"] = np.broadcast_to(np.where((j == 0) | (j >= NBLK - 2), 1e30, 0.0), (P, NBLK)).astype(np.float32)
    c["earlier"] = np.broadcast_to((j[None, :] < j[:, None]).astype(np.float32).reshape(-1), (P, NBLK * NBLK)).astype(np.float32)
    pick = np.zeros((2, SN, P), np.float32)
    for g in range(2):
        pick[g, 4 * (4 * g + seq) + qs, rows] = 1.0
    c["token_of_row"] = pick.transpose(1, 0, 2).reshape(SN, 2 * P)
    je = (rows % 16 // 4) * 2 + rows % 32 // 16
    c["gate_of_row"] = np.tile((np.arange(8)[None, :] == je[:, None]).astype(np.float32), (1, 3))
    return {k: np.ascontiguousarray(v) for k, v in c.items()}


def tiles(w):
    k, n = w.shape
    return w.reshape(k // P, P, n // P, P).transpose(2, 1, 0, 3)


def by_partition(v):
    return v.reshape(-1, P).T


def lay_out(x_prompt, x_sample, cache_a_kv, cache_b_kv, cache_b_win, cache_mem_kv, cache_ffn_conv, page_table,
            mem_prompt, g_mix, w_in, g_qa, g_ka, g_qb, g_kb, pe_cmp, w_cmp1, w_cmp2, w_br_a, w_br_b, w_o, g_xattn,
            g_mem, w_mq, w_mkv, g_mq, g_mk, w_mo, g_ffn, w_ffn_up, w_conv, b_conv, w_ffn_down):
    a = dict(constants())
    feature = lambda x: x.reshape(-1, D).T.reshape(KD, P, -1).transpose(1, 0, 2)
    a["x"] = np.concatenate([feature(x_prompt), feature(x_sample)], 2)
    a["mem"] = feature(mem_prompt)
    w = w_in[0]
    at = np.cumsum([0, 512, 512, 512, 512, 768, 24, 2048])
    qa, ka, va, qb, kvb, gb, gm = (w[:, at[i]:at[i + 1]] for i in range(7))
    qb = qb.reshape(D, 2, 4, HD).transpose(0, 2, 1, 3).reshape(D, 512)
    gb = gb.reshape(D, 3, 2, 4).transpose(0, 1, 3, 2).reshape(D, 24)
    kv = [kvb[:, i * P:(i + 1) * P] for i in range(6)]
    a["w_proj"] = tiles(np.concatenate([qa, ka, qb, kv[0], kv[2], kv[4], kv[1]], 1))
    a["w_val"] = np.concatenate([va, kv[3], kv[5], gb], 1).reshape(KD, P, VCOL).transpose(1, 0, 2)
    a["w_memk"] = tiles(w_mkv[0][:, :512])
    a["w_memv"] = w_mkv[0][:, 512:].reshape(KD, P, 512).transpose(1, 0, 2)
    two = lambda g: np.tile(g, 2)
    a["g_heads"] = np.stack([two(g_qa[0])] * 4 + [two(g_ka[0])] * 4 + [two(g_qb[0])] * 4
                            + [two(g_kb[0, i]) for i in range(3)], 1)
    a["g_model"] = np.concatenate([by_partition(g[0]) for g in (g_mix, g_mem, g_xattn, g_ffn)], 1)
    a["g_memh"] = np.stack([g_mk[0], g_mq[0]], 1)
    a["w_cmp1"] = w_cmp1[0].reshape(2, 2, 8, 2 * HD, P).transpose(3, 0, 1, 2, 4)
    a["pe_cmp"] = pe_cmp[0].reshape(2, 2, 8, 2 * HD).transpose(3, 0, 1, 2)
    k2 = np.zeros((P, 2, P), np.float32)
    k2[:, 0, :HD] = k2[:, 1, HD:] = w_cmp2[0, 0]
    a["w_cmp2"] = np.concatenate([k2.reshape(P, 2 * P), w_cmp2[0, 1]], 1)
    gates = tiles(gm)
    br_a = tiles(w_br_a[0])
    br_b = tiles(w_br_b[0].reshape(2, 4, HD, D).transpose(1, 0, 2, 3).reshape(512, D))
    chunks = []
    for n in range(KD):
        chunks += [gates[n], gates[KD + n], np.concatenate([br_a[n], br_b[n]], 1)]
    chunks += list(tiles(w_o[0])) + list(tiles(w_mq[0]))
    mo = tiles(w_mo[0])
    chunks += [np.concatenate([mo[n], mo[n + 1]], 1) for n in range(0, KD, 2)]
    up = tiles(w_ffn_up[0])
    for n in range(KF):
        chunks += [up[n], up[KF + n]]
    down = tiles(w_ffn_down[0])
    for n in range(KD):
        padded = np.zeros((P, 24, P), np.float32)
        padded[:, :KF] = down[n]
        chunks += [padded[:, i:i + 8] for i in (0, 8, 16)]
    a["w_close"] = np.stack(chunks)
    cw = w_conv[0].reshape(3, 2 * KF, P).transpose(2, 1, 0)
    a["w_conv"] = np.concatenate([cw, b_conv[0].reshape(2 * KF, P).T[:, :, None]], 2)
    a["ffn_past"] = cache_ffn_conv[0].reshape(NSEQ, 2, 2 * KF, P).transpose(3, 2, 0, 1)
    ka_, va_ = cache_a_kv[0, :, :, 0], cache_a_kv[0, :, :, 1]
    a["past_ka"] = ka_[:, KEYS_A].reshape(NSEQ, NKEY_A, 4, P).transpose(0, 3, 2, 1)
    a["past_va"] = va_[:, KEYS_A].reshape(NSEQ, 7, P, 512).transpose(0, 2, 1, 3)
    pg = cache_b_kv[0]
    n_phys = pg.shape[0]
    cmp_ = pg[:, :, 0:2].reshape(n_phys, 8, 8, 2, 2, 2, HD).transpose(0, 3, 6, 4, 5, 2, 1).reshape(n_phys, P, 256)
    ks_ = pg[:, :, 2].reshape(n_phys, PAGE, P).transpose(0, 2, 1)
    a["pages_k"] = np.concatenate([cmp_, ks_], 2)
    a["pages_v"] = pg[:, :, 3].reshape(n_phys, PAGE, P)
    a["past_kw"] = cache_b_win[0, :, :, 0].reshape(NSEQ, 512, P).transpose(0, 2, 1)
    a["past_vw"] = cache_b_win[0, :, :, 1].reshape(NSEQ, 4, P, P).transpose(0, 2, 1, 3)
    a["past_km"] = cache_mem_kv[0, :, :, 0].transpose(0, 3, 2, 1)
    a["past_vm"] = cache_mem_kv[0, :, :, 1].reshape(NSEQ, 2, P, 512).transpose(0, 2, 1, 3)
    a["page_table"] = page_table.reshape(1, -1).astype(np.int32)
    return {k: np.ascontiguousarray(v) for k, v in a.items()}


OUTS = {
    "o_y": (P, KD, NT), "o_z": (P, NTILE, NT), "o_va": (P, QT, 512), "o_vas": (SN, 512),
    "o_vb": (P, QT, 256), "o_vbs": (SN, 256), "o_mk": (P, MH, MTOK), "o_mv": (P, 2, 512),
    "o_conv": (P, 2 * KF, 18),
}


def lay_back(o):
    y = o["o_y"].transpose(2, 1, 0).reshape(NT, D)
    z = o["o_z"].transpose(2, 1, 0)
    va = np.concatenate([o["o_va"].transpose(1, 0, 2).reshape(T, 512), o["o_vas"]])
    vb = np.concatenate([o["o_vb"].transpose(1, 0, 2).reshape(T, 256), o["o_vbs"]])
    ka = z[:, KA:KA + 4].reshape(NT, 8, HD)
    new_a = np.stack([ka, va.reshape(NT, 8, HD)], 1)
    head = lambda v: v.reshape(NT, 2, HD)
    new_b = np.stack([head(z[:, KC]), head(z[:, VC]), head(z[:, KS]), head(vb[:, :P])], 1)
    new_w = np.stack([head(z[:, KW]), head(vb[:, P:])], 1)
    mk = o["o_mk"].transpose(2, 1, 0)
    mv = o["o_mv"].transpose(1, 0, 2).reshape(MTOK, MH, MHD)
    conv = o["o_conv"].transpose(2, 1, 0).reshape(18, 2 * FF)
    smp = lambda v: v[T:].reshape((1, NSEQ, S) + v.shape[1:])
    pro = lambda v: v[:T].reshape((1, 1, T) + v.shape[1:])
    out = (y[:T].reshape(1, T, D), y[T:].reshape(NSEQ, S, D), pro(new_a), pro(new_b), pro(new_w),
           np.stack([mk, mv], 1)[None, None], conv[:2].reshape(1, 1, 2, 2 * FF),
           smp(new_a), smp(new_b), smp(new_w), conv[2:].reshape(1, NSEQ, 2, 2 * FF))
    return tuple(np.ascontiguousarray(v) for v in out)


class Steps:

    def __init__(self, engine, sem):
        self.engine, self.sem, self.n, self.offset = engine, sem, 0, None

    def done(self, instruction):
        instruction.then_inc(self.sem, 1)
        self.n += 1
        return self.n

    def wait(self, n=None):
        n = self.n if n is None else n
        self.engine.wait_ge(self.sem, n if self.offset is None else self.offset + n)


def halves(ap):
    return ap.rearrange("p (a b) -> p a b", a=2)


def reciprocal_root(dve, act, who, v, y, t, v_ready, y_ready, n, steps=None):
    if who == "act":
        act.wait_ge(v_ready, n + 1)
        act.activation(y, v, ACT.Ln).then_inc(y_ready, 1)
        act.wait_ge(y_ready, 2 * n + 1)
        act.activation(y, y, ACT.Exp, scale=-0.5).then_inc(y_ready, 1)
    else:
        dve.wait_ge(y_ready, 2 * n + 2)
        steps.done(dve.scalar_tensor_tensor(out=t, in0=v, scalar=-0.5, in1=y, op0=ALU.mult, op1=ALU.mult))
        steps.wait()
        steps.done(dve.tensor_tensor(t, t, y, ALU.mult))
        steps.wait()
        steps.done(dve.scalar_tensor_tensor(out=y, in0=t, scalar=1.5, in1=y, op0=ALU.add, op1=ALU.mult))
        steps.wait()


def project(nc, d, m, sem):
    with ExitStack() as mine:
        def sb(name, shape, dt=F32):
            return mine.enter_context(nc.sbuf_tensor(name, shape, dt))

        ps = m.ps
        x, h = sb("x", [P, KD, NT]), sb("h", [P, KD, NT])
        ring = sb("proj_ring", [P, RING, KD, P])
        w_val = sb("w_val_sb", [P, KD, VCOL])
        w_memv = sb("w_memv_sb", [P, KD, 512])
        mem = sb("mem_sb", [P, KD, MTOK])
        head_ones = sb("head_ones_sb", [P, P])
        rot = sb("rot_sb", [P, P])
        cos, sin = sb("cos_sb", [P, NT]), sb("sin_sb", [P, NT])
        g_heads = sb("g_heads_sb", [P, 15])
        mean, root, scratch = sb("mean", [P, NT]), sb("root", [P, NT]), sb("scratch", [P, NT])
        raw, square, normed = sb("raw", [P, 2, NT]), sb("square", [P, 2, NT]), sb("normed", [P, 2, NT])
        hm = m.oa

        def z_pair(j):
            return ps[:, 2 * (j % 2):2 * (j % 2) + 2, 0:HALF]

        sum_pair, rot_pair = ps[:, 4:6, 0:HALF], ps[:, 6:8, 0:HALF]
        order = [VC] + list(range(VC))
        NJOB = NTILE + MH
        NVAL = QT + 1 + 2

        const_in, x_in, mem_in = sem("const_in"), sem("x_in"), sem("mem_in")
        val_in, memv_in = sem("val_in"), sem("memv_in")
        chunk_in = [sem(f"proj_chunk{i}") for i in range(RING)]
        squared, sum_full = sem("squared"), sem("sum_full")
        v_ready, y_ready = sem("mean_ready"), sem("root_ready")
        h_ready = sem("h_ready")
        z_full, z_out = sem("z_full"), sem("z_out")
        n_ready, rot_full, tile_done = sem("normed_ready"), sem("rot_full"), sem("tile_done")
        val_full, val_out, gate_ready = sem("val_full"), sem("val_out"), sem("gate_ready")
        dve_step = sem("proj_dve_step")
        stored = sem("proj_stored")

        with nc.Block() as block:
            @block.sync
            def _(sp):
                for dst, name in ((m.ones, "ones"), (m.g_model, "g_model"), (head_ones, "head_ones"), (rot, "rot"),
                                  (cos, "cos"), (sin, "sin"), (g_heads, "g_heads"), (m.g_memh, "g_memh"),
                                  (m.ident, "ident")):
                    sp.dma_start(dst[:, :], d[name]).then_inc(const_in, 16)
                for j in range(NJOB):
                    if j >= RING:
                        sp.wait_ge(z_full, j - RING + 1)
                    src = d["w_proj"][order[j]] if j < NTILE else d["w_memk"][j - NTILE]
                    sp.dma_start(ring[:, j % RING], src).then_inc(chunk_in[j % RING], 16)
                sp.wait_ge(z_out, 1)
                sp.wait_ge(tile_done, NJOB - 1)
                sp.dma_start(d["o_z"], m.z[:, :, :]).then_inc(stored, 16)
                sp.dma_start(d["o_mk"], m.mk[:, :, :]).then_inc(stored, 16)
                sp.wait_ge(val_out, NVAL)
                sp.dma_start(d["o_va"], m.va[:, 0:QT, :]).then_inc(stored, 16)
                sp.dma_start(d["o_vas"], m.va[0:SN, QT, :]).then_inc(stored, 16)
                sp.dma_start(d["o_vb"], m.vb[:, 0:QT, :]).then_inc(stored, 16)
                sp.dma_start(d["o_vbs"], m.vb[0:SN, QT, :]).then_inc(stored, 16)
                sp.dma_start(d["o_mv"], m.mv[:, :, :]).then_inc(stored, 16)
                sp.wait_ge(stored, 16 * 7)

            @block.scalar
            def _(act):
                act.dma_start(x[:, :, :], d["x"]).then_inc(x_in, 16)
                act.dma_start(mem[:, :, :], d["mem"]).then_inc(mem_in, 16)
                act.dma_start(w_val[:, :, :], d["w_val"]).then_inc(val_in, 16)
                act.dma_start(w_memv[:, :, :], d["w_memv"]).then_inc(memv_in, 16)
                act.wait_ge(x_in, 16)
                for k in range(KD):
                    act.activation(h[:, k, :], x[:, k, :], ACT.Square).then_inc(squared, 1)
                act.wait_ge(mem_in, 16)
                for k in range(KD):
                    act.activation(hm[:, k, 0:MTOK], mem[:, k, :], ACT.Square).then_inc(squared, 1)
                reciprocal_root(None, act, "act", mean[:, :], root[:, :], None, v_ready, y_ready, 0)
                reciprocal_root(None, act, "act", mean[:, 0:MTOK], root[:, 0:MTOK], None, v_ready, y_ready, 1)

                def roots(j):
                    c = slice(0, NT if j < NTILE else MTOK)
                    reciprocal_root(None, act, "act", mean[:, c], root[:, c], None, v_ready, y_ready, j + 1)

                for j in range(NJOB):
                    act.wait_ge(z_full, j + 1)
                    if j == 0:
                        act.copy(halves(m.z[:, VC, :]), z_pair(0)).then_inc(z_out, 1)
                        continue
                    if j >= 3:
                        act.wait_ge(tile_done, j - 2)
                        act.wait_ge(sum_full, j)
                    if j < NTILE:
                        act.copy(halves(raw[:, j % 2, :]), z_pair(j))
                        act.activation(halves(square[:, j % 2, :]), z_pair(j), ACT.Square).then_inc(z_out, 1)
                    else:
                        act.copy(raw[:, j % 2, 0:MTOK], z_pair(j)[:, 0, 0:MTOK])
                        act.activation(square[:, j % 2, 0:MTOK], z_pair(j)[:, 0, 0:MTOK], ACT.Square)\
                            .then_inc(z_out, 1)
                    if j >= 2:
                        roots(j - 1)
                roots(NJOB - 1)
                for u in range(NVAL):
                    act.wait_ge(val_full, u + 1)
                    wide, narrow = ps[:, 2 * (u % 2), :], ps[:, 2 * (u % 2) + 1, :]
                    if u > QT:
                        act.copy(m.mv[:, u - QT - 1, :], wide).then_inc(val_out, 1)
                        continue
                    n = P if u < QT else SN
                    act.copy(m.va[0:n, u, :], wide[0:n])
                    act.copy(m.vb[0:n, u, :], narrow[0:n, 0:256])
                    act.activation(m.gate[0:n, u, :], narrow[0:n, 256:280], ACT.Exp, scale=-1.0).then_inc(val_out, 1)

            @block.tensor
            def _(pe):
                def sums(j, lhs, src, width, k_tiles):
                    for k in range(k_tiles):
                        if width == NT:
                            for a in range(2):
                                last = pe.matmul(ps[:, 4 + a, 0:HALF], lhs, src(k)[:, a * HALF:(a + 1) * HALF],
                                                 start=(k == 0), stop=(k == k_tiles - 1))
                        else:
                            last = pe.matmul(ps[:, 4, 0:width], lhs, src(k)[:, 0:width],
                                             start=(k == 0), stop=(k == k_tiles - 1))
                    last.then_inc(sum_full, 1)

                pe.wait_ge(const_in, 16 * 9)
                pe.wait_ge(squared, KD)
                sums(0, m.ones[:, :], lambda k: h[:, k, :], NT, KD)
                pe.wait_ge(squared, 2 * KD)
                pe.wait_ge(v_ready, 1)
                sums(0, m.ones[:, :], lambda k: hm[:, k, :], MTOK, KD)
                pe.wait_ge(h_ready, 1)

                def product(j):
                    pe.wait_ge(chunk_in[j % RING], 16 * (j // RING + 1))
                    if j >= 2:
                        pe.wait_ge(z_out, j - 1)
                    if j == NTILE:
                        pe.wait_ge(h_ready, 2)
                    for k in range(KD):
                        w = ring[:, j % RING, k, :]
                        if j < NTILE:
                            for a in range(2):
                                last = pe.matmul(ps[:, 2 * (j % 2) + a, 0:HALF], w, h[:, k, a * HALF:(a + 1) * HALF],
                                                 start=(k == 0), stop=(k == KD - 1))
                        else:
                            last = pe.matmul(ps[:, 2 * (j % 2), 0:MTOK], w, hm[:, k, 0:MTOK],
                                             start=(k == 0), stop=(k == KD - 1))
                    last.then_inc(z_full, 1)

                def job_sum(j):
                    pe.wait_ge(z_out, j + 1)
                    pe.wait_ge(v_ready, j + 1)
                    lhs = head_ones if j < NTILE else m.ones
                    sums(j, lhs[:, :], lambda k: square[:, j % 2, :], NT if j < NTILE else MTOK, 1)

                def job_rot(j):
                    pe.wait_ge(n_ready, j)
                    if j >= 2:
                        pe.wait_ge(tile_done, j - 1)
                    for a in range(2):
                        last = pe.matmul(ps[:, 6 + a, 0:HALF], rot[:, :], normed[:, j % 2, a * HALF:(a + 1) * HALF],
                                         start=True, stop=True)
                    last.then_inc(rot_full, 1)

                for j in range(NJOB + 2):
                    if j < NJOB:
                        product(j)
                    if 1 <= j - 1 < NJOB:
                        job_sum(j - 1)
                    if 1 <= j - 2 < NTILE:
                        job_rot(j - 2)
                pe.wait_ge(val_in, 16)
                pe.wait_ge(memv_in, 16)
                for u in range(NVAL):
                    pe.wait_ge(z_out, NJOB)
                    if u >= 2:
                        pe.wait_ge(val_out, u - 1)
                    wide, narrow = ps[:, 2 * (u % 2), :], ps[:, 2 * (u % 2) + 1, :]
                    if u > QT:
                        for k in range(KD):
                            last = pe.matmul(wide, hm[:, k, (u - QT - 1) * P:(u - QT) * P], w_memv[:, k, :],
                                             start=(k == 0), stop=(k == KD - 1))
                    else:
                        n = P if u < QT else SN
                        for cols, out in ((slice(0, 512), wide[0:n]), (slice(512, VCOL), narrow[0:n, 0:VCOL - 512])):
                            for k in range(KD):
                                last = pe.matmul(out, h[:, k, u * P:u * P + n], w_val[:, k, cols],
                                                 start=(k == 0), stop=(k == KD - 1))
                    last.then_inc(val_full, 1)

            @block.vector
            def _(dve):
                step = Steps(dve, dve_step)

                def root_of(j, full, cols, divisor):
                    dve.wait_ge(sum_full, j + 1)
                    pair, mean_ = full
                    dve.tensor_scalar(mean_, pair, 1.0 / divisor, EPS, ALU.mult, ALU.add).then_inc(v_ready, 1)
                    dve.wait_ge(v_ready, j + 1)
                    reciprocal_root(dve, None, "dve", mean[:, 0:cols], root[:, 0:cols], scratch[:, 0:cols],
                                    v_ready, y_ready, j, step)

                dve.wait_ge(const_in, 16 * 9)
                root_of(0, (sum_pair, halves(mean[:, :])), NT, D)
                for k in range(KD):
                    last = dve.scalar_tensor_tensor(out=h[:, k, :], in0=x[:, k, :], scalar=m.g_model[:, k:k + 1],
                                                    in1=root[:, :], op0=ALU.mult, op1=ALU.mult)
                last.then_inc(h_ready, 1)
                dve.wait_ge(h_ready, 1)
                root_of(1, (ps[:, 4, 0:MTOK], mean[:, 0:MTOK]), MTOK, D)
                for k in range(KD):
                    last = dve.scalar_tensor_tensor(out=hm[:, k, 0:MTOK], in0=mem[:, k, :],
                                                    scalar=m.g_model[:, KD + k:KD + k + 1],
                                                    in1=root[:, 0:MTOK], op0=ALU.mult, op1=ALU.mult)
                last.then_inc(h_ready, 1)
                for j in range(1, NJOB):
                    if j < NTILE:
                        root_of(j + 1, (sum_pair, halves(mean[:, :])), NT, HD)
                        t = order[j]
                        if j >= 3:
                            dve.wait_ge(rot_full, j - 2)
                        dve.scalar_tensor_tensor(out=normed[:, j % 2, :], in0=raw[:, j % 2, :],
                                                 scalar=g_heads[:, t:t + 1], in1=root[:, :],
                                                 op0=ALU.mult, op1=ALU.mult).then_inc(n_ready, 1)
                        dve.wait_ge(rot_full, j)
                        step.done(dve.tensor_tensor(halves(scratch[:, :]), rot_pair, halves(sin[:, :]), ALU.mult))
                        dve.wait_ge(n_ready, j)
                        step.done(dve.tensor_tensor(m.z[:, t, :], normed[:, j % 2, :], cos[:, :], ALU.mult))
                        step.wait()
                        dve.tensor_tensor(m.z[:, t, :], m.z[:, t, :], scratch[:, :], ALU.add).then_inc(tile_done, 1)
                        dve.wait_ge(tile_done, j)
                    else:
                        root_of(j + 1, (ps[:, 4, 0:MTOK], mean[:, 0:MTOK]), MTOK, MHD)
                        dve.scalar_tensor_tensor(out=m.mk[:, j - NTILE, :], in0=raw[:, j % 2, 0:MTOK],
                                                 scalar=m.g_memh[:, 0:1], in1=root[:, 0:MTOK],
                                                 op0=ALU.mult, op1=ALU.mult).then_inc(tile_done, 1)
                        dve.wait_ge(tile_done, j)
                dve.wait_ge(val_out, QT + 1)
                for part in (m.gate[:, 0:QT, :], m.gate[0:SN, QT, :]):
                    step.done(dve.tensor_scalar(part, part, 1.0, None, ALU.add))
                    step.wait()
                    dve.reciprocal(part, part).then_inc(gate_ready, 1)


def one(t, index, cols):
    return t[:, ds(index, 1), cols].rearrange("p a n -> p (a n)")


class Compress:

    GELU, CUBE = -2.0 * (2.0 / np.pi) ** 0.5, 0.044715

    def __init__(self, sb, sem, ps, w1, w2, bias, n, banks):
        self.ps, self.w1, self.w2, self.bias, self.n = ps, w1, w2, bias, n
        self.proj, self.small = banks[0:2], banks[2]
        self.second = sb(f"cmp_second{n}", [P, 2, 2, n])
        self.hid = sb(f"cmp_hid{n}", [P, 2, 2, n])
        self.cube = sb(f"cmp_cube{n}", [P, 2, 2, n])
        self.proj_full, self.second_ready = sem(f"cmp_proj_full{n}"), sem(f"cmp_second_ready{n}")
        self.inner_ready, self.exp_ready = sem(f"cmp_inner_ready{n}"), sem(f"cmp_exp_ready{n}")
        self.hid_ready, self.small_full, self.small_out = (sem(f"cmp_hid_ready{n}"), sem(f"cmp_small_full{n}"),
                                                          sem(f"cmp_small_out{n}"))

    def parts(self, kv):
        v = self.ps[:, self.proj[kv], 0:4 * self.n].rearrange("p (r g c) -> p r g c", r=2, g=2)
        return v[:, 0], v[:, 1]

    def pe_project(self, pe, kv, x):
        for r in range(2):
            for s1 in range(8):
                last = pe.matmul(self.parts(kv)[r], self.w1[:, kv, r, s1, :], x(s1), start=(s1 == 0), stop=(s1 == 7))
        last.then_inc(self.proj_full, 1)

    def act_second(self, act, turn, kv):
        act.wait_ge(self.proj_full, turn + 1)
        act.activation(self.second[:, kv], self.parts(kv)[1], ACT.Identity, bias=self.bias[:, kv:kv + 1])\
            .then_inc(self.second_ready, 1)

    def dve_inner(self, dve, step, turn, kv):
        n = self.n
        a, b = self.hid[:, kv, :, 0:n - 1], self.cube[:, kv, :, 0:n - 1]
        dve.wait_ge(self.second_ready, turn + 1)
        step.done(dve.tensor_tensor(a, self.second[:, kv, :, 1:n], self.parts(kv)[0][:, :, 0:n - 1], ALU.add))
        step.wait()
        step.done(dve.tensor_tensor(b, a, a, ALU.mult))
        step.wait()
        step.done(dve.scalar_tensor_tensor(out=b, in0=b, scalar=self.CUBE, in1=a, op0=ALU.mult, op1=ALU.mult))
        step.wait()
        step.done(dve.tensor_tensor(b, b, a, ALU.add))
        step.wait()
        dve.tensor_scalar(b, b, -50.0, None, ALU.max).then_inc(self.inner_ready, 1)

    def act_exp(self, act, turn, kv):
        b = self.cube[:, kv, :, 0:self.n - 1]
        act.wait_ge(self.inner_ready, turn + 1)
        act.activation(b, b, ACT.Exp, scale=self.GELU).then_inc(self.exp_ready, 1)

    def dve_hidden(self, dve, step, turn, kv):
        a, b = self.hid[:, kv, :, 0:self.n - 1], self.cube[:, kv, :, 0:self.n - 1]
        dve.wait_ge(self.exp_ready, turn + 1)
        step.done(dve.tensor_scalar(b, b, 1.0, None, ALU.add))
        step.wait()
        step.done(dve.reciprocal(b, b))
        step.wait()
        dve.tensor_tensor(a, a, b, ALU.mult).then_inc(self.hid_ready, 1)

    def pe_small(self, pe, turn, kv):
        n = self.n
        pe.wait_ge(self.hid_ready, turn + 1)
        for g in range(2):
            if kv == 0:
                last = pe.matmul(self.ps[:, self.small, 0:n - 1], self.w2[:, g * P:(g + 1) * P],
                                 self.hid[:, kv, g, 0:n - 1], start=(g == 0), stop=(g == 1))
            else:
                last = pe.matmul(self.ps[0:n - 1, self.small, P + g * HD:P + (g + 1) * HD],
                                 self.hid[:, kv, g, 0:n - 1], self.w2[:, 2 * P:2 * P + HD], start=True, stop=True)
        last.then_inc(self.small_full, 1)

    def act_small(self, act, turn, kv, dst):
        act.wait_ge(self.small_full, turn + 1)
        n = self.n
        src = self.ps[:, self.small, 0:n - 1] if kv == 0 else self.ps[0:n - 1, self.small, P:2 * P]
        act.copy(dst, src).then_inc(self.small_out, 1)


def attend_prompt(nc, d, m, sem):
    with ExitStack() as mine:
        def sb(name, shape, dt=F32):
            return mine.enter_context(nc.sbuf_tensor(name, shape, dt))

        ps = m.ps
        mask_dil, mask_causal = sb("mask_dil_sb", [P, T]), sb("mask_causal_sb", [P, T])
        mask_cmp, live = sb("mask_cmp_sb", [P, QT * NCMP_P]), sb("cmp_live_sb", [P, QT])
        w1, w2, pe_col = sb("pw1", [P, 2, 2, 8, P]), sb("pw2", [P, 320]), sb("pe_col", [P, 2, 2, 8])
        chunked = sb("chunked", [P, 2, 2, 8, 32])
        q_pad = [sb(f"q_pad{i}", [P, T]) for i in range(4)]
        kc, vc = sb("kc", [P, NCMP_P]), sb("vc", [NCMP_P, P])
        score, prob_t = sb("score", [P, 4, T]), sb("prob_t", [P, 3, T])
        low, total, factor = sb("low", [P, 8]), sb("total", [P, 8]), sb("factor", [P, 2])
        o_dil, o_nsa = sb("o_dil", [P, QT, P]), sb("o_nsa", [P, QT, P])

        const_in = sem("prompt_const_in")
        chunked_ready, bias_full, bias_out = sem("chunked_ready"), sem("bias_full"), sem("bias_out")
        zeroed, pads_ready = sem("pads_zeroed"), sem("pads_ready")
        s_full, s_done, e_done = sem("s_full"), sem("s_done"), sem("e_done")
        pt_full, pt_out = sem("pt_full"), sem("pt_out")
        o_full, o_out = sem("o_full"), sem("o_out")
        ot_full, ot_out = sem("ot_full"), sem("ot_out")
        dve_step, begun = sem("prompt_dve_step"), sem("prompt_begun")
        cmp = Compress(sb, sem, ps, w1, w2, m.cmp_bias, 32, (4, 7, 5))
        DIL, SLC, WIN, CMP = range(4)
        units = [(e, kind, qt) for e in range(2) for kind in (DIL, SLC, WIN, CMP) for qt in range(QT)]
        U = len(units)

        def width(u):
            return NCMP_P if units[u][1] == CMP else (units[u][2] + 1) * P

        with nc.Block() as block:
            @block.sync
            def _(sp):
                for dst, name in ((w1, "w_cmp1"), (pe_col, "pe_cmp"), (w2, "w_cmp2"), (mask_dil, "mask_dil"),
                                  (mask_causal, "mask_causal"), (mask_cmp, "mask_cmp"), (live, "cmp_live")):
                    full = (slice(None),) * len(dst.shape)
                    sp.dma_start(dst[full], d[name]).then_inc(const_in, 16)

            @block.gpsimd
            def _(pool):
                for dst, src in ((m.zs[:, :, :], m.z[:, :, T:NT]), (m.vas[:, :], m.va[0:SN, QT, :]),
                                 (m.vbs[:, :], m.vb[0:SN, QT, :]), (m.gates[:, :], m.gate[0:SN, QT, :])):
                    pool.tensor_copy(dst, src)
                for i in range(4):
                    pool.memset(q_pad[i][:, :], 0.0).then_inc(zeroed, 1)
                pool.wait_ge(zeroed, 4)
                with pool.Fori(0, 4) as j:
                    for i in range(4):
                        e = i % 2
                        src = one(m.z, j + (QA if i < 2 else QB), slice(0, T))
                        pool.tensor_copy(q_pad[i][e * HD:(e + 1) * HD, :], src[e * HD:(e + 1) * HD, :])\
                            .then_inc(pads_ready, 1)
                    pool.wait_ge(s_full, j * U + U)

            @block.scalar
            def _(act):
                act.wait_ge(bias_full, 1)
                act.copy(m.cmp_bias[:, :], ps[:, 6, 0:2]).then_inc(bias_out, 1)
                act.wait_ge(bias_out, 1)
                for kv in range(2):
                    cmp.act_second(act, kv, kv)
                for kv in range(2):
                    cmp.act_exp(act, kv, kv)
                for kv in range(2):
                    cmp.act_small(act, kv, kv, (kc, vc)[kv][:, :])
                with act.Fori(0, 4) as j:
                    for u in range(U + 3):
                        if u < U:
                            n = width(u)
                            act.wait_ge(s_done, j * U + (u + 1))
                            act.activation(score[:, u % 4, 0:n], score[:, u % 4, 0:n], ACT.Exp,
                                           bias=low[:, u % 8:u % 8 + 1], scale=-1.0,
                                           accum_out=total[:, u % 8:u % 8 + 1]).then_inc(e_done, 1)
                        if u >= 3:
                            v = u - 3
                            act.wait_ge(pt_full, j * U + (v + 1))
                            if v >= 3:
                                act.wait_ge(o_full, j * U + (v - 2))
                            if units[v][1] == CMP:
                                act.copy(prob_t[0:NCMP_P, v % 3, 0:P], ps[0:NCMP_P, 4 + v % 2, 0:P])\
                                    .then_inc(pt_out, 1)
                            else:
                                act.copy(prob_t[:, v % 3, 0:width(v)], ps[:, 4 + v % 2, 0:width(v)])\
                                    .then_inc(pt_out, 1)
                    for i in range(2):
                        act.wait_ge(ot_full, j * 2 + (i + 1))
                        act.copy(one(m.oa, j + 4 * i, slice(0, T)), ps[:, 4 + i, :]).then_inc(ot_out, 1)

            @block.tensor
            def _(pe):
                pe.wait_ge(const_in, 16 * 7)
                for kv in range(2):
                    for r in range(2):
                        for s1 in range(8):
                            last = pe.matmul(ps[:, 6, kv:kv + 1], w1[:, kv, r, s1, :], pe_col[:, kv, r, s1:s1 + 1],
                                             start=(r + s1 == 0), stop=(r + s1 == 8))
                last.then_inc(bias_full, 1)
                pe.wait_ge(chunked_ready, 8)
                for kv in range(2):
                    cmp.pe_project(pe, kv, lambda s1: chunked[:, kv, :, s1, :])
                for kv in range(2):
                    if kv == 1:
                        pe.wait_ge(cmp.small_out, 1)
                    cmp.pe_small(pe, kv, kv)
                pe.wait_ge(cmp.small_out, 2)
                with pe.Fori(0, 4) as j:
                    def scores(u):
                        e, kind, qt = units[u]
                        if u >= 4:
                            pe.wait_ge(s_done, j * U + (u - 3))
                        key = {DIL: lambda n: one(m.z, j + KA, slice(0, n)), SLC: lambda n: m.z[:, KS, 0:n],
                               WIN: lambda n: m.z[:, KW, 0:n], CMP: lambda n: kc[:, 0:n]}[kind]
                        q = q_pad[e if kind == DIL else 2 + e]
                        pe.matmul(ps[:, u % 4, 0:width(u)], q[:, qt * P:(qt + 1) * P], key(width(u)),
                                  start=True, stop=True).then_inc(s_full, 1)

                    def turn(u):
                        e, kind, qt = units[u]
                        pe.wait_ge(e_done, j * U + (u + 1))
                        if u >= 2:
                            pe.wait_ge(pt_out, j * U + (u - 1))
                        if kind == CMP:
                            last = pe.transpose(ps[0:NCMP_P, 4 + u % 2, 0:P], score[:, u % 4, 0:NCMP_P], m.ident[:, :])
                        else:
                            for k in range(qt + 1):
                                last = pe.transpose(ps[:, 4 + u % 2, k * P:(k + 1) * P],
                                                    score[:, u % 4, k * P:(k + 1) * P], m.ident[:, :])
                        last.then_inc(pt_full, 1)

                    def values(u):
                        e, kind, qt = units[u]
                        pe.wait_ge(pt_out, j * U + (u + 1))
                        if u >= 2:
                            pe.wait_ge(o_out, j * U + (u - 1))
                        out = ps[:, 6 + u % 2, 0:HD]
                        if kind == CMP:
                            last = pe.matmul(out, prob_t[0:NCMP_P, u % 3, 0:P], vc[:, e * HD:(e + 1) * HD],
                                             start=True, stop=True)
                        else:
                            for k in range(qt + 1):
                                v = m.va[:, k, ds(j * P + e * HD, HD)] if kind == DIL else \
                                    m.vb[:, k, (kind == WIN) * P + e * HD:(kind == WIN) * P + (e + 1) * HD]
                                last = pe.matmul(out, prob_t[:, u % 3, k * P:(k + 1) * P], v,
                                                 start=(k == 0), stop=(k == qt))
                        last.then_inc(o_full, 1)

                    pe.wait_ge(pads_ready, j * 4 + 4)
                    for u in range(U + 5):
                        if u < U:
                            scores(u)
                        if 0 <= u - 3 < U:
                            turn(u - 3)
                        if 0 <= u - 5 < U:
                            values(u - 5)
                    pe.wait_ge(o_out, j * U + U)
                    for i, o in enumerate((o_dil, o_nsa)):
                        for qt in range(QT):
                            last = pe.transpose(ps[:, 4 + i, qt * P:(qt + 1) * P], o[:, qt, :], m.ident[:, :])
                        last.then_inc(ot_full, 1)
                    pe.wait_ge(ot_out, j * 2 + 2)

            @block.vector
            def _(dve):
                step = Steps(dve, dve_step)
                for kv, tile in enumerate((KC, VC)):
                    v = m.z[:, tile, 0:T].rearrange("p (c s t) -> p t s c", s=8, t=2)
                    for g in range(2):
                        for s2 in range(2):
                            dve.tensor_copy(chunked[s2 * HD:(s2 + 1) * HD, kv, g], v[g * HD:(g + 1) * HD, s2])\
                                .then_inc(chunked_ready, 1)
                for kv in range(2):
                    cmp.dve_inner(dve, step, kv, kv)
                for kv in range(2):
                    cmp.dve_hidden(dve, step, kv, kv)
                dve.wait_ge(const_in, 16 * 7)
                with dve.Fori(0, 4) as j:
                    PER = 64
                    first, step.offset = step.n, j * PER

                    def finish_unit(u):
                        e, kind, qt = units[u]
                        r, f = total[:, u % 8:u % 8 + 1], factor[:, u % 2:u % 2 + 1]
                        step.done(dve.reciprocal(f, r))
                        step.wait()
                        if kind != DIL:
                            branch = (CMP, SLC, WIN).index(kind)
                            gate = m.gate[:, qt, ds(j * 2 + branch * 8 + e, 1)]
                            if kind == CMP:
                                step.done(dve.tensor_tensor(f, f, live[:, qt:qt + 1], ALU.mult))
                                step.wait()
                            step.done(dve.tensor_tensor(f, f, gate, ALU.mult))
                            step.wait()
                        o = (o_dil if kind == DIL else o_nsa)[:, qt, e * HD:(e + 1) * HD]
                        src = ps[:, 6 + u % 2, 0:HD]
                        dve.wait_ge(o_full, j * U + (u + 1))
                        if kind in (DIL, SLC):
                            dve.tensor_scalar(o, src, f, None, ALU.mult).then_inc(o_out, 1)
                        else:
                            dve.wait_ge(o_out, j * U + (u - 3))
                            dve.scalar_tensor_tensor(out=o, in0=src, scalar=f, in1=o, op0=ALU.mult, op1=ALU.add)\
                                .then_inc(o_out, 1)

                    for u in range(U + 6):
                        if u < U:
                            e, kind, qt = units[u]
                            n = width(u)
                            table = {DIL: mask_dil, SLC: mask_causal, WIN: mask_causal}.get(kind)
                            mask = mask_cmp[:, qt * NCMP_P:(qt + 1) * NCMP_P] if kind == CMP else table[:, T - n:T]
                            dve.wait_ge(s_full, j * U + (u + 1))
                            if u >= 4:
                                dve.wait_ge(pt_full, j * U + (u - 3))
                            dve.sem_inc(begun, 1)
                            dve.tensor_tensor_reduce(score[:, u % 4, 0:n], ps[:, u % 4, 0:n], mask, -SCALE, 3e38,
                                                     ALU.add, ALU.min, low[:, u % 8:u % 8 + 1]).then_inc(s_done, 1)
                        if u >= 6:
                            dve.wait_ge(e_done, j * U + (u - 5))
                            finish_unit(u - 6)
                    dve.wait_ge(ot_full, j * 2 + 2)
                    assert step.n - first == PER
                step.offset = None




def attend_sample(nc, d, m, sem):
    with ExitStack() as mine:
        def sb(name, shape, dt=F32):
            return mine.enter_context(nc.sbuf_tensor(name, shape, dt))

        ps = m.ps
        NB = NPAGE
        pages = sb("pages", [P, 2, NB * 384])
        dil = sb("dil", [P, 2, 7 * 512])
        win = sb("win", [P, 2, 512])
        w1, w2 = sb("sw1", [P, 2, 2, 8, P]), sb("sw2", [P, 320])
        q_dil, q_nsa = sb("q_dil", [P, 4, P]), sb("q_nsa", [P, P])
        s_dil, s_slc = sb("s_dil", [P, NKEY_A + SN]), sb("s_slc", [P, PAST + SN])
        s_win, s_cmp = sb("s_win", [P, 512 + SN]), sb("s_cmp", [P, NCMP_S])
        mask_dil, mask_win = sb("mask_sdil_sb", [P, NKEY_A + SN]), sb("mask_swin_sb", [P, 512 + SN])
        mask_new, pick = sb("mask_snew_sb", [P, SN]), sb("pick_sb", [SN, P])
        t_dil, t_slc = sb("t_dil", [P, 8, P]), sb("t_slc", [P, 18, P])
        t_win, t_cmp, t_cmpg = sb("t_win", [P, 5, P]), sb("t_cmp", [P, P]), sb("t_cmpg", [P, P])
        kc, vc = sb("skc", [P, NCMP_S]), sb("svc", [NCMP_S, 4, P])
        overlap, same = sb("overlap_sb", [NCMP_S, NBLK]), sb("same_sb", [P, P])
        forced, earlier = sb("forced_sb", [P, NBLK]), sb("earlier_sb", [P, NBLK * NBLK])
        gate_pick, gates = sb("gate_pick_sb", [P, 24]), sb("gates", [P, 24])
        o_rows = sb("o_rows", [P, 640])
        gate3, importance = sb("gate3", [P, 3]), sb("importance", [P, NBLK])
        points, drop = sb("points", [P, NBLK]), sb("drop", [P, NBLK])
        small = sb("small_s", [P, 16])
        low, total, factor = (lambda i: small[:, i:i + 1]), (lambda i: small[:, 4 + i:5 + i]), \
            (lambda i: small[:, 8 + i:9 + i])
        table = sb("page_table_sb", [1, NSEQ * NPAGE], I32)
        rank = t_slc[:, :, :].rearrange("p a b -> p (a b)")
        beats, ties = (rank[:, i * NBLK * NBLK:(i + 1) * NBLK * NBLK].rearrange("p (j i) -> p j i", i=NBLK)
                       for i in range(2))

        table_in, const_in = sem("table_in"), sem("sample_const_in")
        pages_in = [sem(f"pages_in{i}") for i in range(2)]
        dil_in = [sem(f"dil_in{i}") for i in range(2)]
        win_in = [sem(f"win_in{i}") for i in range(2)]
        values_used, dil_used = sem("values_used"), sem("dil_used")
        loads_begun = sem("loads_begun")
        group_in, group_used = sem("group_in"), sem("group_used")
        q_zero, q_ready, k_pass = sem("q_zero"), sem("q_ready"), sem("k_pass")
        tile_full, tile_act, tile_dve = sem("tile_full"), sem("tile_act"), sem("tile_dve")
        new_full, new_out = sem("new_full"), sem("new_out")
        low_ready, exp_ready, prob_ready = sem("low_ready"), sem("sexp_ready"), sem("prob_ready")
        turn_full, turn_out = sem("turn_full"), sem("turn_out")
        imp_full, imp_out, points_full = sem("imp_full"), sem("imp_out"), sem("points_full")
        rows_out, so_full, so_out = sem("rows_out"), sem("so_full"), sem("so_out")
        dve_step, begun = sem("sample_dve_step"), sem("sample_begun")
        cmp = Compress(sb, sem, ps, w1, w2, m.cmp_bias, 128, (0, 6, 1))
        C, A, W, S_ = range(4)
        turns = [(1, s_cmp, [0], t_cmp), (2, s_cmp, [0], t_cmpg), (3, s_dil, [0, 1, 2, 3], t_dil),
                 (3, s_dil, [4, 5, 6, 7], t_dil), (4, s_win, [0, 1, 2, 3], t_win), (4, s_win, [4], t_win)] \
            + [(5, s_slc, list(range(a, min(a + 4, NB + 1))), t_slc) for a in range(0, NB + 1, 4)]
        NTURN = len(turns)

        with nc.Block() as block:
            @block.sync
            def _(sp):
                sp.dma_start(table[:, :], d["page_table"]).then_inc(table_in, 16)
                for dst, name in ((w1, "w_cmp1"), (w2, "w_cmp2"), (overlap, "overlap"), (same, "same_query"),
                                  (forced, "forced"), (earlier, "earlier"), (gate_pick, "gate_of_row")):
                    sp.dma_start(dst[(slice(None),) * len(dst.shape)], d[name]).then_inc(const_in, 16)
                sp.wait_ge(table_in, 16)
                sp.sem_inc(values_used, 2)
                sp.sem_inc(group_used, 1)
                with sp.Fori(0, 2) as g:
                    for load in range(8):
                        i, slot = load % 4, load % 2
                        seq = g * 4 + i
                        if load < 2 or load >= 6:
                            sp.wait_ge(values_used, g * 4 + (load + 1 if load < 2 else load - 3))
                        else:
                            sp.wait_ge(tile_full, g * 32 + (8 * (load - 2) + 6))
                        sp.sem_inc(loads_begun, 1)
                        with sp.Fori(0, NB // 4) as p4:
                            _, at = nc.values_load_multi_w_load_instructions(
                                table[0:1, ds(seq * NPAGE + p4 * 4, 4)], engines=(mybir.EngineType.SP,), min_val=0,
                                max_val=d["pages_k"].shape[0] - 1)
                            for c, page in enumerate(at):
                                p = p4 * 4 + c
                                if load < 4:
                                    dst, src = pages[:, slot, ds(p * 384, 384)], d["pages_k"]
                                else:
                                    dst, src = pages[:, slot, ds(p * P, P)], d["pages_v"]
                                sp.dma_start(dst, src[ds(page, 1)].rearrange("a p n -> p (a n)"))\
                                    .then_inc(pages_in[slot], 16)
                        if load == 0:
                            sp.wait_ge(group_used, g + 1)
                            for dst, name in ((mask_dil, "mask_sdil"), (mask_win, "mask_swin"), (mask_new, "mask_snew")):
                                sp.dma_start(dst[:, :], d[name][ds(g, 1)].rearrange("a p n -> p (a n)"))\
                                    .then_inc(group_in, 16)
                            sp.dma_start(pick[:, :], d["token_of_row"][:, ds(g * P, P)]).then_inc(group_in, 16)

            @block.gpsimd
            def _(pool):
                pool.sem_inc(dil_used, 2)
                pool.memset(q_dil[:, :, :], 0.0).then_inc(q_zero, 1)
                pool.memset(q_nsa[:, :], 0.0).then_inc(q_zero, 1)
                pool.wait_ge(q_zero, 2)
                with pool.Fori(0, 2) as g:
                    for e in range(2):
                        half = slice(e * HD, (e + 1) * HD)
                        for hp in range(4):
                            dst = q_dil[half, hp, :].rearrange("p (i h q) -> p i h q", i=4, q=S)[:, :, 2 * hp + e, :]
                            src = m.zs[half, QA + hp, ds(g * 16, 16)].rearrange("p (i q) -> p i q", q=S)
                            pool.tensor_copy(dst, src).then_inc(q_ready, 1)
                        for r in range(4):
                            dst = q_nsa[half, :].rearrange("p (i e r q) -> p i e r q", i=4, e=2, q=S)[:, :, e, r, :]
                            src = m.zs[half, QB + r, ds(g * 16, 16)].rearrange("p (i q) -> p i q", q=S)
                            pool.tensor_copy(dst, src).then_inc(q_ready, 1)
                    for load in range(8):
                        i, slot = load % 4, load % 2
                        seq = g * 4 + i
                        if load < 2 or load >= 6:
                            pool.wait_ge(dil_used, g * 4 + (load + 1 if load < 2 else load - 3))
                        else:
                            pool.wait_ge(tile_full, g * 32 + (8 * (load - 2) + 2))
                        name = "past_ka" if load < 4 else "past_va"
                        pool.sem_inc(loads_begun, 1)
                        pool.dma_start(dil[:, slot, :], d[name][ds(seq, 1)].rearrange("a p h n -> p (a h n)"))\
                            .then_inc(dil_in[slot], 16)
                        if load < 2 or load >= 6:
                            pool.wait_ge(values_used, g * 4 + (load + 1 if load < 2 else load - 3))
                        else:
                            pool.wait_ge(tile_full, g * 32 + (8 * (load - 2) + 7))
                        src = d["past_kw"][ds(seq, 1)].rearrange("a p n -> p (a n)") if load < 4 else \
                            d["past_vw"][ds(seq, 1)].rearrange("a p h n -> p (a h n)")
                        pool.sem_inc(loads_begun, 1)
                        pool.dma_start(win[:, slot, :], src).then_inc(win_in[slot], 16)
                    pool.wait_ge(new_full, g + 1)

            @block.scalar
            def _(act):
                with act.Fori(0, 2) as g:
                    for i in range(4):
                        rows = slice(32 * i, 32 * i + 32)

                        def take(k):
                            act.wait_ge(tile_full, g * 32 + (8 * i + k + 1))
                            dst = {0: s_dil[rows, 0:448], 2: s_slc[rows, 0:512], 4: s_slc[rows, 1024:1536],
                                   6: s_win[rows, 0:512]}[k]
                            act.copy(dst, ps[rows, 2 + k % 4, 0:dst.shape[-1]]).then_inc(tile_act, 1)

                        turn = g * 8 + 2 * i
                        cmp.act_second(act, turn, 0)
                        cmp.act_second(act, turn + 1, 1)
                        cmp.act_exp(act, turn, 0)
                        cmp.act_exp(act, turn + 1, 1)
                        take(0)
                        if i > 0:
                            act.wait_ge(tile_full, g * 32 + 8 * i)
                        cmp.act_small(act, turn, 0, kc[:, :])
                        take(2)
                        take(4)
                        cmp.act_small(act, turn + 1, 1, vc[:, i, :])
                        take(6)
                    act.wait_ge(new_full, g * 1 + 1)
                    act.copy(s_dil[:, NKEY_A:], ps[:, 2, 0:SN])
                    act.copy(s_slc[:, PAST:], ps[:, 2, SN:2 * SN])
                    act.copy(s_win[:, 512:], ps[:, 2, 2 * SN:3 * SN])
                    act.copy(gates[:, :], ps[:, 3, 0:24]).then_inc(new_out, 1)

                    def exp(n, which, scores, scale):
                        act.wait_ge(low_ready, g * 4 + (n + 1))
                        act.activation(scores[:, :], scores[:, :], ACT.Exp, bias=low(which), scale=scale,
                                       accum_out=total(which)).then_inc(exp_ready, 1)

                    def take_turn(b):
                        _, scores, blocks, dst = turns[b]
                        act.wait_ge(turn_full, g * NTURN + (b + 1))
                        if b == 6:
                            act.wait_ge(low_ready, g * 4 + 4)
                        part = P if blocks[-1] * P + P <= scores.shape[1] else scores.shape[1] - blocks[-1] * P
                        bank = ps[:, 6 + b % 2, :]
                        if scores is s_cmp:
                            act.copy(dst[0:NCMP_S, :], bank[0:NCMP_S, 0:P]).then_inc(turn_out, 1)
                            return
                        whole = len(blocks) - (part < P)
                        if whole:
                            c = act.copy(dst[:, blocks[0]:blocks[0] + whole, :],
                                         bank[:, 0:whole * P].rearrange("p (a b) -> p a b", b=P))
                        if part < P:
                            c = act.copy(dst[0:part, blocks[-1], :], bank[0:part, whole * P:(whole + 1) * P])
                        c.then_inc(turn_out, 1)

                    exp(0, C, s_cmp, SCALE)
                    exp(1, A, s_dil, -1.0)
                    take_turn(0)
                    act.wait_ge(imp_full, g * 1 + 1)
                    act.copy(importance[:, :], ps[:, 4, 0:NBLK]).then_inc(imp_out, 1)
                    for b in range(1, 4):
                        take_turn(b)
                    exp(2, W, s_win, -1.0)
                    for b in range(4, 6):
                        take_turn(b)
                    exp(3, S_, s_slc, SCALE)
                    for b in range(6, NTURN):
                        take_turn(b)
                    act.wait_ge(values_used, g * 4 + 6)
                    act.copy(o_rows[:, 0:512], ps[:, 2, :]).then_inc(rows_out, 1)

            @block.tensor
            def _(pe):
                pe.wait_ge(const_in, 16 * 7)
                with pe.Fori(0, 2) as g:
                    pe.wait_ge(q_ready, g * 16 + 16)
                    for i in range(4):
                        slot, rows, cols = i % 2, slice(32 * i, 32 * i + 32), slice(32 * i, 32 * i + 32)
                        page = pages[:, slot, :].rearrange("p (n w) -> p n w", w=384)
                        rounds = g * 4 + (i // 2 + 1)

                        def chunks(kv):
                            v = page[:, :, kv * P:(kv + 1) * P].rearrange("p n (e s c) -> p e s n c", e=2, c=8)
                            return lambda s1: v[:, :, s1]

                        def room(k):
                            if k >= 4:
                                pe.wait_ge((tile_act, tile_dve)[k % 2], g * 16 + (4 * i + k // 2 - 1))
                            elif i > 0:
                                pe.wait_ge((tile_act, tile_dve)[k % 2], g * 16 + (4 * i + k // 2 - 1))

                        def dilated(k):
                            room(k)
                            for hp in range(4):
                                last = pe.matmul(ps[rows, 2 + k, 0:448], q_dil[:, hp, cols],
                                                 dil[:, slot, hp * NKEY_A + k * 448:hp * NKEY_A + k * 448 + 448],
                                                 start=(hp == 0), stop=(hp == 3))
                            last.then_inc(tile_full, 1)

                        pe.wait_ge(pages_in[slot], rounds * (16 * NB))
                        turn = g * 8 + 2 * i
                        cmp.pe_project(pe, 0, chunks(0))
                        cmp.pe_project(pe, 1, chunks(1))
                        pe.wait_ge(dil_in[slot], rounds * 16)
                        dilated(0)
                        dilated(1)
                        if i > 0:
                            pe.wait_ge(cmp.small_out, turn)
                        cmp.pe_small(pe, turn, 0)
                        for k in range(2, 6):
                            room(k)
                            pe.matmul(ps[rows, 2 + k % 4, :], q_nsa[:, cols], page[:, 4 * (k - 2):4 * (k - 1), 256:384],
                                      start=True, stop=True).then_inc(tile_full, 1)
                        pe.wait_ge(cmp.small_out, turn + 1)
                        cmp.pe_small(pe, turn + 1, 1)
                        room(6)
                        pe.wait_ge(win_in[slot], rounds * 16)
                        pe.matmul(ps[rows, 4, :], q_nsa[:, cols], win[:, slot, :], start=True, stop=True)\
                            .then_inc(tile_full, 1)
                        room(7)
                        pe.matmul(ps[rows, 5, 0:NCMP_S], q_nsa[:, cols], kc[:, :], start=True, stop=True)\
                            .then_inc(tile_full, 1)
                    pe.wait_ge(tile_act, g * 16 + 16)
                    pe.wait_ge(tile_dve, g * 16 + 16)
                    pe.wait_ge(cmp.small_out, g * 8 + 8)
                    for hp in range(4):
                        pe.matmul(ps[:, 2, 0:SN], q_dil[:, hp, :], m.zs[:, KA + hp, :], start=(hp == 0), stop=(hp == 3))
                    pe.matmul(ps[:, 2, SN:2 * SN], q_nsa[:, :], m.zs[:, KS, :], start=True, stop=True)
                    pe.matmul(ps[:, 2, 2 * SN:3 * SN], q_nsa[:, :], m.zs[:, KW, :], start=True, stop=True)
                    pe.wait_ge(group_in, g * 64 + 64)
                    pe.matmul(ps[:, 3, 0:24], pick[:, :], m.gates[:, :], start=True, stop=True).then_inc(new_full, 1)

                    def turn_bank(b):
                        need, scores, blocks, _ = turns[b]
                        pe.wait_ge(prob_ready, g * 5 + need)
                        if b >= 2:
                            pe.wait_ge(turn_out, g * NTURN + (b - 1))
                        for c, k in enumerate(blocks):
                            n = min(P, scores.shape[1] - k * P)
                            last = pe.transpose(ps[0:n, 6 + b % 2, c * P:(c + 1) * P], scores[:, k * P:k * P + n],
                                                m.ident[:, :])
                        last.then_inc(turn_full, 1)

                    turn_bank(0)
                    pe.wait_ge(turn_out, g * NTURN + 1)
                    pe.matmul(ps[:, 4, 0:NBLK], t_cmp[0:NCMP_S, :], overlap[:, :], start=True, stop=True)\
                        .then_inc(imp_full, 1)
                    pe.wait_ge(imp_out, g * 1 + 1)
                    pe.matmul(ps[:, 5, 0:NBLK], same[:, :], importance[:, :], start=True, stop=True)\
                        .then_inc(points_full, 1)
                    def dilated_values(i):
                        slot, rows = i % 2, slice(32 * i, 32 * i + 32)
                        pe.wait_ge(dil_in[slot], (g * 4 + (i // 2 + 3)) * 16)
                        for k in range(7):
                            pe.matmul(ps[rows, 2, :], t_dil[:, k, rows], dil[:, slot, k * 512:(k + 1) * 512],
                                      start=(k == 0), stop=False)
                        pe.matmul(ps[rows, 2, :], t_dil[0:SN, 7, rows], m.vas[:, :], start=False, stop=True)\
                            .then_inc(dil_used, 1)

                    def nsa_values(i):
                        slot, rows = i % 2, slice(32 * i, 32 * i + 32)
                        rounds = g * 4 + (i // 2 + 3)
                        out = ps[rows, 3, 0:P]
                        pe.matmul(out, t_cmpg[0:NCMP_S, rows], vc[:, i, :], start=True, stop=False)
                        pe.matmul(out, t_slc[0:SN, NB, rows], m.vbs[:, 0:P], start=False, stop=False)
                        pe.matmul(out, t_win[0:SN, 4, rows], m.vbs[:, P:2 * P], start=False, stop=False)
                        pe.wait_ge(pages_in[slot], rounds * (16 * NB))
                        for k in range(NB):
                            pe.matmul(out, t_slc[:, k, rows], pages[:, slot, k * P:(k + 1) * P], start=False, stop=False)
                        pe.wait_ge(win_in[slot], rounds * 16)
                        for k in range(4):
                            last = pe.matmul(out, t_win[:, k, rows], win[:, slot, k * P:(k + 1) * P], start=False,
                                             stop=(k == 3))
                        last.then_inc(values_used, 1)

                    for b in range(1, 4):
                        turn_bank(b)
                    pe.wait_ge(turn_out, g * NTURN + 4)
                    for i in range(2):
                        dilated_values(i)
                    for b in range(4, NTURN):
                        turn_bank(b)
                    pe.wait_ge(turn_out, g * NTURN + NTURN)
                    for i in range(4):
                        nsa_values(i)
                        if i < 2:
                            dilated_values(i + 2)
                    pe.wait_ge(rows_out, g * 2 + 2)
                    for f in range(5):
                        last = pe.transpose(ps[:, 4 + f // 4, (f % 4) * P:(f % 4 + 1) * P], o_rows[:, f * P:(f + 1) * P],
                                            m.ident[:, :])
                    last.then_inc(so_full, 1)
                    pe.wait_ge(so_out, g * 10 + 10)

            @block.vector
            def _(dve):
                step = Steps(dve, dve_step)
                dve.wait_ge(const_in, 16 * 7)
                with dve.Fori(0, 2) as g:
                    PER = 67
                    first, step.offset = step.n, g * PER
                    for i in range(4):
                        rows = slice(32 * i, 32 * i + 32)

                        def take(k):
                            dve.wait_ge(tile_full, g * 32 + (8 * i + k + 1))
                            dst = {1: s_dil[rows, 448:896], 3: s_slc[rows, 512:1024], 5: s_slc[rows, 1536:2048],
                                   7: s_cmp[rows, :]}[k]
                            dve.tensor_copy(dst, ps[rows, 2 + k % 4, 0:dst.shape[-1]]).then_inc(tile_dve, 1)

                        turn = g * 8 + 2 * i
                        cmp.dve_inner(dve, step, turn, 0)
                        cmp.dve_inner(dve, step, turn + 1, 1)
                        cmp.dve_hidden(dve, step, turn, 0)
                        cmp.dve_hidden(dve, step, turn + 1, 1)
                        take(1)
                        take(3)
                        take(5)
                        take(7)
                    dve.wait_ge(tile_dve, g * 16 + 16)
                    step.done(dve.tensor_reduce(low(C), s_cmp[:, :], AX_X, ALU.max))
                    step.wait()
                    dve.tensor_scalar(low(C), low(C), -SCALE, None, ALU.mult).then_inc(low_ready, 1)
                    dve.wait_ge(group_in, g * 64 + 64)
                    dve.wait_ge(new_out, g * 1 + 1)
                    dve.wait_ge(tile_act, g * 16 + 16)
                    dve.sem_inc(begun, 1)
                    dve.tensor_tensor_reduce(s_dil[:, :], s_dil[:, :], mask_dil[:, :], -SCALE, 3e38, ALU.add,
                                             ALU.min, low(A)).then_inc(low_ready, 1)
                    step.done(dve.tensor_tensor(gates[:, :], gates[:, :], gate_pick[:, :], ALU.mult))
                    step.wait()
                    step.done(dve.tensor_reduce(gate3[:, :], gates[:, :].rearrange("p (b h) -> p b h", b=3),
                                                AX_X, ALU.add))
                    dve.wait_ge(exp_ready, g * 4 + 1)
                    step.done(dve.reciprocal(factor(C), total(C)))
                    step.wait()
                    dve.tensor_scalar(s_cmp[:, :], s_cmp[:, :], factor(C), None, ALU.mult).then_inc(prob_ready, 1)
                    dve.wait_ge(turn_full, g * NTURN + 1)
                    dve.tensor_scalar(s_cmp[:, :], s_cmp[:, :], gate3[:, 0:1], None, ALU.mult).then_inc(prob_ready, 1)
                    dve.wait_ge(exp_ready, g * 4 + 2)
                    step.done(dve.reciprocal(factor(A), total(A)))
                    step.wait()
                    dve.tensor_scalar(s_dil[:, :], s_dil[:, :], factor(A), None, ALU.mult).then_inc(prob_ready, 1)
                    dve.wait_ge(points_full, g * 1 + 1)
                    step.done(dve.tensor_tensor(points[:, :], ps[:, 5, 0:NBLK], forced[:, :], ALU.add))
                    step.wait()
                    other = points[:, :].unsqueeze(1).broadcast_to([P, NBLK, NBLK])
                    this = points[:, :].unsqueeze(2).broadcast_to([P, NBLK, NBLK])
                    step.done(dve.tensor_tensor(beats, other, this, ALU.is_gt))
                    step.done(dve.tensor_tensor(ties, other, this, ALU.is_equal))
                    step.wait()
                    step.done(dve.tensor_tensor(ties, ties, earlier[:, :].rearrange("p (j i) -> p j i", i=NBLK), ALU.mult))
                    step.wait()
                    step.done(dve.tensor_tensor(beats, beats, ties, ALU.add))
                    step.wait()
                    step.done(dve.tensor_reduce(drop[:, :], beats, AX_X, ALU.add))
                    step.wait()
                    step.done(dve.tensor_scalar(drop[:, :], drop[:, :], TOPK - 0.5, NEG, ALU.is_gt, ALU.mult))
                    dve.sem_inc(begun, 1)
                    dve.tensor_tensor_reduce(s_win[:, :], s_win[:, :], mask_win[:, :], -SCALE, 3e38, ALU.add,
                                             ALU.min, low(W)).then_inc(low_ready, 1)
                    step.done(dve.tensor_tensor(s_slc[:, PAST:], s_slc[:, PAST:], mask_new[:, :], ALU.add))
                    step.wait()
                    dve.sem_inc(group_used, 1)
                    past = s_slc[:, 0:PAST].rearrange("p (b t) -> p b t", t=64)
                    step.done(dve.tensor_tensor(past, past, drop[:, 0:32].unsqueeze(2).broadcast_to([P, 32, 64]),
                                                ALU.add))
                    step.wait()
                    step.done(dve.tensor_reduce(low(S_), s_slc[:, :], AX_X, ALU.max))
                    step.wait()
                    dve.wait_ge(exp_ready, g * 4 + 3)
                    step.done(dve.reciprocal(factor(W), total(W)))
                    step.wait()
                    step.done(dve.tensor_tensor(factor(W), factor(W), gate3[:, 2:3], ALU.mult))
                    step.wait()
                    dve.tensor_scalar(low(S_), low(S_), -SCALE, None, ALU.mult).then_inc(low_ready, 1)
                    dve.tensor_scalar(s_win[:, :], s_win[:, :], factor(W), None, ALU.mult).then_inc(prob_ready, 1)
                    dve.wait_ge(exp_ready, g * 4 + 4)
                    step.done(dve.reciprocal(factor(S_), total(S_)))
                    step.wait()
                    step.done(dve.tensor_tensor(factor(S_), factor(S_), gate3[:, 1:2], ALU.mult))
                    step.wait()
                    dve.tensor_scalar(s_slc[:, :], s_slc[:, :], factor(S_), None, ALU.mult).then_inc(prob_ready, 1)
                    dve.wait_ge(values_used, g * 4 + 6)
                    dve.tensor_copy(o_rows[:, 512:640], ps[:, 3, 0:P]).then_inc(rows_out, 1)
                    dve.wait_ge(so_full, g + 1)
                    for e in range(2):
                        half = slice(e * HD, (e + 1) * HD)
                        def new(tiles):
                            return m.oa[half, tiles, ds(g * 16 + T, 16)].rearrange("p r (i q) -> p r i q", q=S)
                        for hp in range(4):
                            a = ps[half, 4, hp * P:(hp + 1) * P].rearrange("p (i h q) -> p h i q", i=4, q=S)
                            dve.tensor_copy(new(slice(hp, hp + 1)), a[:, 2 * hp + e:2 * hp + e + 1]).then_inc(so_out, 1)
                        b = ps[half, 5, 0:P].rearrange("p (i e r q) -> p e r i q", i=4, e=2, q=S)[:, e]
                        dve.tensor_copy(new(slice(4, 8)), b).then_inc(so_out, 1)
                    assert step.n - first == PER
                step.offset = None




def finish(nc, d, m, sem):
    with ExitStack() as mine:
        def sb(name, shape, dt=F32):
            return mine.enter_context(nc.sbuf_tensor(name, shape, dt))

        ps = m.ps
        x, h = sb("fx", [P, KD, NT]), sb("fh", [P, KD, NT])
        ring = sb("ring", [P, RING, KD * P])
        mean, root, scratch = sb("fmean", [P, NT]), sb("froot", [P, NT]), sb("fscratch", [P, NT])
        merged = sb("merged", [P, KD, NT])
        q_mem, o_mem = merged[:, 0:MH, :], merged[:, MH:2 * MH, :]
        wide = sb("wide", [P, 2 * NSEQ * 1024])
        km = wide[:, 0:NSEQ * 1024].rearrange("p (n h t) -> p n h t", n=NSEQ, h=MH)
        vm = wide[:, NSEQ * 1024:].rearrange("p (n k f) -> p n k f", n=NSEQ, k=2)
        act_a = wide[:, 0:KF * NT].rearrange("p (f t) -> p f t", f=KF)
        prob = sb("m_prob", [P, 2, QT, MTOK])
        prob_t = sb("m_prob_t", [P, 2, T])
        low, total = sb("m_low", [P, QT]), sb("m_total", [P, QT])
        CW = 2 + T + NSEQ * 6
        u, c = sb("u", [P, 2, CW]), sb("c", [P, 2, CW])
        e_a, e_b = sb("e_a", [P, CW]), sb("e_b", [P, NT])
        s_keys = e_a[:, 0:MTOK].rearrange("p (k r) -> p k r", k=2)
        s_prob_t = e_a[:, MTOK:2 * MTOK].rearrange("p (k r) -> p k r", k=2)
        s_prob = e_b[:, 0:MTOK]
        w_conv, past = sb("w_conv_sb", [P, 2 * KF, 4]), sb("ffn_past_sb", [P, 2 * KF, 16])
        last_u = sb("last_u", [P, 2 * KF, 18])
        C0 = CW - 2

        T_O, T_Q, T_M, T_UP, T_DOWN = 32, 40, 44, 52, 96
        N_O, N_Q, N_M, N_UP, N_DOWN, N_ALL = 24, 32, 36, 40, 84, 108

        x_in, past_in, kv_in = sem("fx_in"), sem("past_in"), sem("kv_in")
        chunk_in = [sem(f"chunk_in{i}") for i in range(RING)]
        acc_full, acc_out = sem("acc_full"), [sem("acc_out0"), sem("acc_out1")]
        q_full, q_out = sem("q_full"), sem("q_out")
        s_low, s_exp, s_soft = sem("s_low"), sem("s_exp"), sem("s_soft")
        down_part = sem("down_part")
        x_ready, squared, sum_full = sem("x_ready"), sem("fsquared"), sem("fsum_full")
        v_ready, y_ready, h_ready = sem("fmean_ready"), sem("froot_ready"), sem("fh_ready")
        gate_ready, merged_ready = sem("fgate_ready"), sem("merged_ready")
        q_ready, q_square = sem("q_mem_ready"), sem("q_square")
        ms_full, ms_low, ms_exp, ms_prob = sem("ms_full"), sem("ms_low"), sem("ms_exp"), sem("ms_prob")
        mt_full, mt_out, mo_full, mo_out = sem("mt_full"), sem("mt_out"), sem("mo_full"), sem("mo_out")
        past_put, rows_kept, conv_done = sem("past_put"), sem("rows_kept"), sem("conv_done")
        silu_exp, a_ready, y_done = sem("silu_exp"), sem("a_ready"), sem("y_done")
        edge_zero = sem("edge_zero")
        dve_step = sem("finish_dve_step")
        stored = sem("finish_stored")

        def pair(t):
            return ps[:, 2 * (t % 2):2 * (t % 2) + 2, 0:HALF]

        with nc.Block() as block:
            @block.sync
            def _(sp):
                def load(chunk, slot):
                    src = d["w_close"][ds(chunk, 1)].rearrange("a p k n -> p (a k n)")
                    sp.dma_start(ring[:, slot, :], src).then_inc(chunk_in[slot], 16)

                sp.dma_start(x[:, :, :], d["x"]).then_inc(x_in, 16)
                for i in range(RING):
                    load(i, i)
                sp.dma_start(w_conv[:, :, :], d["w_conv"]).then_inc(past_in, 16)
                sp.dma_start(past[:, :, :], d["ffn_past"].rearrange("p f n r -> p f (n r)")).then_inc(past_in, 16)
                with sp.Fori(0, 2) as i:
                    for n in range(12):
                        sp.wait_ge(acc_full, i * 16 + (4 * (n // 3) + (1, 2, 4)[n % 3]))
                        load(i * 12 + (n + RING), n % 4)
                with sp.Fori(0, 2) as i:
                    for n in range(4):
                        sp.wait_ge(acc_full, i * 4 + (T_O + n + 1))
                        load(i * 4 + (N_O + n + RING), n)
                for n in range(4):
                    sp.wait_ge(acc_full, T_Q + n + 1)
                    load(N_Q + n + RING, n)
                for n in range(4):
                    sp.wait_ge(acc_full, T_M + 2 * n + 2)
                    load(N_M + n + RING, n)
                with sp.Fori(0, KF // 2) as i:
                    for n in range(4):
                        sp.wait_ge(acc_full, i * 4 + (T_UP + n + 1))
                        load(i * 4 + (N_UP + n + RING), n)
                for n in range(N_ALL - N_DOWN - RING):
                    if n % 3 == 2:
                        sp.wait_ge(acc_full, T_DOWN + n // 3 + 1)
                    else:
                        sp.wait_ge(down_part, n // 3 * 2 + n % 3 + 1)
                    load(N_DOWN + n + RING, n % 4)
                sp.wait_ge(rows_kept, 2 * KF)
                sp.dma_start(d["o_conv"], last_u[:, :, :]).then_inc(stored, 16)
                sp.wait_ge(y_done, KD)
                sp.dma_start(d["o_y"], x[:, :, :]).then_inc(stored, 16)
                sp.wait_ge(stored, 32)

            @block.gpsimd
            def _(pool):
                for p in range(2):
                    pool.memset(u[:, p, 0:2], 0.0).then_inc(edge_zero, 1)
                pool.wait_ge(past_in, 32)
                with pool.Fori(0, KF) as f:
                    for p in range(2):
                        heads = u[:, p, 2 + T:].rearrange("p (n s) -> p n s", s=6)
                        src = one(past, f + p * KF, slice(0, 16)).rearrange("p (n r) -> p n r", r=2)
                        pool.tensor_copy(heads[:, :, 0:2], src).then_inc(past_put, 1)
                    for p in range(2):
                        pool.wait_ge(acc_out[p], f * 1 + (T_UP // 2 + 1))
                        dst = one(last_u, f + p * KF, slice(0, 18))
                        heads = u[:, p, 2 + T:].rearrange("p (n s) -> p n s", s=6)
                        pool.tensor_copy(dst[:, 0:2], u[:, p, T:T + 2])
                        pool.tensor_copy(dst[:, 2:18].rearrange("p (n r) -> p n r", r=2), heads[:, :, 4:6])\
                            .then_inc(rows_kept, 1)
                    pool.wait_ge(conv_done, f * 2 + 2)

            @block.scalar
            def _(act):
                act.dma_start(km.rearrange("p n h t -> p n (h t)"), d["past_km"].rearrange("n p h t -> p n (h t)"))\
                    .then_inc(kv_in, 16)
                act.dma_start(vm.rearrange("p n k f -> p n (k f)"), d["past_vm"].rearrange("n p k f -> p n (k f)"))\
                    .then_inc(kv_in, 16)

                def norm(n, ready, first):
                    for k in range(KD):
                        if ready is not None:
                            act.wait_ge(ready, first + k + 1)
                        act.activation(h[:, k, :], x[:, k, :], ACT.Square).then_inc(squared, 1)
                    reciprocal_root(None, act, "act", mean[:, :], root[:, :], None, v_ready, y_ready, n)

                act.wait_ge(x_in, 16)
                norm(0, None, 0)
                with act.Fori(0, 2) as i:
                    for n in range(4):
                        for b, e in ((0, e_a), (1, e_b)):
                            act.wait_ge(acc_full, i * 16 + (4 * n + b + 1))
                            if n > 0:
                                act.wait_ge(merged_ready, i * 4 + n)
                            act.activation(halves(e[:, 0:NT]), pair(b), ACT.Exp, scale=-1.0).then_inc(acc_out[b], 1)
                    act.wait_ge(merged_ready, i * 4 + 4)
                act.wait_ge(acc_full, T_Q)
                norm(1, x_ready, 0)
                for j in range(MH):
                    act.wait_ge(acc_full, T_Q + j + 1)
                    act.copy(halves(q_mem[:, j, :]), pair(j))
                    act.activation(halves(o_mem[:, j, :]), pair(j), ACT.Square).then_inc(acc_out[j % 2], 1)
                for j in range(MH):
                    reciprocal_root(None, act, "act", mean[:, :], root[:, :], None, v_ready, y_ready, 2 + j)

                def exps(j):
                    act.wait_ge(ms_low, j + 1)
                    if j >= 2:
                        act.wait_ge(mt_full, j - 1)
                    for i in range(QT):
                        last = act.activation(prob[:, j % 2, i, :], ps[:, 4 + i // 2, (i % 2) * MTOK:(i % 2 + 1) * MTOK],
                                              ACT.Exp, bias=low[:, i:i + 1], scale=MSCALE, accum_out=total[:, i:i + 1])
                    last.then_inc(ms_exp, 1)

                def take_turned(j):
                    act.wait_ge(mt_full, j + 1)
                    if j >= 1:
                        act.wait_ge(mo_full, j)
                    act.copy(prob_t[:, 0, :], ps[:, 6, :])
                    act.copy(prob_t[:, 1, :], ps[:, 7, :]).then_inc(mt_out, 1)

                def take_output(j):
                    act.wait_ge(mo_full, j + 1)
                    act.copy(o_mem[:, j, 0:T], ps[:, j % 2, :]).then_inc(mo_out, 1)

                two = lambda v: v.rearrange("p (a b) -> p a b", b=P)
                exps(0)
                act.wait_ge(q_full, 1)
                act.copy(s_keys, two(ps[:, 2, 0:MTOK])).then_inc(q_out, 1)
                exps(1)
                take_turned(0)
                take_output(0)
                exps(2)
                take_turned(1)
                act.wait_ge(q_full, 2)
                act.copy(s_prob, ps[:, 3, 0:MTOK]).then_inc(q_out, 1)
                take_output(1)
                act.wait_ge(s_low, 1)
                act.activation(s_prob, s_prob, ACT.Exp, bias=low[:, 0:1], scale=MSCALE, accum_out=total[:, 0:1])\
                    .then_inc(s_exp, 1)
                exps(3)
                take_turned(2)
                act.wait_ge(q_full, 3)
                act.copy(s_prob_t, two(ps[:, 3, 0:MTOK])).then_inc(q_out, 1)
                take_output(2)
                take_turned(3)
                act.wait_ge(q_full, 4)
                out = ps[:, 2, 0:P].rearrange("p (n h q) -> p n h q", n=NSEQ, h=MH)
                for j in range(MH):
                    last = act.copy(o_mem[:, j, T:NT].rearrange("p (n q) -> p n q", q=S), out[:, :, j, :])
                last.then_inc(q_out, 1)
                take_output(3)
                norm(6, x_ready, KD)
                act.wait_ge(edge_zero, 2)
                with act.Fori(0, KF) as f:
                    for p in range(2):
                        act.wait_ge(acc_full, f * 2 + (T_UP + p + 1))
                        act.wait_ge(past_put, f * 2 + (p + 1))
                        act.copy(u[:, p, 2:2 + HALF], ps[:, 2 * p, 0:HALF])
                        act.copy(u[:, p, 2 + HALF:2 + T], ps[:, 2 * p + 1, 0:T - HALF])
                        act.copy(u[:, p, 2 + T:].rearrange("p (n s) -> p n s", s=6)[:, :, 2:6],
                                 ps[:, 2 * p + 1, T - HALF:HALF].rearrange("p (n s) -> p n s", s=S))\
                            .then_inc(acc_out[p], 1)
                    act.wait_ge(conv_done, f * 2 + 1)
                    act.wait_ge(a_ready, f + 1)
                    act.activation(e_a[:, 0:C0], c[:, 0, 0:C0], ACT.Exp, scale=-1.0).then_inc(silu_exp, 1)
                    act.wait_ge(conv_done, f * 2 + 2)
                    act.wait_ge(rows_kept, f * 2 + 2)

            @block.tensor
            def _(pe):
                def sums(rhs, first_bank=4, k_tiles=KD, step=None):
                    for k in range(k_tiles):
                        if step is not None:
                            pe.wait_ge(squared, step + k + 1)
                        for a in range(2):
                            last = pe.matmul(ps[:, first_bank + a, 0:HALF], m.ones[:, :],
                                             rhs(k)[:, a * HALF:(a + 1) * HALF], start=(k == 0), stop=(k == k_tiles - 1))
                    last.then_inc(sum_full, 1)

                def tile(p, parts, rhs):
                    k, total_k = 0, sum(n for _, _, n in parts)
                    for slot, w0, n in parts:
                        for w in range(n):
                            for a in range(2):
                                last = pe.matmul(ps[:, 2 * p + a, 0:HALF], ring[:, slot, (w0 + w) * P:(w0 + w + 1) * P],
                                                 rhs(k)[:, a * HALF:(a + 1) * HALF],
                                                 start=(k == 0), stop=(k == total_k - 1))
                            k += 1
                        if k < total_k:
                            last.then_inc(down_part, 1)
                    last.then_inc(acc_full, 1)

                sums(lambda k: h[:, k, :], step=0)
                pe.wait_ge(h_ready, KD)
                with pe.Fori(0, 2) as i:
                    for n in range(4):
                        for b in range(4):
                            chunk, p = 3 * n + min(b, 2), b % 2
                            if b < 3:
                                pe.wait_ge(chunk_in[chunk % 4], (i * 3 + (chunk // 4 + 1)) * 16)
                            if n + b // 2 > 0:
                                pe.wait_ge(acc_out[p], i * 8 + (2 * n + b // 2))
                            if b < 2:
                                tile(p, [(chunk % 4, 0, 8)], lambda k: h[:, k, :])
                            else:
                                tile(p, [(chunk % 4, 4 * (b - 2), 4)], lambda k: m.oa[:, 4 * (b - 2) + k, :])
                    for p in range(2):
                        pe.wait_ge(acc_out[p], i * 8 + 8)
                pe.wait_ge(merged_ready, KD)
                with pe.Fori(0, 2) as i:
                    for n in range(4):
                        pe.wait_ge(chunk_in[n], (i + (N_O // 4 + 1)) * 16)
                        pe.wait_ge(acc_out[n % 2], i * 2 + (T_O // 2 + n // 2))
                        tile(n % 2, [(n, 0, 8)], lambda k: merged[:, k, :])
                sums(lambda k: h[:, k, :], step=KD)
                for n in range(MH):
                    pe.wait_ge(h_ready, 2 * KD)
                    pe.wait_ge(chunk_in[n], (N_Q // 4 + 1) * 16)
                    pe.wait_ge(acc_out[n % 2], (T_Q + n) // 2)
                    tile(n % 2, [(n, 0, 8)], lambda k: h[:, k, :])
                for j in range(MH):
                    pe.wait_ge(acc_out[j % 2], (T_Q + j) // 2 + 1)
                    pe.wait_ge(v_ready, 2 + j)
                    sums(lambda k: o_mem[:, j, :], k_tiles=1)
                def head_scores(j):
                    pe.wait_ge(q_ready, MH)
                    if j >= 1:
                        pe.wait_ge(ms_exp, j)
                    for qt in range(QT):
                        last = pe.matmul(ps[:, 4 + qt // 2, (qt % 2) * MTOK:(qt % 2 + 1) * MTOK],
                                         q_mem[:, j, qt * P:(qt + 1) * P], m.mk[:, j, :], start=True, stop=True)
                    last.then_inc(ms_full, 1)

                def head_turn(j):
                    pe.wait_ge(ms_prob, j + 1)
                    if j >= 1:
                        pe.wait_ge(mt_out, j)
                    for k in range(2):
                        for qt in range(QT):
                            last = pe.transpose(ps[:, 6 + k, qt * P:(qt + 1) * P], prob[:, j % 2, qt, k * P:(k + 1) * P],
                                                m.ident[:, :])
                    last.then_inc(mt_full, 1)

                def head_values(j):
                    pe.wait_ge(mt_out, j + 1)
                    if j >= 2:
                        pe.wait_ge(mo_out, j - 1)
                    for k in range(2):
                        last = pe.matmul(ps[:, j % 2, :], m.mv[:, k, j * P:(j + 1) * P], prob_t[:, k, :],
                                         start=(k == 0), stop=(k == 1))
                    last.then_inc(mo_full, 1)

                head_scores(0)
                pe.wait_ge(kv_in, 32)
                for k in range(2):
                    for n in range(NSEQ):
                        for j in range(MH):
                            at = k * P + n * 16 + j * 4
                            last = pe.matmul(ps[:, 2, at:at + 4], km[:, n, j, k * P:(k + 1) * P],
                                             q_mem[:, j, T + 4 * n:T + 4 * n + 4], start=True, stop=True)
                last.then_inc(q_full, 1)
                head_scores(1)
                head_turn(0)
                head_values(0)
                head_scores(2)
                head_turn(1)
                pe.wait_ge(q_out, 1)
                for k in range(2):
                    last = pe.transpose(ps[:, 3, k * P:(k + 1) * P], s_keys[:, k, :], m.ident[:, :])
                last.then_inc(q_full, 1)
                head_values(1)
                head_scores(3)
                head_turn(2)
                pe.wait_ge(s_soft, 1)
                for k in range(2):
                    last = pe.transpose(ps[:, 3, k * P:(k + 1) * P], s_prob[:, k * P:(k + 1) * P], m.ident[:, :])
                last.then_inc(q_full, 1)
                head_values(2)
                pe.wait_ge(q_out, 3)
                for n in range(NSEQ):
                    for j in range(MH):
                        at = n * 16 + j * 4
                        for k in range(2):
                            last = pe.matmul(ps[:, 2, at:at + 4], vm[:, n, k, j * P:(j + 1) * P],
                                             s_prob_t[:, k, at:at + 4], start=(k == 0), stop=(k == 1))
                last.then_inc(q_full, 1)
                head_turn(3)
                head_values(3)
                pe.wait_ge(mo_out, MH)
                pe.wait_ge(q_out, 4)
                for n in range(KD):
                    pe.wait_ge(chunk_in[n // 2], (N_M // 4 + 1) * 16)
                    pe.wait_ge(acc_out[n % 2], (T_M + n) // 2)
                    tile(n % 2, [(n // 2, 4 * (n % 2), 4)], lambda k: o_mem[:, k, :])
                sums(lambda k: h[:, k, :], step=2 * KD)
                pe.wait_ge(h_ready, 3 * KD)
                with pe.Fori(0, KF // 2) as i:
                    for n in range(4):
                        pe.wait_ge(chunk_in[n], (i + (N_UP // 4 + 1)) * 16)
                        pe.wait_ge(acc_out[n % 2], i * 2 + (T_UP // 2 + n // 2))
                        tile(n % 2, [(n, 0, 8)], lambda k: h[:, k, :])
                pe.wait_ge(a_ready, KF + 1)
                with pe.Fori(0, 2) as i:
                    for n in range(4):
                        for b in range(3):
                            chunk = 3 * n + b
                            pe.wait_ge(chunk_in[chunk % 4], (i * 3 + (N_DOWN // 4 + chunk // 4 + 1)) * 16)
                        pe.wait_ge(acc_out[n % 2], i * 2 + (T_DOWN // 2 + n // 2))
                        tile(n % 2, [((3 * n + b) % 4, 0, 8 if b < 2 else KF - 16) for b in range(3)],
                             lambda k: act_a[:, k, :])

            @block.vector
            def _(dve):
                step = Steps(dve, dve_step)

                def root_of(n, divisor):
                    dve.wait_ge(sum_full, n + 1)
                    dve.tensor_scalar(halves(mean[:, :]), ps[:, 4:6, 0:HALF], 1.0 / divisor, EPS, ALU.mult, ALU.add)\
                        .then_inc(v_ready, 1)
                    dve.wait_ge(v_ready, n + 1)
                    reciprocal_root(dve, None, "dve", mean[:, :], root[:, :], scratch[:, :], v_ready, y_ready, n, step)

                def norm(n, which, model):
                    root_of(n, D)
                    for k in range(KD):
                        dve.scalar_tensor_tensor(out=h[:, k, :], in0=x[:, k, :],
                                                 scalar=m.g_model[:, model * KD + k:model * KD + k + 1],
                                                 in1=root[:, :], op0=ALU.mult, op1=ALU.mult).then_inc(h_ready, 1)
                    dve.wait_ge(h_ready, (which + 1) * KD)

                def add_to_x(k, full, t):
                    dve.wait_ge(acc_full, full)
                    return dve.tensor_tensor(halves(k), halves(k), pair(t), ALU.add)

                dve.wait_ge(x_in, 16)
                norm(0, 0, 0)
                with dve.Fori(0, 2) as i:
                    PER = 4 * 5
                    first, step.offset = step.n, i * PER
                    for n in range(4):
                        for b, e in ((0, e_a), (1, e_b)):
                            dve.wait_ge(acc_out[b], i * 8 + (2 * n + 1))
                            step.done(dve.tensor_scalar(e[:, 0:NT], e[:, 0:NT], 1.0, None, ALU.add))
                            step.wait()
                            step.done(dve.reciprocal(e[:, 0:NT], e[:, 0:NT]))
                            step.wait()
                        dst = one(merged, i * 4 + n, slice(0, NT))
                        for b, e, to in ((0, e_a[:, 0:NT], dst), (1, e_b[:, :], e_b[:, :])):
                            dve.wait_ge(acc_full, i * 16 + (4 * n + b + 3))
                            dve.tensor_tensor(halves(to), pair(b), halves(e), ALU.mult).then_inc(acc_out[b], 1)
                        dve.wait_ge(acc_out[0], i * 8 + (2 * n + 2))
                        dve.wait_ge(acc_out[1], i * 8 + (2 * n + 2))
                        step.done(dve.tensor_tensor(dst, dst, e_b[:, :], ALU.add))
                        step.wait()
                        dve.sem_inc(merged_ready, 1)
                    assert step.n - first == PER
                    step.n = first + 2 * PER
                step.offset = None
                with dve.Fori(0, 2) as i:
                    for n in range(4):
                        add_to_x(one(x, i * 4 + n, slice(0, NT)), i * 4 + (T_O + n + 1), n).then_inc(acc_out[n % 2], 1)
                        dve.wait_ge(acc_out[n % 2], i * 2 + (T_O // 2 + n // 2 + 1))
                        dve.sem_inc(x_ready, 1)
                norm(1, 1, 2)
                for j in range(MH):
                    root_of(2 + j, MHD)
                    dve.wait_ge(acc_out[j % 2], (T_Q + j) // 2 + 1)
                    dve.scalar_tensor_tensor(out=q_mem[:, j, :], in0=q_mem[:, j, :], scalar=m.g_memh[:, 1:2],
                                             in1=root[:, :], op0=ALU.mult, op1=ALU.mult).then_inc(q_ready, 1)
                    dve.wait_ge(q_ready, j + 1)

                def softmax(src, dst, prob_rows, low_ready, exp_ready, done, count):
                    n = len(prob_rows)
                    step.done(dve.tensor_reduce(dst, src, AX_X, ALU.max))
                    step.wait()
                    dve.tensor_scalar(low[:, 0:n], low[:, 0:n], -MSCALE, None, ALU.mult).then_inc(low_ready, 1)
                    dve.wait_ge(exp_ready, count)
                    step.done(dve.reciprocal(total[:, 0:n], total[:, 0:n]))
                    step.wait()
                    for i, row in enumerate(prob_rows):
                        last = dve.tensor_scalar(row, row, total[:, i:i + 1], None, ALU.mult)
                    last.then_inc(done, 1)
                    dve.wait_ge(done, count)

                def head_softmax(j):
                    dve.wait_ge(ms_full, j + 1)
                    softmax(ps[:, 4:6, :].rearrange("p a (b k) -> p a b k", b=2),
                            low[:, 0:QT].rearrange("p (a b) -> p a b", b=2),
                            [prob[:, j % 2, i, :] for i in range(QT)], ms_low, ms_exp, ms_prob, j + 1)

                for j in range(3):
                    head_softmax(j)
                dve.wait_ge(q_out, 2)
                softmax(s_prob, low[:, 0:1], [s_prob], s_low, s_exp, s_soft, 1)
                head_softmax(3)
                for n in range(KD):
                    add_to_x(x[:, n, :], T_M + n + 1, n).then_inc(acc_out[n % 2], 1)
                    dve.wait_ge(acc_out[n % 2], (T_M + n) // 2 + 1)
                    dve.sem_inc(x_ready, 1)
                norm(6, 2, 3)
                dve.wait_ge(past_in, 32)
                dve.sem_inc(a_ready, 1)
                with dve.Fori(0, KF) as f:
                    PER = 8
                    first, step.offset = step.n, f * PER
                    for p in range(2):
                        w = one(w_conv, f + p * KF, slice(0, 4))
                        cc = c[:, p, 0:C0]
                        dve.wait_ge(acc_out[p], f + (T_UP // 2 + 1))
                        dve.wait_ge(past_put, f * 2 + (p + 1))
                        step.done(dve.tensor_scalar(cc, u[:, p, 0:C0], w[:, 0:1], w[:, 3:4], ALU.mult, ALU.add))
                        step.wait()
                        step.done(dve.scalar_tensor_tensor(out=cc, in0=u[:, p, 1:1 + C0], scalar=w[:, 1:2], in1=cc,
                                                           op0=ALU.mult, op1=ALU.add))
                        step.wait()
                        dve.scalar_tensor_tensor(out=cc, in0=u[:, p, 2:2 + C0], scalar=w[:, 2:3], in1=cc,
                                                 op0=ALU.mult, op1=ALU.add).then_inc(conv_done, 1)
                    dve.wait_ge(conv_done, f * 2 + 2)
                    dve.wait_ge(silu_exp, f + 1)
                    e = e_a[:, 0:C0]
                    step.done(dve.tensor_scalar(e, e, 1.0, None, ALU.add))
                    step.wait()
                    step.done(dve.reciprocal(e, e))
                    step.wait()
                    step.done(dve.tensor_tensor(e, e, c[:, 0, 0:C0], ALU.mult))
                    step.wait()
                    a = one(act_a, f, slice(0, NT))
                    step.done(dve.tensor_tensor(a[:, 0:T], e[:, 0:T], c[:, 1, 0:T], ALU.mult))
                    of_seq = lambda v: v[:, 2 + T:2 + T + 48].rearrange("p (n s) -> p n s", s=6)[:, :, 0:S]
                    dve.tensor_tensor(a[:, T:NT].rearrange("p (n q) -> p n q", q=S), of_seq(e_a[:, :]),
                                      of_seq(c[:, 1, :]), ALU.mult).then_inc(a_ready, 1)
                    dve.wait_ge(a_ready, f + 2)
                    assert step.n - first == PER
                step.offset = None
                for n in range(KD):
                    add_to_x(x[:, n, :], T_DOWN + n + 1, n).then_inc(acc_out[n % 2], 1)
                    dve.wait_ge(acc_out[n % 2], (T_DOWN + n) // 2 + 1)
                    dve.sem_inc(y_done, 1)




def program(nc, d):
    with ExitStack() as ctx:
        def sem(name):
            return ctx.enter_context(nc.semaphore(name))

        def sb(name, shape, dt=F32):
            return ctx.enter_context(nc.sbuf_tensor(name, shape, dt))

        class Shared:
            pass

        m = Shared()
        m.ps = ctx.enter_context(nc.psum_tensor("ps", [P, 8, 512], F32))
        m.oa = sb("attended", [P, 8, NT])
        m.mk, m.mv = sb("mk", [P, MH, MTOK]), sb("mv", [P, 2, 512])
        m.ones, m.ident = sb("ones_sb", [P, P]), sb("ident_sb", [P, P])
        m.cmp_bias = sb("cmp_bias", [P, 2])
        m.g_model, m.g_memh = sb("g_model_sb", [P, 4 * KD]), sb("g_memh_sb", [P, 2])
        m.zs, m.vas, m.vbs, m.gates = sb("zs", [P, NTILE, SN]), sb("vas", [SN, 512]), sb("vbs", [SN, 256]), \
            sb("gates_s", [SN, 24])
        with ExitStack() as tokens:
            m.z = tokens.enter_context(nc.sbuf_tensor("z", [P, NTILE, NT], F32))
            m.va = tokens.enter_context(nc.sbuf_tensor("va", [P, QT + 1, 512], F32))
            m.vb = tokens.enter_context(nc.sbuf_tensor("vb", [P, QT + 1, 256], F32))
            m.gate = tokens.enter_context(nc.sbuf_tensor("gate", [P, QT + 1, 24], F32))
            project(nc, d, m, sem)
            attend_prompt(nc, d, m, sem)
        attend_sample(nc, d, m, sem)
        finish(nc, d, m, sem)


def kernel(**inputs):
    import concourse.bacc as bacc
    from concourse.bass_utils import run_bass_kernel_spmd

    nc = bacc.Bacc("TRN2", target_bir_lowering=False, num_devices=1)
    laid = lay_out(**{k: np.asarray(v) for k, v in inputs.items()})
    arrays = {"in_" + k: v for k, v in laid.items()}
    d = {k: nc.dram_tensor("in_" + k, v.shape, mybir.dt.from_np(v.dtype), kind="ExternalInput").ap()
         for k, v in laid.items()}
    d |= {k: nc.dram_tensor(k, s, F32, kind="ExternalOutput").ap() for k, s in OUTS.items()}
    program(nc, d)
    r = run_bass_kernel_spmd(nc, [arrays], core_ids=[0])
    return lay_back({k: np.asarray(r.results[0][k]) for k in OUTS})
```
